# Optimizing a Trainium2 kernel written in Bass

```python
import math
import jax
import jax.numpy as jnp
from jax import lax
import numpy as np

D_MODEL = 1024
BATCH = 1
SEQ = 512
DEPTH = 1
DEC_BATCH = 8
DEC_SEQ = 16
PAST_LEN = 256

CHUNK = 64
N_META = 16
META_CHUNK = -1
Q_BLOCK = 128
D_CONV = D_MODEL
CONV_W = 3
N_HEADS = 8
D_QK = 64
D_V = 2 * D_QK
D_ATTN = N_HEADS * D_V
PROJ_SIZES = (D_CONV, D_CONV, D_CONV, N_HEADS * 2 * D_QK, N_HEADS * 2 * D_QK, D_ATTN, D_MODEL, D_MODEL)
PROJ_SPLITS = (D_CONV, 2 * D_CONV, 3 * D_CONV, 3 * D_CONV + N_HEADS * 2 * D_QK, 3 * D_CONV + N_HEADS * 4 * D_QK, 3 * D_CONV + N_HEADS * 4 * D_QK + D_ATTN, 3 * D_CONV + N_HEADS * 4 * D_QK + D_ATTN + D_MODEL)
D_PROJ = 3 * D_CONV + N_HEADS * 4 * D_QK + D_ATTN + 2 * D_MODEL
N_GROUPS = 4
EXP_PER_GROUP = 8
N_EXPERTS = N_GROUPS * EXP_PER_GROUP
TOP_K_INNER = 2
D_EXPERT = D_MODEL // 4
ALPHA = (2.0 * DEPTH) ** 0.25
BETA = (8.0 * DEPTH) ** -0.25
LN_EPS = 1e-5
RMS_EPS = 1e-5

kernel_name = 'hybrid_conv_diffattn_hmoe_stream_step'

def layer_norm(x, g, b):
    xf = x.astype(jnp.float32)
    mu = jnp.mean(xf, axis=-1, keepdims=True)
    xc = xf - mu
    var = jnp.mean(xc * xc, axis=-1, keepdims=True)
    return (xc * lax.rsqrt(var + LN_EPS) * g + b).astype(x.dtype)

def frame_chunk_ids(start, n):
    return (start + jnp.arange(n, dtype=jnp.int32)) // CHUNK

def split_proj(p):
    h, bg, cg, q, k, v, gc, ga = jnp.split(p, PROJ_SPLITS, axis=-1)
    lead = p.shape[:-1]
    q = q.reshape(lead + (N_HEADS, 2, D_QK))
    k = k.reshape(lead + (N_HEADS, 2, D_QK))
    v = v.reshape(lead + (N_HEADS, D_V))
    return h, bg, cg, q, k, v, gc, ga

def causal_conv3(u_hist, w):
    L = u_hist.shape[1] - (CONV_W - 1)
    return sum(w[i] * u_hist[:, i:i + L] for i in range(CONV_W))

def conv_branch(h, bg, cg, u_prev, w):
    u = cg * h
    u_hist = jnp.concatenate([u_prev.astype(u.dtype), u], axis=1)
    return bg * causal_conv3(u_hist, w), u_hist[:, -(CONV_W - 1):]

def diff_lambda(lam_qk, lam_init):
    lf = lam_qk.astype(jnp.float32)
    return jnp.exp(jnp.sum(lf[0] * lf[1])) - jnp.exp(jnp.sum(lf[2] * lf[3])) + lam_init

def diff_attention(q, k, v, q_chunk, k_chunk, lam, lam_init, subln_g):
    s = jnp.einsum('bqhmd,bkhmd->bhmqk', q, k).astype(jnp.float32) * (D_QK ** -0.5)
    mask = k_chunk[None, :] <= q_chunk[:, None]
    p = jax.nn.softmax(jnp.where(mask, s, -jnp.inf), axis=-1)
    a = p[:, :, 0] - lam * p[:, :, 1]
    o = jnp.einsum('bhqk,bkhd->bqhd', a.astype(v.dtype), v).astype(jnp.float32)
    o = o * lax.rsqrt(jnp.mean(o * o, axis=-1, keepdims=True) + RMS_EPS) * subln_g * (1.0 - lam_init)
    return o.astype(v.dtype)

def prompt_attention(q, k, v, lam, lam_init, subln_g):
    B, L = q.shape[0], q.shape[1]
    n = L - N_META
    nb = n // Q_BLOCK
    cid = jnp.concatenate([jnp.full((N_META,), META_CHUNK, jnp.int32), frame_chunk_ids(0, n)])
    o_meta = diff_attention(q[:, :N_META], k, v, cid[:N_META], cid, lam, lam_init, subln_g)
    qf = jnp.moveaxis(q[:, N_META:].reshape(B, nb, Q_BLOCK, N_HEADS, 2, D_QK), 1, 0)
    cf = cid[N_META:].reshape(nb, Q_BLOCK)
    o_f = lax.map(lambda qc: diff_attention(qc[0], k, v, qc[1], cid, lam, lam_init, subln_g), (qf, cf))
    o_f = jnp.moveaxis(o_f, 0, 1).reshape(B, n, N_HEADS, D_V)
    return jnp.concatenate([o_meta, o_f], axis=1).reshape(B, L, D_ATTN)

def hier_moe(x, w_group, b_group, w_router, b_router, w_gate_up, w_down):
    T = x.shape[0]
    p_group = jax.nn.softmax((x @ w_group + b_group).astype(jnp.float32), axis=-1)
    p_g, g_idx = lax.top_k(p_group, 1)
    logits_e = (x @ w_router + b_router).astype(jnp.float32)
    in_group = g_idx * EXP_PER_GROUP + jnp.arange(EXP_PER_GROUP, dtype=jnp.int32)[None, :]
    top_vals, top_idx = lax.top_k(jnp.take_along_axis(logits_e, in_group, axis=1), TOP_K_INNER)
    weights = p_g * jax.nn.softmax(top_vals, axis=-1)
    expert_id = jnp.take_along_axis(in_group, top_idx, axis=1)
    gates = jnp.zeros((T, N_EXPERTS), jnp.float32).at[jnp.arange(T)[:, None], expert_id].add(weights)

    def expert_step(acc, ws):
        wgu, wd, g = ws
        a, b = jnp.split(x @ wgu, 2, axis=-1)
        return acc + g[:, None] * ((jax.nn.silu(a) * b) @ wd), None

    out, _ = lax.scan(expert_step, jnp.zeros_like(x), (w_gate_up, w_down, gates.T.astype(x.dtype)))
    return out

def layer_tail(x, yc, ya, gc, ga, w_branch, w_out, ln1_g, ln1_b, w_group, b_group, w_router, b_router, w_gate_up, w_down, ln2_g, ln2_b):
    merged = jax.nn.sigmoid(gc) * (yc @ w_branch[0]) + jax.nn.sigmoid(ga) * (ya @ w_branch[1])
    h = layer_norm(ALPHA * x + merged @ w_out, ln1_g, ln1_b)
    Bn, L, D = h.shape
    f = hier_moe(h.reshape(Bn * L, D), w_group, b_group, w_router, b_router, w_gate_up, w_down).reshape(Bn, L, D)
    return layer_norm(ALPHA * h + f, ln2_g, ln2_b)

def setup_inputs(seed: int = 0) -> dict:
    key = jax.random.key(seed)
    ks = jax.random.split(key, 24)
    nrm = jax.random.normal
    f32 = jnp.float32
    return {
        'x_prompt': nrm(ks[0], (BATCH, SEQ, D_MODEL), f32),
        'x_sample': nrm(ks[1], (DEC_BATCH, DEC_SEQ, D_MODEL), f32),
        'cache_k': nrm(ks[2], (DEPTH, DEC_BATCH, N_META + PAST_LEN, N_HEADS, 2 * D_QK), f32),
        'cache_v': nrm(ks[3], (DEPTH, DEC_BATCH, N_META + PAST_LEN, N_HEADS, D_V), f32),
        'state_conv': nrm(ks[4], (DEPTH, DEC_BATCH, CONV_W - 1, D_CONV), f32),
        'meta_tokens': nrm(ks[5], (N_META, D_MODEL), f32),
        'w_in': nrm(ks[6], (DEPTH, D_MODEL, D_PROJ), f32) * D_MODEL ** -0.5,
        'conv_w': nrm(ks[7], (DEPTH, CONV_W, D_CONV), f32) * CONV_W ** -0.5,
        'lambda_qk': nrm(ks[8], (DEPTH, 4, D_QK), f32) * 0.1,
        'subln_g': 1.0 + 0.02 * nrm(ks[9], (DEPTH, D_V), f32),
        'w_branch': nrm(ks[10], (DEPTH, 2, D_CONV, D_MODEL), f32) * D_CONV ** -0.5,
        'w_out': nrm(ks[11], (DEPTH, D_MODEL, D_MODEL), f32) * (D_MODEL ** -0.5 * BETA),
        'ln1_g': 1.0 + 0.02 * nrm(ks[12], (DEPTH, D_MODEL), f32),
        'ln1_b': 0.02 * nrm(ks[13], (DEPTH, D_MODEL), f32),
        'w_group': nrm(ks[14], (DEPTH, D_MODEL, N_GROUPS), f32) * D_MODEL ** -0.5,
        'b_group': 0.01 * nrm(ks[15], (DEPTH, N_GROUPS), f32),
        'w_router': nrm(ks[16], (DEPTH, D_MODEL, N_EXPERTS), f32) * D_MODEL ** -0.5,
        'b_router': 0.01 * nrm(ks[17], (DEPTH, N_EXPERTS), f32),
        'w_gate_up': nrm(ks[18], (DEPTH, N_EXPERTS, D_MODEL, 2 * D_EXPERT), f32) * D_MODEL ** -0.5,
        'w_down': nrm(ks[19], (DEPTH, N_EXPERTS, D_EXPERT, D_MODEL), f32) * (D_EXPERT ** -0.5 * BETA),
        'ln2_g': 1.0 + 0.02 * nrm(ks[20], (DEPTH, D_MODEL), f32),
        'ln2_b': 0.02 * nrm(ks[21], (DEPTH, D_MODEL), f32),
    }

def reference(x_prompt, x_sample, cache_k, cache_v, state_conv, meta_tokens, w_in, conv_w, lambda_qk, subln_g, w_branch, w_out, ln1_g, ln1_b, w_group, b_group, w_router, b_router, w_gate_up, w_down, ln2_g, ln2_b):
    Bp = x_prompt.shape[0]
    Bs, S = x_sample.shape[0], x_sample.shape[1]
    past = cache_k.shape[2] - N_META
    meta = jnp.broadcast_to(meta_tokens[None].astype(x_prompt.dtype), (Bp, N_META, D_MODEL))
    h_p = jnp.concatenate([meta, x_prompt], axis=1)
    h_s = x_sample
    cid_k = jnp.concatenate([jnp.full((N_META,), META_CHUNK, jnp.int32), frame_chunk_ids(0, past), frame_chunk_ids(past, S)])
    cid_q = frame_chunk_ids(past, S)
    nk_p, nv_p, nc_p, nk_s, nv_s, nc_s = [], [], [], [], [], []
    for l in range(DEPTH):
        lam_init = 0.8 - 0.6 * math.exp(-0.3 * l)
        lam = diff_lambda(lambda_qk[l], lam_init)
        hh, bg, cg, q, k, v, gc, ga = split_proj(h_p @ w_in[l])
        yc, conv_p = conv_branch(hh, bg, cg, jnp.zeros((Bp, CONV_W - 1, D_CONV), hh.dtype), conv_w[l])
        ya = prompt_attention(q, k, v, lam, lam_init, subln_g[l])
        nk_p.append(k.reshape(k.shape[:3] + (2 * D_QK,)))
        nv_p.append(v)
        nc_p.append(conv_p)
        sh, sbg, scg, sq, sk, sv, sgc, sga = split_proj(h_s @ w_in[l])
        syc, conv_s = conv_branch(sh, sbg, scg, state_conv[l], conv_w[l])
        k_all = jnp.concatenate([cache_k[l].reshape(Bs, N_META + past, N_HEADS, 2, D_QK).astype(sk.dtype), sk], axis=1)
        v_all = jnp.concatenate([cache_v[l].astype(sv.dtype), sv], axis=1)
        sya = diff_attention(sq, k_all, v_all, cid_q, cid_k, lam, lam_init, subln_g[l]).reshape(Bs, S, D_ATTN)
        nk_s.append(sk.reshape(Bs, S, N_HEADS, 2 * D_QK))
        nv_s.append(sv)
        nc_s.append(conv_s)
        h_p = layer_tail(h_p, yc, ya, gc, ga, w_branch[l], w_out[l], ln1_g[l], ln1_b[l], w_group[l], b_group[l], w_router[l], b_router[l], w_gate_up[l], w_down[l], ln2_g[l], ln2_b[l])
        h_s = layer_tail(h_s, syc, sya, sgc, sga, w_branch[l], w_out[l], ln1_g[l], ln1_b[l], w_group[l], b_group[l], w_router[l], b_router[l], w_gate_up[l], w_down[l], ln2_g[l], ln2_b[l])
    y_prompt = h_p[:, N_META:]
    y_sample = h_s
    return (y_prompt, y_sample, jnp.stack(nk_p), jnp.stack(nv_p), jnp.stack(nc_p), jnp.stack(nk_s), jnp.stack(nv_s), jnp.stack(nc_s))


_drawn_inputs = setup_inputs


def setup_inputs(seed=0):
    import zlib

    import numpy as np

    out = dict(_drawn_inputs(seed))
    spreads = {}
    factors = {'subln_g': 6.148, 'b_group': 174.034, 'b_router': 8.0, 'ln2_g': 25.573, 'ln2_b': 23.831}
    for name, (base, spread) in spreads.items():
        noise = np.random.default_rng([zlib.crc32(name.encode()), seed]).standard_normal(out[name].shape)
        drawn = base * np.exp(spread * noise) if base else spread * noise
        out[name] = jnp.asarray(drawn.astype(out[name].dtype))
    for name, factor in factors.items():
        out[name] = (out[name] * factor).astype(out[name].dtype)
    return out
```

```python
from contextlib import ExitStack

import concourse.bass as bass
import numpy as np
from concourse import mybir

F32 = mybir.dt.float32
F32R = mybir.dt.float32r
U32 = mybir.dt.uint32
I32 = mybir.dt.int32
ALU = mybir.AluOpType
ACT = mybir.ActivationFunctionType
AX = mybir.AxisListType

P = 128
D = 1024
KT = D // P
META, SEQ, STREAMS, NEW, PAST = 16, 512, 8, 16, 256
SAMPLE = STREAMS * NEW
T = META + SEQ + SAMPLE
TOK = SEQ + SAMPLE
HALF = T // 2
TB = TOK // P
QB = SEQ // P
CHUNK = 64
HEADS = 8
CACHED = META + PAST
OWN = 2
LAM_INIT = 0.2
ALPHA = 2.0 ** 0.25
EPS = 1e-5
SCALE = 64 ** -0.5
MASKED = -1e30
EXPERTS, PER_GROUP, GROUPS = 32, 8, 4
DE = 256
BLOCKS = (2 * TOK + EXPERTS * (P - 1)) // P
COL = {"h": 0, "bg": D, "cg": 2 * D, "q": 3 * D, "k": 4 * D, "v": 5 * D, "gc": 6 * D, "ga": 7 * D}
UNITS = ["h", "cg", "bg", "gc", "ga", "k", "v", "q"]
NU = len(UNITS)

C_ID, C_SPREAD, C_MASK, C_UPPER = 0, 128, 384, 640
C_GROUP, C_EXPERT, C_BLOCK, C_SIGN, C_TOKEN, C_END = 768, 800, 832, 880, 881, 888


def constants():
    c = np.zeros((P, C_END), np.float32)
    row = np.arange(P)
    c[:, C_ID:C_ID + P] = np.eye(P)
    for g in range(2):
        for r in range(P):
            s, q = 4 * g + r // 32, r % 16
            c[r, C_SPREAD + P * g + 16 * s + q] = 1.0
            c[r, C_MASK + P * g:C_MASK + P * (g + 1)] = np.where(row // 16 == s, 0.0, MASKED)
    c[:, C_UPPER:C_UPPER + P] = row[:, None] < row[None, :]
    c[:, C_GROUP:C_GROUP + EXPERTS] = np.arange(EXPERTS) // PER_GROUP
    c[:, C_EXPERT:C_EXPERT + EXPERTS] = np.arange(EXPERTS)
    c[:, C_BLOCK:C_BLOCK + BLOCKS] = np.arange(BLOCKS)
    c[:, C_SIGN] = (row // 16) % 2
    for b in range(TB):
        c[:, C_TOKEN + b] = P * b + row
    return c


def wait(eng, sem, value):
    if not isinstance(value, int) or value > 0:
        eng.wait_ge(sem, value)


def project_and_attend(nc, d, keep):
    with ExitStack() as ctx:
        sb = lambda name, shape, dt=F32: ctx.enter_context(nc.sbuf_tensor(name, shape, dt))
        pb = lambda name, shape: ctx.enter_context(nc.psum_tensor(name, shape, F32))
        sem = lambda name: ctx.enter_context(nc.semaphore(name))
        yc, ya, const = keep["yc"], keep["ya"], keep["const"]

        x_hi, x_lo = sb("x_hi", [P, KT, T], F32R), sb("x_lo", [P, KT, T], F32R)
        w_raw = sb("w_raw", [P, 2, KT, P])
        w_hi, w_lo = sb("w_hi", [P, 2, KT, P], F32R), sb("w_lo", [P, 2, KT, P], F32R)
        h_buf, u_buf, conv = sb("h_buf", [P, T]), sb("u_buf", [P, T]), sb("conv", [P, TOK])
        u_hist = sb("u_hist", [P, STREAMS, NEW + 2])
        u_last = sb("u_last", [P, KT, 18])
        hist_T = sb("hist_T", [P, KT, 16])
        taps = sb("taps", [P, KT, 3])
        gate = sb("gate", [P, 2, TOK])
        kT, vT, qT = sb("kT", [P, T]), sb("vT", [P, T]), sb("qT", [P, TOK])
        q_maps = sb("q_maps", [P, STREAMS, 32])
        q_pad = sb("q_pad", [P, STREAMS * P + P])
        k_rows, v_rows = sb("k_rows", [P, 6, P]), sb("v_rows", [P, 6, P])
        k_cache, v_cache = sb("k_cache", [P, 17, P]), sb("v_cache", [P, 17, P])
        kcT = sb("kcT", [P, 17 * P])
        prob = sb("prob", [P, 2, META + SEQ])
        mix = sb("mix", [P, 2, META + SEQ])
        mixT, mixT_meta = sb("mixT", [P, QB, SEQ]), sb("mixT_meta", [META, SEQ])
        own_T = sb("own_T", [P, OWN, STREAMS * P + P])
        shared_T = sb("shared_T", [P, 2, P])
        spread = sb("spread", [P, 2, P])
        neg_max, row_sum = sb("neg_max", [P, 2]), sb("row_sum", [P, 2])
        inv = sb("inv", [P, 4])
        lam = sb("lam", [P, 8])
        lam_in, lam_tmp = sb("lam_in", [P, 256]), sb("lam_tmp", [P, 64])
        x_rows = [k_cache[:, 0:8, :].rearrange("p a b -> p (a b)"), v_cache[:, 0:8, :].rearrange("p a b -> p (a b)")]
        meta_rows = kcT[0:META, 0:D]
        state_rows = mixT[0:16, 0:2, :].rearrange("p a b -> p (a b)")
        last_rows = mixT[0:18, 0:2, :].rearrange("p a b -> p (a b)")

        bank_u = [pb("bank_u0", [P, 512]), pb("bank_u1", [P, 512])]
        bank_s = [pb("bank_s0", [P, 1024]), pb("bank_s1", [P, 1024])]
        bank_t, bank_o = pb("bank_t", [P, 512]), pb("bank_o", [P, 512])
        meta_T = bank_t[0:META, 384:512]
        ident = const[:, C_ID:C_ID + P]

        names = ["const_in", "meta_in", "state_in", "taps_in", "lam_in_sem", "zeroed", "lam_ready", "lam_sums", "lam_exp",
                 "turned", "turned_hi", "turned_lo", "hist_done", "split_hi", "split_lo", "half_done", "hist_ready",
                 "k_cache_in", "v_cache_in", "t_full", "t_free", "o_full", "o_free", 
                 "max_ready0", "max_ready1", "exp_done0", "exp_done1", "scores0", "scores1", "mix_ready", "spread_ready",
                 "q_maps_ready", "kv_stored", "last_stored"]
        s = {n: sem("a_" + n) for n in names}
        x_in = [sem("a_x_in0"), sem("a_x_in1")]
        w_in_sem = [sem("a_w_in0"), sem("a_w_in1")]
        gate_stored = [sem("a_gate_stored0"), sem("a_gate_stored1")]
        evicted = [sem("a_evicted0"), sem("a_evicted1")]
        scores = [s["scores0"], s["scores1"]]
        max_ready = [s["max_ready0"], s["max_ready1"]]
        exp_done = [s["exp_done0"], s["exp_done1"]]
        block = ctx.enter_context(nc.Block())

        fill_t = lambda i, n: 11 * i - 9 + n
        fill_o = lambda i, n: 6 * i - 4 + n
        fill_s = lambda i, n: 5 * (i - 1) + n
        T_SAMPLE, T_PROMPT, T_META, T_ROWS, O_SAMPLE, O_PROMPT, O_ROWS = 3, 4, 8, 9, 2, 3, 4

        def turns(eng, body):
            body(0, True, False)
            with eng.Fori(1, HEADS) as i:
                body(i, True, True)
            body(HEADS, False, True)

        w_view = d["w_in"][0].rearrange("(k p) n -> p k n", p=P)
        keys = lambda b: META + P * (b + 1)

        @block.sync
        def _(sp):
            sp.dma_start(const[:], d["const"]).then_inc(s["const_in"], 16)
            sp.dma_start(meta_rows, d["meta_tokens"]).then_inc(s["meta_in"], 16)
            for b in range(TB):
                wait(sp, s["turned"], 2 * (b - 1))
                src = d["x_prompt"][0, P * b:P * (b + 1), :] if b < QB else d["x_sample"].rearrange("s q d -> (s q) d")
                sp.dma_start(x_rows[b % 2], src).then_inc(x_in[b % 2], 16)
                if b == 0:
                    sp.dma_start(state_rows, d["state_conv"][0].rearrange("s j d -> (s j) d")).then_inc(s["state_in"], 16)
                    sp.dma_start(lam_in[:], d["lambda_qk"].rearrange("l a b -> l (a b)").to_broadcast((P, 256))).then_inc(s["lam_in_sem"], 16)
                    with nc.allow_non_contiguous_dma(reason="three taps of each channel, once"):
                        for k in range(KT):
                            sp.dma_start(taps[:, k, :], d["conv_w"][0, :, P * k:P * (k + 1)].rearrange("w p -> p w")).then_inc(s["taps_in"], 16)

            def body(i, units, attend):
                if not units:
                    return
                for u, name in enumerate(UNITS):
                    n = NU * i + u
                    src = w_view[:, :, bass.ds(sp.snap(i * P + COL[name]) if not isinstance(i, int) else i * P + COL[name], P)]
                    wait(sp, s["split_lo"], n - 1)
                    sp.dma_start(w_raw[:, u % 2], src).then_inc(w_in_sem[u % 2], 16)
                    if u == 6:
                        for name, buf, done in (("cache_k", k_cache, "k_cache_in"), ("cache_v", v_cache, "v_cache_in")):
                            srcs = [d[name][0, :, P * t:P * (t + 1), bass.ds(sp.snap(i + 0) if not isinstance(i, int) else i, 1), :]
                                    .rearrange("s p h d -> p s (h d)") for t in range(OWN)]
                            srcs.append(d[name][0, :, OWN * P:CACHED, bass.ds(sp.snap(i + 0) if not isinstance(i, int) else i, 1), :])
                            if isinstance(i, int):
                                sp.wait_ge(s["turned"], 2 * TB + 3)
                            else:
                                sp.wait_ge(s["o_full"], fill_o(i, O_SAMPLE) + 1)
                            for t in range(OWN):
                                sp.dma_start(buf[:, t:OWN * STREAMS:OWN, :], srcs[t]).then_inc(s[done], 16)
                            sp.dma_start(buf[:, 16, :], srcs[OWN]).then_inc(s[done], 16)

            turns(sp, body)

        @block.tensor
        def _(pe):
            pe.wait_ge(s["const_in"], 16)
            for f in range(2 * TB + 2):
                b, half = divmod(f, 2)
                rows, w = (x_rows[b % 2], P) if b < TB else (meta_rows, META)
                if b < TB:
                    pe.wait_ge(x_in[b % 2], 16 * (b // 2 + 1))
                else:
                    pe.wait_ge(s["meta_in"], 16)
                wait(pe, s["turned_lo"], f - 1)
                bank = (bank_t, bank_o)[f % 2][:].rearrange("p (k c) -> p k c", k=4)
                for k in range(4):
                    kk = 4 * half + k
                    last = pe.transpose(bank[:, k, 0:w], rows[:, P * kk:P * (kk + 1)], ident[0:w, 0:w])
                last.then_inc(s["turned"], 1)
            pe.wait_ge(s["state_in"], 16)
            pe.wait_ge(s["turned_lo"], 2 * TB + 1)
            for k in range(KT):
                last = pe.transpose(bank_t[:, 16 * k:16 * k + 16], state_rows[:, P * k:P * (k + 1)], ident[0:16, 0:16])
            last.then_inc(s["turned"], 1)
            pe.wait_ge(s["hist_done"], 1)

            def unit(i, u):
                n = NU * i + u
                pe.wait_ge(s["split_lo"], n + 1)
                for half in range(2):
                    wait(pe, evicted[half], n)
                    out = bank_u[half][:, 0:HALF]
                    cols = slice(HALF * half, HALF * (half + 1))
                    for k in range(KT):
                        pe.matmul(out, w_hi[:, u % 2, k, :], x_hi[:, k, cols], start=(k == 0), stop=False)
                        pe.matmul(out, w_hi[:, u % 2, k, :], x_lo[:, k, cols], start=False, stop=False)
                        last = pe.matmul(out, w_lo[:, u % 2, k, :], x_hi[:, k, cols], start=False, stop=(k == KT - 1))
                    last.then_inc(s["half_done"], 1)

            def turn_cache(i):
                pe.wait_ge(s["k_cache_in"], 48 * i)
                for f in range(5):
                    if f % 2 == 0:
                        bank, full, free, n = bank_t, "t_full", "t_free", fill_t(i, f // 2)
                    else:
                        bank, full, free, n = bank_o, "o_full", "o_free", fill_o(i, f // 2)
                    pe.wait_ge(s[free], n)
                    for k in range(4 * f, min(4 * f + 4, 17)):
                        last = pe.transpose(bank[:, P * (k % 4):P * (k % 4) + P], k_cache[:, k, :], ident)
                    last.then_inc(s[full], 1)

            def sample_scores(i):
                pe.wait_ge(s["q_maps_ready"], i)
                pe.wait_ge(s["t_free"], fill_t(i, 3))
                pe.wait_ge(s["o_free"], fill_o(i, 2))
                for g in range(2):
                    for j in range(4):
                        st = 4 * g + j
                        pe.matmul(bank_s[g][:, 0:2 * P], q_pad[:, P * st:P * (st + 1)], kcT[:, 2 * P * st:2 * P * (st + 1)],
                                  start=(j == 0), stop=(j == 3))
                    q_all = q_maps[:, 4 * g:4 * g + 4, :].rearrange("p s c -> p (s c)")
                    pe.matmul(bank_s[g][:, 2 * P:3 * P], q_all, kcT[:, 16 * P:17 * P], start=True, stop=True)
                    pe.matmul(bank_s[g][:, 3 * P:4 * P], q_all, kT[:, META + SEQ:T], start=True, stop=True).then_inc(scores[g], 1)

            def sample_mix(i):
                pe.wait_ge(s["spread_ready"], i)
                pe.wait_ge(s["t_free"], fill_t(i, T_SAMPLE))
                for t in range(4):
                    for g in range(2):
                        last = pe.matmul(bank_t[:, P * t:P * (t + 1)], prob[:, g, P * t:P * (t + 1)], spread[:, g, :],
                                         start=(g == 0), stop=(g == 1))
                last.then_inc(s["t_full"], 1)

            def sample_values(i):
                pe.wait_ge(s["v_cache_in"], 48 * i)
                pe.wait_ge(s["t_free"], fill_t(i, T_SAMPLE) + 1)
                pe.wait_ge(s["o_free"], fill_o(i, O_SAMPLE))
                out = bank_o[:, 0:P]
                for st in range(STREAMS):
                    for t in range(OWN):
                        pe.matmul(out, v_cache[:, OWN * st + t, :], own_T[:, t, P * st:P * (st + 1)],
                                  start=(st == 0 and t == 0), stop=False)
                pe.matmul(out, v_cache[:, 16, :], shared_T[:, 0, :], start=False, stop=False)
                pe.matmul(out, v_rows[:, 4, :], shared_T[:, 1, :], start=False, stop=True).then_inc(s["o_full"], 1)

            def prompt_scores(i, b):
                for m in range(2):
                    wait(pe, exp_done[m], fill_s(i, 1 + b))
                    r = slice(64 * m, 64 * m + 64)
                    w = keys(b)
                    last = pe.matmul(bank_s[m][:, 0:min(w, 512)], qT[r, P * b:P * (b + 1)], kT[r, 0:min(w, 512)], start=True, stop=True)
                    if w > 512:
                        last = pe.matmul(bank_s[m][:, 512:w], qT[r, P * b:P * (b + 1)], kT[r, 512:w], start=True, stop=True)
                    last.then_inc(scores[m], 1)

            def prompt_turn(i, b):
                pe.wait_ge(s["mix_ready"], 4 * (i - 1) + b + 1)
                pe.wait_ge(s["t_free"], fill_t(i, T_PROMPT + b))
                for t in range(b + 1):
                    last = pe.transpose(bank_t[:, P * t:P * (t + 1)], mix[:, b % 2, META + P * t:META + P * (t + 1)], ident)
                if b == QB - 1:
                    last.then_inc(s["t_full"], 1)
                    pe.wait_ge(s["t_free"], fill_t(i, T_META))
                pe.transpose(meta_T, mix[:, b % 2, 0:META], ident).then_inc(s["t_full"], 1)

            def prompt_values(i):
                pe.wait_ge(s["t_free"], fill_t(i, T_META) + 1)
                pe.wait_ge(s["o_free"], fill_o(i, O_PROMPT))
                pe.matmul(bank_o[:], v_rows[0:META, 5, :], mixT_meta[:], start=True, stop=False)
                for t in range(QB):
                    last = pe.matmul(bank_o[:, P * t:SEQ], v_rows[:, t, :], mixT[:, t, P * t:SEQ], start=False, stop=(t == QB - 1))
                last.then_inc(s["o_full"], 1)

            def turn_rows(i):
                for n, (src, u) in enumerate(((kT, 5), (vT, 6))):
                    for half in range(2):
                        pe.wait_ge(evicted[half], NU * i + u + 1)
                    wait(pe, s["t_free"], fill_t(i, T_ROWS + n))
                    for t in range(QB):
                        last = pe.transpose(bank_t[:, P * t:P * (t + 1)], src[:, META + P * t:META + P * (t + 1)], ident)
                    last.then_inc(s["t_full"], 1)
                    wait(pe, s["o_free"], fill_o(i, O_ROWS + n))
                    pe.transpose(bank_o[:, 0:P], src[:, META + SEQ:T], ident)
                    pe.transpose(bank_o[0:META, P:2 * P], src[:, 0:META], ident).then_inc(s["o_full"], 1)

            def body(i, units, attend):
                for u in range(NU):
                    if units:
                        unit(i, u)
                    if attend:
                        if u == 0:
                            turn_cache(i)
                            sample_scores(i)
                        if u == 1:
                            sample_mix(i)
                            prompt_scores(i, 0)
                        if u == 2:
                            sample_values(i)
                        if 2 <= u <= 5:
                            prompt_turn(i, u - 2)
                        if 2 <= u <= 4:
                            prompt_scores(i, u - 1)
                        if u == 6:
                            prompt_values(i)
                if units:
                    turn_rows(i)

            turns(pe, body)
            pe.wait_ge(s["hist_ready"], KT)
            pe.wait_ge(s["t_free"], fill_t(HEADS, T_ROWS))
            for k in range(4):
                last = pe.transpose(bank_t[0:18, P * k:P * (k + 1)], u_last[:, k, :], ident)
            last.then_inc(s["t_full"], 1)
            pe.wait_ge(s["o_free"], fill_o(HEADS, O_ROWS))
            for k in range(4):
                last = pe.transpose(bank_o[0:18, P * k:P * (k + 1)], u_last[:, 4 + k, :], ident)
            last.then_inc(s["o_full"], 1)

        @block.scalar
        def _(act):
            act.wait_ge(s["lam_sums"], 1)
            act.activation(lam[:, 2:4], lam[:, 0:2], ACT.Exp).then_inc(s["lam_exp"], 1)
            for f in range(2 * TB + 2):
                b, half = divmod(f, 2)
                w, at = (P, META + P * b) if b < TB else (META, 0)
                bank = (bank_t, bank_o)[f % 2][:].rearrange("p (k c) -> p k c", k=4)
                act.wait_ge(s["turned"], f + 1)
                act.copy(x_hi[:, 4 * half:4 * half + 4, at:at + w], bank[:, :, 0:w]).then_inc(s["turned_hi"], 1)
            act.wait_ge(s["turned"], 2 * TB + 3)
            act.copy(hist_T[:], bank_t[:, 0:P].rearrange("p (k c) -> p k c", k=KT)).then_inc(s["hist_done"], 1)

            def split(i, u):
                n = NU * i + u
                act.wait_ge(w_in_sem[u % 2], 16 * ((NU // 2) * i + u // 2 + 1))
                wait(act, s["half_done"], 2 * (n - 1))
                act.copy(w_hi[:, u % 2], w_raw[:, u % 2]).then_inc(s["split_hi"], 1)

            def evict(i, u):
                n = NU * i + u
                name = UNITS[u]
                for half in range(2):
                    lo, hi = HALF * half, HALF * (half + 1)
                    skip = META if half == 0 else 0
                    if name in ("gc", "ga") and half == 0:
                        wait(act, gate_stored[name == "ga"], 16 * i)
                    if name == "h" and half == 0:
                        for x in range(2):
                            wait(act, evicted[x], NU * (i - 1) + 2)
                    if name in ("k", "q") and half == 0 and not isinstance(i, int):
                        act.wait_ge(s["scores1"], fill_s(i, 4) + 1)
                    if name == "q" and half == 0:
                        wait(act, s["q_maps_ready"], i)
                    act.wait_ge(s["half_done"], 2 * n + half + 1)
                    src = bank_u[half][:, 0:HALF]
                    if name == "h":
                        ins = act.copy(h_buf[:, lo:hi], src)
                    elif name in ("gc", "ga"):
                        ins = act.copy(gate[:, int(name == "ga"), lo + skip - META:hi - META], src[:, skip:])
                    elif name in ("k", "v"):
                        ins = act.copy((kT if name == "k" else vT)[:, lo:hi], src)
                    elif name == "q":
                        ins = act.copy(qT[:, lo + skip - META:hi - META], src[:, skip:])
                    ins.then_inc(evicted[half], 1)
                if name in ("gc", "ga"):
                    for half in range(2):
                        act.wait_ge(evicted[half], n + 1)
                    act.dma_start(d["gates"][int(name == "ga"), bass.ds(i, 1)].rearrange("a p t -> p (a t)"),
                                  gate[:, int(name == "ga"), :]).then_inc(gate_stored[name == "ga"], 16)

            def take_cache(i):
                for f in range(0, 5, 2):
                    act.wait_ge(s["t_full"], fill_t(i, f // 2) + 1)
                    w = P * min(4, 17 - 4 * f)
                    act.copy(kcT[:, 4 * P * f:4 * P * f + w], bank_t[:, 0:w]).then_inc(s["t_free"], 1)

            def exponent(i, n, w):
                for m in range(2):
                    act.wait_ge(max_ready[m], fill_s(i, n) + 1)
                    if n > 1:
                        act.wait_ge(s["mix_ready"], 4 * (i - 1) + n - 1)
                    act.activation(prob[:, m, 0:w], bank_s[m][:, 0:w], ACT.Exp, bias=neg_max[:, m:m + 1], scale=SCALE,
                                   accum_out=row_sum[:, m:m + 1]).then_inc(exp_done[m], 1)

            def take_turned(i, b):
                act.wait_ge(s["t_full"], fill_t(i, T_PROMPT + b) + 1)
                ins = act.copy(mixT[:, 0:b + 1, P * b:P * (b + 1)], bank_t[:, 0:P * (b + 1)].rearrange("p (t q) -> p t q", q=P))
                if b == QB - 1:
                    ins.then_inc(s["t_free"], 1)
                    act.wait_ge(s["t_full"], fill_t(i, T_META) + 1)
                act.copy(mixT_meta[:, P * b:P * (b + 1)], meta_T).then_inc(s["t_free"], 1)

            def take_output(i, n, first, w):
                act.wait_ge(s["o_full"], fill_o(i, n) + 1)
                act.copy(ya[:, bass.ds(i - 1, 1), first:first + w].rearrange("p a t -> p (a t)"), bank_o[:, 0:w]).then_inc(s["o_free"], 1)

            def take_rows(i):
                wait(act, s["kv_stored"], 96 * i)
                for n, rows in enumerate((k_rows, v_rows)):
                    act.wait_ge(s["t_full"], fill_t(i, T_ROWS + n) + 1)
                    act.copy(rows[:, 0:QB, :], bank_t[:].rearrange("p (t c) -> p t c", c=P)).then_inc(s["t_free"], 1)
                    act.wait_ge(s["o_full"], fill_o(i, O_ROWS + n) + 1)
                    act.copy(rows[:, 4, :], bank_o[:, 0:P])
                    act.copy(rows[0:META, 5, :], bank_o[0:META, P:2 * P]).then_inc(s["o_free"], 1)
                act.wait_ge(s["t_free"], fill_t(i, T_ROWS + 1) + 1)
                act.wait_ge(s["o_free"], fill_o(i, O_ROWS + 1) + 1)
                for which, rows in (("k", k_rows), ("v", v_rows)):
                    out = d["new_" + which + "_prompt"][0, 0, :, bass.ds(i, 1), :].rearrange("t a c -> t (a c)")
                    act.dma_start(out[0:META, :], rows[0:META, 5, :]).then_inc(s["kv_stored"], 16)
                    act.dma_start(out[META:META + SEQ, :].rearrange("(b p) c -> p b c", p=P), rows[:, 0:QB, :]).then_inc(s["kv_stored"], 16)
                    out = d["new_" + which + "_sample"][0, :, :, bass.ds(i, 1), :].rearrange("s q a c -> (s q) (a c)")
                    act.dma_start(out, rows[:, 4, :]).then_inc(s["kv_stored"], 16)

            def body(i, units, attend):
                if units:
                    split(i, 0)
                for u in range(NU):
                    if units:
                        if u + 1 < NU:
                            split(i, u + 1)
                        if UNITS[u] not in ("cg", "bg"):
                            evict(i, u)
                    if attend:
                        if u == 0:
                            take_cache(i)
                            exponent(i, 0, 4 * P)
                        if 1 <= u <= 4:
                            if u == 2:
                                take_output(i, O_SAMPLE, SEQ, P)
                            if u >= 2:
                                take_turned(i, u - 2)
                            exponent(i, u, keys(u - 1))
                        if u == 5:
                            take_turned(i, 3)
                        if u == 6:
                            take_output(i, O_PROMPT, 0, SEQ)
                if units:
                    take_rows(i)

            turns(act, body)
            act.wait_ge(s["t_full"], fill_t(HEADS, T_ROWS) + 1)
            act.copy(last_rows[:, 0:512], bank_t[0:18, :])
            act.wait_ge(s["o_full"], fill_o(HEADS, O_ROWS) + 1)
            act.copy(last_rows[:, 512:1024], bank_o[0:18, :]).then_inc(s["t_free"], 1)
            act.wait_ge(s["t_free"], fill_t(HEADS, T_ROWS) + 1)
            act.dma_start(d["new_conv_prompt"][0, 0], last_rows[0:2, :]).then_inc(s["last_stored"], 16)
            act.dma_start(d["new_conv_sample"][0].rearrange("s j c -> (s j) c"), last_rows[2:18, :]).then_inc(s["last_stored"], 16)
            act.wait_ge(s["last_stored"], 32)
            act.wait_ge(s["kv_stored"], 96 * HEADS)
            for x in range(2):
                act.wait_ge(gate_stored[x], 16 * KT)

        @block.vector
        def _(v):
            v.memset(q_maps[:], 0.0)
            v.memset(q_pad[:], 0.0)
            v.memset(own_T[:], 0.0)
            v.wait_ge(s["lam_in_sem"], 16)
            for x in range(2):
                v.tensor_tensor_reduce(lam_tmp[:], lam_in[:, 128 * x:128 * x + 64], lam_in[:, 128 * x + 64:128 * x + 128],
                                       1.0, 0.0, ALU.mult, ALU.add, lam[:, x:x + 1])
                v.drain()
            v.sem_inc(s["lam_sums"], 1)
            v.wait_ge(s["lam_exp"], 1)
            v.scalar_tensor_tensor(lam[:, 4:5], lam[:, 3:4], -LAM_INIT, lam[:, 2:3], ALU.add, ALU.subtract)
            v.drain()
            v.wait_ge(s["const_in"], 16)
            v.tensor_scalar(lam[:, 6:7], lam[:, 4:5], -1.0, None, ALU.add)
            v.drain()
            v.tensor_scalar(lam[:, 5:6], lam[:, 6:7], const[:, C_SIGN:C_SIGN + 1], 1.0, ALU.mult, ALU.add)
            for f in range(2 * TB + 2):
                b, half = divmod(f, 2)
                w, at = (P, META + P * b) if b < TB else (META, 0)
                bank = (bank_t, bank_o)[f % 2][:].rearrange("p (k c) -> p k c", k=4)
                v.wait_ge(s["turned_hi"], f + 1)
                v.tensor_tensor(x_lo[:, 4 * half:4 * half + 4, at:at + w], bank[:, :, 0:w],
                                x_hi[:, 4 * half:4 * half + 4, at:at + w].bitcast(F32), ALU.subtract).then_inc(s["turned_lo"], 1)
            v.wait_ge(s["taps_in"], 16 * KT)
            v.wait_ge(s["hist_done"], 1)

            def split(i, u):
                n = NU * i + u
                v.wait_ge(s["split_hi"], n + 1)
                v.tensor_tensor(w_lo[:, u % 2], w_raw[:, u % 2], w_hi[:, u % 2].bitcast(F32), ALU.subtract).then_inc(s["split_lo"], 1)

            def evict_cg(i):
                n = NU * i + 1
                for half in range(2):
                    lo, hi = HALF * half, HALF * (half + 1)
                    v.wait_ge(evicted[half], n)
                    v.wait_ge(s["half_done"], 2 * n + half + 1)
                    v.tensor_tensor(u_buf[:, lo:hi], bank_u[half][:, 0:HALF], h_buf[:, lo:hi], ALU.mult).then_inc(evicted[half], 1)
                v.drain()
                v.tensor_copy(u_hist[:, :, 2:NEW + 2], u_buf[:, META + SEQ:T].rearrange("p (s q) -> p s q", q=NEW))
                v.tensor_copy(u_hist[:, :, 0:2], hist_T[:, bass.ds(i, 1), :].rearrange("p a (s j) -> p (a s) j", j=2))
                v.tensor_copy(u_last[:, bass.ds(i, 1), 0:2].rearrange("p a c -> p (a c)"), u_buf[:, META + SEQ - 2:META + SEQ])
                v.drain()
                v.tensor_copy(u_last[:, bass.ds(i, 1), 2:18].rearrange("p a (s j) -> p (a s) j", j=2), u_hist[:, :, NEW:NEW + 2]).then_inc(s["hist_ready"], 1)
                for t in (2, 1, 0):
                    tap = taps[:, bass.ds(i, 1), t:t + 1].rearrange("p a b -> p (a b)")
                    to = conv[:, SEQ:TOK].rearrange("p (s q) -> p s q", q=NEW)
                    prompt, sample = u_buf[:, META - 2 + t:META - 2 + t + SEQ], u_hist[:, :, t:t + NEW]
                    if t == 2:
                        v.tensor_scalar(conv[:, 0:SEQ], prompt, tap, None, ALU.mult)
                        v.tensor_scalar(to, sample, tap, None, ALU.mult)
                    else:
                        v.scalar_tensor_tensor(conv[:, 0:SEQ], prompt, tap, conv[:, 0:SEQ], ALU.mult, ALU.add)
                        v.scalar_tensor_tensor(to, sample, tap, to, ALU.mult, ALU.add)
                    v.drain()

            def evict_bg(i):
                n = NU * i + 2
                for half in range(2):
                    lo, hi = HALF * half, HALF * (half + 1)
                    skip = META if half == 0 else 0
                    v.wait_ge(s["half_done"], 2 * n + half + 1)
                    v.tensor_tensor(yc[:, bass.ds(i, 1), lo + skip - META:hi - META].rearrange("p a t -> p (a t)"),
                                    bank_u[half][:, skip:HALF], conv[:, lo + skip - META:hi - META], ALU.mult).then_inc(evicted[half], 1)

            def take_cache(i):
                for f in (1, 3):
                    v.wait_ge(s["o_full"], fill_o(i, f // 2) + 1)
                    v.tensor_copy(kcT[:, 4 * P * f:4 * P * (f + 1)], bank_o[:]).then_inc(s["o_free"], 1)

            def maximum(i, n, w):
                for m in range(2):
                    v.wait_ge(scores[m], fill_s(i, n) + 1)
                    if n == 0:
                        v.tensor_tensor(bank_s[m][:, 2 * P:4 * P].rearrange("p (x c) -> p x c", x=2),
                                        bank_s[m][:, 2 * P:4 * P].rearrange("p (x c) -> p x c", x=2),
                                        const[:, C_MASK + P * m:C_MASK + P * (m + 1)].rearrange("p (x c) -> p x c", x=1).to_broadcast((P, 2, P)), ALU.add)
                    else:
                        v.memset(bank_s[m][0:CHUNK, w - CHUNK:w], MASKED)
                    v.drain()
                    v.tensor_reduce(neg_max[:, m:m + 1], bank_s[m][:, 0:w], AX.X, ALU.max)
                    v.drain()
                    v.tensor_scalar(neg_max[:, m:m + 1], neg_max[:, m:m + 1], -SCALE, None, ALU.mult).then_inc(max_ready[m], 1)

            def spread_rows(i):
                for g in range(2):
                    v.wait_ge(exp_done[g], fill_s(i, 0) + 1)
                    v.reciprocal(inv[:, g:g + 1], row_sum[:, g:g + 1])
                    v.drain()
                    v.tensor_scalar(spread[:, g, :], const[:, C_SPREAD + P * g:C_SPREAD + P * (g + 1)], inv[:, g:g + 1], lam[:, 5:6],
                                    ALU.mult, ALU.mult)
                v.drain()
                v.sem_inc(s["spread_ready"], 1)

            def take_sample_mix(i):
                v.wait_ge(s["t_full"], fill_t(i, T_SAMPLE) + 1)
                for t in range(OWN):
                    to = own_T[:, t, :].rearrange("p (s c) -> p s c", c=P + NEW)[:, 0:STREAMS, 0:NEW]
                    v.tensor_copy(to, bank_t[:, P * t:P * (t + 1)].rearrange("p (s q) -> p s q", q=NEW))
                v.tensor_copy(shared_T[:], bank_t[:, 2 * P:4 * P].rearrange("p (t c) -> p t c", c=P)).then_inc(s["t_free"], 1)

            def combine_maps(i, b):
                w = keys(b)
                v.wait_ge(exp_done[0], fill_s(i, 1 + b) + 1)
                v.wait_ge(exp_done[1], fill_s(i, 1 + b) + 1)
                v.reciprocal(inv[:, 0:2], row_sum[:])
                v.drain()
                v.tensor_scalar(mix[:, b % 2, 0:w], prob[:, 0, 0:w], inv[:, 0:1], None, ALU.mult)
                v.tensor_scalar(inv[:, 2:3], inv[:, 1:2], lam[:, 4:5], None, ALU.mult)
                v.drain()
                v.scalar_tensor_tensor(mix[:, b % 2, 0:w], prob[:, 1, 0:w], inv[:, 2:3], mix[:, b % 2, 0:w], ALU.mult, ALU.add).then_inc(s["mix_ready"], 1)

            def lay_out_q(i):
                for half in range(2):
                    v.wait_ge(evicted[half], NU * i + 8)
                for m in range(2):
                    r = slice(64 * m, 64 * m + 64)
                    q = qT[r, SEQ:TOK].rearrange("p (s q) -> p s q", q=NEW)
                    v.tensor_copy(q_maps[r, :, NEW * m:NEW * (m + 1)], q)
                    for g in range(2):
                        to = q_pad[r, 4 * P * g:4 * P * g + 640].rearrange("p (s c) -> p s c", c=P + 32)
                        last = v.tensor_copy(to[:, :, NEW * m:NEW * (m + 1)], q[:, 4 * g:4 * g + 4, :])
                last.then_inc(s["q_maps_ready"], 1)

            def body(i, units, attend):
                if units:
                    split(i, 0)
                for u in range(NU):
                    if units:
                        if u + 1 < NU:
                            split(i, u + 1)
                        if UNITS[u] == "cg":
                            evict_cg(i)
                        if UNITS[u] == "bg":
                            evict_bg(i)
                    if attend:
                        if u == 0:
                            take_cache(i)
                            maximum(i, 0, 4 * P)
                            spread_rows(i)
                        if u == 1:
                            take_sample_mix(i)
                        if 1 <= u <= 4:
                            maximum(i, u, keys(u - 1))
                            combine_maps(i, u - 1)
                if units:
                    lay_out_q(i)

            turns(v, body)


def merge_branches(nc, d, keep):
    with ExitStack() as ctx:
        sb = lambda name, shape, dt=F32: ctx.enter_context(nc.sbuf_tensor(name, shape, dt))
        pb = lambda name: ctx.enter_context(nc.psum_tensor(name, [P, 512], F32))
        sem = lambda name: ctx.enter_context(nc.semaphore("m_" + name))
        yc, ya = keep["yc"], keep["ya"]
        H = TOK // 2
        w_raw = sb("mw_raw", [P, 2, KT, P])
        w_hi, w_lo = sb("mw_hi", [P, 2, KT, P], F32R), sb("mw_lo", [P, 2, KT, P], F32R)
        y_hi = [sb("yc_hi", [P, KT, TOK], F32R), sb("ya_hi", [P, KT, TOK], F32R)]
        y_lo = [sb("yc_lo", [P, KT, TOK], F32R), sb("ya_lo", [P, KT, TOK], F32R)]
        merged = sb("merged", [P, KT, TOK])
        gate_a = yc
        square, root, normed, gated = (sb(n, [P, TOK]) for n in ("square", "root", "normed", "gated"))
        ones, gain, eps = sb("ones", [P, P]), sb("gain", [P, 2]), sb("eps", [P, 1])
        bank_u = [pb("mbank_u0"), pb("mbank_u1")]
        bank_r = [pb("bank_r0"), pb("bank_r1")]
        w_loaded = [sem("w_loaded0"), sem("w_loaded1")]
        evicted = [sem("evicted0"), sem("evicted1")]
        gc_in, ga_in, gain_in, yc_hi_done, yc_lo_done, gate_ready = (sem(n) for n in ("gc_in", "ga_in", "gain_in", "yc_hi_done", "yc_lo_done", "gate_ready"))
        split_hi, split_lo, half_done, consts_done = (sem(n) for n in ("split_hi", "split_lo", "half_done", "consts_done"))
        squared, summed, rooted, norm_done, ya_hi_done, ya_lo_done, gated_sem = (sem(n) for n in ("squared", "summed", "rooted", "norm_done", "ya_hi_done", "ya_lo_done", "gated_sem"))
        block = ctx.enter_context(nc.Block())

        @block.sync
        def _(sp):
            sp.dma_start(merged[:], d["gates"][0].rearrange("k p t -> p k t")).then_inc(gc_in, 16)
            with nc.allow_non_contiguous_dma(reason="one value a partition"):
                sp.dma_start(gain[:, 0:1], d["subln_g"].rearrange("l p -> p l")).then_inc(gain_in, 16)

            def body(i, u, br):
                n = 2 * i + u
                view = d["w_branch"][0, br].rearrange("(k p) n -> p k n", p=P)
                col = (i - 4 * br) * 2 * P + u * P
                src = view[:, :, bass.ds(col if isinstance(i, int) else sp.snap(col), P)]
                wait(sp, split_lo, n - 1)
                sp.dma_start(w_raw[:, u], src).then_inc(w_loaded[u], 16)

            for u in range(2):
                body(0, u, 0)
            sp.wait_ge(yc_lo_done, KT)
            sp.dma_start(gate_a[:], d["gates"][1].rearrange("k p t -> p k t")).then_inc(ga_in, 16)
            with sp.Fori(1, 4) as i:
                for u in range(2):
                    body(i, u, 0)
            with sp.Fori(4, 8) as i:
                for u in range(2):
                    body(i, u, 1)

        def turns(eng, body):
            for u in range(2):
                body(0, u, 0)
            with eng.Fori(1, 4) as i:
                for u in range(2):
                    body(i, u, 0)
            with eng.Fori(4, 8) as i:
                for u in range(2):
                    body(i, u, 1)

        @block.tensor
        def _(pe):
            pe.wait_ge(consts_done, 1)

            def body(i, u, br):
                n = 2 * i + u
                if br == 0 and isinstance(i, int) and u == 0:
                    pe.wait_ge(yc_lo_done, KT)
                if br == 1 and u == 0:
                    pe.wait_ge(ya_lo_done, KT)
                pe.wait_ge(split_lo, n + 1)
                for half in range(2):
                    wait(pe, evicted[half], n)
                    out, cols = bank_u[half][:, 0:H], slice(H * half, H * (half + 1))
                    for k in range(KT):
                        pe.matmul(out, w_hi[:, u, k, :], y_hi[br][:, k, cols], start=(k == 0), stop=False)
                        pe.matmul(out, w_hi[:, u, k, :], y_lo[br][:, k, cols], start=False, stop=False)
                        last = pe.matmul(out, w_lo[:, u, k, :], y_hi[br][:, k, cols], start=False, stop=(k == KT - 1))
                    last.then_inc(half_done, 1)
                if br == 0:
                    pe.wait_ge(squared, n + 1)
                    wait(pe, rooted, n)
                    for half in range(2):
                        last = pe.matmul(bank_r[half][:, 0:H], ones[:], square[:, H * half:H * (half + 1)], start=True, stop=True)
                    last.then_inc(summed, 1)

            turns(pe, body)

        @block.scalar
        def _(act):
            for k in range(KT):
                act.copy(y_hi[0][:, k], yc[:, k]).then_inc(yc_hi_done, 1)

            def body(i, u, br):
                n = 2 * i + u
                act.wait_ge(w_loaded[u], 16 * (i + 1))
                wait(act, half_done, 2 * (n - 1))
                act.copy(w_hi[:, u], w_raw[:, u]).then_inc(split_hi, 1)
                if br == 0:
                    if isinstance(i, int) and u == 0:
                        act.wait_ge(gc_in, 16)
                        act.activation(merged[:], merged[:], ACT.Sigmoid).then_inc(gate_ready, 1)
                    wait(act, summed, n)
                    act.activation(square[:], ya[:, bass.ds(n, 1), :].rearrange("p a t -> p (a t)"), ACT.Square).then_inc(squared, 1)
                    act.wait_ge(summed, n + 1)
                    wait(act, norm_done, n)
                    act.activation(root[:, 0:H], bank_r[0][:, 0:H], ACT.Sqrt, bias=eps[:, 0:1], scale=1.0 / P)
                    act.activation(root[:, H:TOK], bank_r[1][:, 0:H], ACT.Sqrt, bias=eps[:, 0:1], scale=1.0 / P).then_inc(rooted, 1)
                    act.wait_ge(norm_done, n + 1)
                    act.copy(y_hi[1][:, bass.ds(n, 1), :].rearrange("p a t -> p (a t)"), normed[:]).then_inc(ya_hi_done, 1)

            act.wait_ge(consts_done, 1)
            for u in range(2):
                body(0, u, 0)
            with act.Fori(1, 4) as i:
                for u in range(2):
                    body(i, u, 0)
            act.wait_ge(ga_in, 16)
            act.activation(gate_a[:], gate_a[:], ACT.Sigmoid).then_inc(gate_ready, 1)
            with act.Fori(4, 8) as i:
                for u in range(2):
                    body(i, u, 1)

        @block.vector
        def _(v):
            v.memset(ones[:], 1.0)
            v.memset(eps[:], EPS).then_inc(consts_done, 1)
            v.wait_ge(gain_in, 16)
            v.tensor_scalar(gain[:, 1:2], gain[:, 0:1], 1.0 - LAM_INIT, None, ALU.mult)
            for k in range(KT):
                v.wait_ge(yc_hi_done, k + 1)
                v.tensor_tensor(y_lo[0][:, k], yc[:, k], y_hi[0][:, k].bitcast(F32), ALU.subtract).then_inc(yc_lo_done, 1)

            def body(i, u, br):
                n = 2 * i + u
                v.wait_ge(split_hi, n + 1)
                v.tensor_tensor(w_lo[:, u], w_raw[:, u], w_hi[:, u].bitcast(F32), ALU.subtract).then_inc(split_lo, 1)
                one = lambda t, x: t[:, bass.ds(x, 1), :].rearrange("p a t -> p (a t)")
                if br == 0:
                    v.wait_ge(rooted, n + 1)
                    wait(v, ya_hi_done, n)
                    v.tensor_scalar(normed[:], one(ya, n), gain[:, 1:2], None, ALU.mult)
                    v.reciprocal(root[:], root[:])
                    v.drain()
                    v.tensor_tensor(normed[:], normed[:], root[:], ALU.mult).then_inc(norm_done, 1)
                    v.wait_ge(ya_hi_done, n + 1)
                    v.tensor_tensor(one(y_lo[1], n), normed[:], one(y_hi[1], n).bitcast(F32), ALU.subtract).then_inc(ya_lo_done, 1)
                v.wait_ge(gate_ready, 1 + br)
                for half in range(2):
                    cols = slice(H * half, H * (half + 1))
                    pick = lambda t, x: t[:, bass.ds(x, 1), cols].rearrange("p a t -> p (a t)")
                    v.wait_ge(half_done, 2 * n + half + 1)
                    if br == 0:
                        v.tensor_tensor(pick(merged, n), bank_u[half][:, 0:H], pick(merged, n), ALU.mult).then_inc(evicted[half], 1)
                    else:
                        m = n - KT
                        v.tensor_tensor(gated[:, cols], bank_u[half][:, 0:H], pick(gate_a, m), ALU.mult).then_inc(evicted[half], 1)
                        v.drain()
                        v.tensor_tensor(pick(ya, m), gated[:, cols], pick(merged, m), ALU.add)

            turns(v, body)


def layer_norm_steps(v, pre, stats, mv, act_root, root_done, n):
    for half in range(2):
        v.bn_stats(stats[:, 6 * half:6 * half + 6], pre[:, 512 * half:512 * (half + 1)])
    v.drain()
    v.bn_aggr(mv, stats[:, 0:12]).then_inc(act_root, 1)
    v.wait_ge(root_done, n)


def route(nc, d, keep):
    with ExitStack() as ctx:
        sb = lambda name, shape, dt=F32: ctx.enter_context(nc.sbuf_tensor(name, shape, dt))
        pb = lambda name: ctx.enter_context(nc.psum_tensor(name, [P, 512], F32))
        sem = lambda name: ctx.enter_context(nc.semaphore("r_" + name))
        merged, const, h = keep["ya"], keep["const"], keep["h"]
        slots, weights, eid = keep["slots"], keep["weights"], keep["eid"]
        ident = const[:, C_ID:C_ID + P]
        w_raw = sb("wo_raw", [P, 2, D])
        w_hi, w_lo = sb("wo_hi", [P, KT, D], F32R), sb("wo_lo", [P, KT, D], F32R)
        m_hi, m_lo = sb("m_hi", [P, KT, TOK], F32R), sb("m_lo", [P, KT, TOK], F32R)
        x_rows, pre = sb("rx_rows", [P, 2, D]), sb("pre", [P, 2, D])
        hT = sb("hT", [P, KT, P])
        ln_g, ln_b = sb("ln1_g_sb", [P, D]), sb("ln1_b_sb", [P, D])
        w_router, b_router = sb("w_router_sb", [P, KT, 36]), sb("b_router_sb", [P, 36])
        stats, mv, root, eps = sb("stats", [P, 12]), sb("mv", [P, 2]), sb("root1", [P, 2]), sb("eps1", [P, 1])
        logits = sb("logits", [P, TB, 36])
        group8, top8, idx8 = sb("group8", [P, TB, 8]), sb("top8", [P, TB, 8]), sb("idx8", [P, TB, 8], U32)
        pick_f = sb("pick_f", [P, 4, TB])
        masked, offm = sb("masked", [P, TB, EXPERTS]), sb("offm", [P, TB, EXPERTS])
        first, second, both = (sb(n, [P, TB, EXPERTS]) for n in ("first", "second", "both"))
        shifted, expd = sb("shifted", [P, TB, 8]), sb("expd", [P, TB, 8])
        soft = sb("soft", [P, 6, TB])
        ones, zeros = sb("ones1", [P, P]), sb("zeros1", [P, EXPERTS])
        per_expert = sb("per_expert", [P, 6, EXPERTS])
        compare = sb("compare", [1, BLOCKS, EXPERTS])
        eid_f = sb("eid_f", [1, BLOCKS])
        tokens = sb("tokens", [P, TB], U32)
        empty = sb("empty", [BLOCKS, P], U32)
        slot_f = sb("slot_f", [P, 2, TB])

        bank = [[pb(f"rbank{a}{b}") for b in range(2)] for a in range(2)]
        bank_h = [pb("bank_h0"), pb("bank_h1")]
        bank_l, bank_c = pb("bank_l"), pb("bank_c")
        w_loaded, x_loaded, h_stored = ([sem(f"{n}{x}") for x in range(2)] for n in ("w_loaded", "x_loaded", "h_stored"))
        small_in, split_hi, split_lo, m_hi_done, m_lo_done, out_done, taken = (sem(n) for n in ("small_in", "split_hi", "split_lo", "m_hi_done", "m_lo_done", "out_done", "taken"))
        var_ready, root_done, h_ready, h_turned, h_taken, logits_done = (sem(n) for n in ("var_ready", "root_done", "h_ready", "h_turned", "h_taken", "logits_done"))
        shifted_ready, exp_ready, both_ready, counted, slots_ready, empty_ready, table_sem, consts_done = (sem(n) for n in ("shifted_ready", "exp_ready", "both_ready", "counted", "slots_ready", "empty_ready", "table_sem", "consts_done"))
        block = ctx.enter_context(nc.Block())
        SMALL = 16 * 6

        @block.sync
        def _(sp):
            for k in range(KT):
                wait(sp, split_lo, k - 1)
                sp.dma_start(w_raw[:, k % 2], d["w_out"][0, P * k:P * (k + 1), :]).then_inc(w_loaded[k % 2], 16)
                if k < 2:
                    sp.dma_start(x_rows[:, k], d["x_prompt"][0, P * k:P * (k + 1), :]).then_inc(x_loaded[k], 16)
                if k == 1:
                    sp.dma_start(ln_g[:], d["ln1_g"].to_broadcast((P, D))).then_inc(small_in, 16)
                    sp.dma_start(ln_b[:], d["ln1_b"].to_broadcast((P, D))).then_inc(small_in, 16)
                    sp.dma_start(b_router[:, 0:4], d["b_group"].to_broadcast((P, 4))).then_inc(small_in, 16)
                    sp.dma_start(b_router[:, 4:36], d["b_router"].to_broadcast((P, 32))).then_inc(small_in, 16)
                    sp.dma_start(w_router[:, :, 0:4], d["w_group"][0].rearrange("(k p) n -> p k n", p=P)).then_inc(small_in, 16)
                    sp.dma_start(w_router[:, :, 4:36], d["w_router"][0].rearrange("(k p) n -> p k n", p=P)).then_inc(small_in, 16)
            for b in range(2, TB):
                src = d["x_prompt"][0, P * b:P * (b + 1), :] if b < QB else d["x_sample"].rearrange("s q d -> (s q) d")
                sp.wait_ge(taken, b - 1)
                sp.dma_start(x_rows[:, b % 2], src).then_inc(x_loaded[b % 2], 16)
            for b in range(TB):
                sp.wait_ge(h_ready, b + 1)
                sp.dma_start(d["h_rows"][P * b:P * (b + 1), :], h[:, b, :]).then_inc(h_stored[b % 2], 16)
            sp.wait_ge(h_stored[0], 48)
            sp.wait_ge(h_stored[1], 32)

        @block.tensor
        def _(pe):
            def out_rows(b):
                wait(pe, taken, b - 1)
                pe.wait_ge(m_lo_done, KT)
                for k in range(KT):
                    pe.wait_ge(split_lo, k + 1)
                    rows = slice(P * b, P * (b + 1))
                    for strip in range(2):
                        out, cols = bank[b % 2][strip][:], slice(512 * strip, 512 * (strip + 1))
                        pe.matmul(out, m_hi[:, k, rows], w_hi[:, k, cols], start=(k == 0), stop=False)
                        pe.matmul(out, m_hi[:, k, rows], w_lo[:, k, cols], start=False, stop=False)
                        last = pe.matmul(out, m_lo[:, k, rows], w_hi[:, k, cols], start=False, stop=(k == KT - 1))
                last.then_inc(out_done, 1)

            def router(b):
                pe.wait_ge(h_ready, b + 1)
                wait(pe, h_taken, 2 * b)
                for k in range(KT):
                    last = pe.transpose(bank_h[k // 4][:, P * (k % 4):P * (k % 4 + 1)], h[:, b, P * k:P * (k + 1)], ident)
                    if k % 4 == 3:
                        last.then_inc(h_turned, 1)
                pe.wait_ge(h_taken, 2 * b + 2)
                if b == 0:
                    pe.wait_ge(small_in, SMALL)
                for k in range(KT):
                    last = pe.matmul(bank_l[:, 64 * b:64 * b + 36], hT[:, k, :], w_router[:, k, :], start=(k == 0), stop=(k == KT - 1))
                last.then_inc(logits_done, 1)

            for b in range(TB + 1):
                if b < TB:
                    out_rows(b)
                if b > 0:
                    router(b - 1)
            pe.wait_ge(both_ready, 1)
            pe.wait_ge(consts_done, 1)
            for b in range(TB):
                out = bank_c[:, EXPERTS * b:EXPERTS * (b + 1)]
                for a in range(b):
                    pe.matmul(out, ones[:], both[:, a, :], start=(a == 0), stop=False)
                pe.matmul(out, const[:, C_UPPER:C_UPPER + P], both[:, b, :], start=(b == 0), stop=True)
            for b in range(TB):
                last = pe.matmul(bank_c[:, EXPERTS * TB:EXPERTS * (TB + 1)], ones[:], both[:, b, :], start=(b == 0), stop=(b == TB - 1))
            last.then_inc(counted, 1)

        @block.scalar
        def _(act):
            for k in range(KT):
                act.copy(m_hi[:, k], merged[:, k]).then_inc(m_hi_done, 1)
                act.wait_ge(w_loaded[k % 2], 16 * (k // 2 + 1))
                act.copy(w_hi[:, k], w_raw[:, k % 2]).then_inc(split_hi, 1)
            act.wait_ge(consts_done, 1)
            for b in range(TB):
                act.wait_ge(var_ready, b + 1)
                act.activation(root[:, 0:1], mv[:, 1:2], ACT.Sqrt, bias=eps[:, 0:1], scale=1.0).then_inc(root_done, 1)
                for half in range(2):
                    act.wait_ge(h_turned, 2 * b + half + 1)
                    wait(act, logits_done, b)
                    act.copy(hT[:, 4 * half:4 * half + 4, :], bank_h[half][:].rearrange("p (k c) -> p k c", k=4)).then_inc(h_taken, 1)
            act.wait_ge(shifted_ready, 1)
            act.activation(expd[:], shifted[:], ACT.Exp).then_inc(exp_ready, 1)

        @block.gpsimd
        def _(g):
            g.wait_ge(empty_ready, 1)
            g.dma_start(d["slot_token"].rearrange("(b p) a -> b (p a)", p=P), empty[:]).then_inc(table_sem, 16)
            g.wait_ge(table_sem, 16)
            g.wait_ge(slots_ready, 1)
            for n in range(2):
                for b in range(TB):
                    g.indirect_dma_start(out=d["slot_token"], out_offset=bass.IndirectOffsetOnAxis(ap=slots[:, n, b:b + 1], axis=0),
                                         in_=tokens[:, b:b + 1], in_offset=None).then_inc(table_sem, 16)
            g.wait_ge(table_sem, 16 * (1 + 2 * TB))

        @block.vector
        def _(v):
            v.memset(ones[:], 1.0)
            v.memset(zeros[:], 0.0)
            v.memset(eps[:], EPS).then_inc(consts_done, 1)
            v.tensor_copy(tokens[:], const[:, C_TOKEN:C_TOKEN + TB])
            v.tensor_scalar(empty[:], const[0:BLOCKS, 0:P], 0.0, None, ALU.mult).then_inc(empty_ready, 1)
            v.memset(group8[:], MASKED)
            for k in range(KT):
                v.wait_ge(m_hi_done, k + 1)
                v.tensor_tensor(m_lo[:, k], merged[:, k], m_hi[:, k].bitcast(F32), ALU.subtract).then_inc(m_lo_done, 1)
                v.wait_ge(split_hi, k + 1)
                v.tensor_tensor(w_lo[:, k], w_raw[:, k % 2], w_hi[:, k].bitcast(F32), ALU.subtract).then_inc(split_lo, 1)
            v.wait_ge(small_in, SMALL)
            for b in range(TB):
                v.wait_ge(out_done, b + 1)
                v.wait_ge(x_loaded[b % 2], 16 * (b // 2 + 1))
                p = pre[:, b % 2, :]
                for strip in range(2):
                    cols = slice(512 * strip, 512 * (strip + 1))
                    last = v.scalar_tensor_tensor(p[:, cols], x_rows[:, b % 2, cols], ALPHA, bank[b % 2][strip][:], ALU.mult, ALU.add)
                last.then_inc(taken, 1)
                v.drain()
                layer_norm_steps(v, p, stats, mv[:], var_ready, root_done, b + 1)
                v.reciprocal(root[:, 1:2], root[:, 0:1])
                v.drain()
                v.tensor_scalar(p, p, mv[:, 0:1], root[:, 1:2], ALU.subtract, ALU.mult)
                v.drain()
                v.tensor_tensor(p, p, ln_g[:], ALU.mult)
                v.drain()
                v.tensor_tensor(h[:, b, :], p, ln_b[:], ALU.add).then_inc(h_ready, 1)

            v.wait_ge(logits_done, TB)
            v.tensor_tensor(logits[:], bank_l[:, 0:64 * TB].rearrange("p (b c) -> p b c", b=TB)[:, :, 0:36],
                            b_router[:].rearrange("p (a c) -> p a c", a=1).to_broadcast((P, TB, 36)), ALU.add)
            v.drain()
            v.tensor_copy(group8[:, :, 0:GROUPS], logits[:, :, 0:GROUPS])
            v.drain()
            for b in range(TB):
                v.max(top8[:, b, :], group8[:, b, :])
            v.drain()
            for b in range(TB):
                v.max_index(idx8[:, b, :], top8[:, b, :], group8[:, b, :])
            v.drain()
            v.tensor_copy(pick_f[:, 0, :], idx8[:, :, 0])
            v.tensor_tensor(shifted[:, :, 0:GROUPS], logits[:, :, 0:GROUPS], top8[:, :, 0:1].to_broadcast((P, TB, GROUPS)), ALU.subtract)
            v.drain()
            for b in range(TB):
                v.tensor_scalar(masked[:, b, :], const[:, C_GROUP:C_GROUP + EXPERTS], pick_f[:, 0, b:b + 1], None, ALU.is_equal)
            v.drain()
            v.tensor_scalar(offm[:], masked[:], -MASKED, MASKED, ALU.mult, ALU.add)
            v.tensor_tensor(masked[:], masked[:], logits[:, :, GROUPS:GROUPS + EXPERTS], ALU.mult)
            v.drain()
            v.tensor_tensor(masked[:], masked[:], offm[:], ALU.add)
            v.drain()
            for b in range(TB):
                v.max(top8[:, b, :], masked[:, b, :])
            v.drain()
            for b in range(TB):
                v.max_index(idx8[:, b, :], top8[:, b, :], masked[:, b, :])
            v.drain()
            v.tensor_copy(pick_f[:, 1, :], idx8[:, :, 0])
            v.tensor_copy(pick_f[:, 2, :], idx8[:, :, 1])
            v.memset(shifted[:, :, 5:8], 0.0)
            v.tensor_tensor(shifted[:, :, 4:5], top8[:, :, 1:2], top8[:, :, 0:1], ALU.subtract).then_inc(shifted_ready, 1)
            v.drain()
            for n, hot in enumerate((first, second)):
                for b in range(TB):
                    v.tensor_scalar(hot[:, b, :], const[:, C_EXPERT:C_EXPERT + EXPERTS], pick_f[:, 1 + n, b:b + 1], None, ALU.is_equal)
            v.drain()
            v.tensor_tensor(both[:], first[:], second[:], ALU.add).then_inc(both_ready, 1)
            v.wait_ge(exp_ready, 1)
            v.tensor_reduce(soft[:, 0, :], expd[:, :, 0:GROUPS], AX.X, ALU.add)
            v.tensor_scalar(soft[:, 1, :], expd[:, :, 4], 1.0, None, ALU.add)
            v.drain()
            v.tensor_tensor(soft[:, 2, :], soft[:, 0, :], soft[:, 1, :], ALU.mult)
            v.drain()
            v.reciprocal(weights[:, 0, :], soft[:, 2, :])
            v.drain()
            v.tensor_tensor(weights[:, 1, :], weights[:, 0, :], expd[:, :, 4], ALU.mult)
            v.wait_ge(counted, 1)
            counts, n_blocks, tmp, ends, starts = (per_expert[:, x, :] for x in range(5))
            v.tensor_copy(counts, bank_c[:, EXPERTS * TB:EXPERTS * (TB + 1)])
            v.memset(n_blocks, 0.0)
            v.drain()
            for x in range(TB):
                v.scalar_tensor_tensor(n_blocks, counts, float(P * x), n_blocks, ALU.is_gt, ALU.add)
                v.drain()
            v.tensor_tensor_scan(ends, n_blocks, zeros[:], 0.0, ALU.add, ALU.add)
            v.drain()
            v.tensor_tensor(starts, ends, n_blocks, ALU.subtract)
            v.drain()
            v.tensor_scalar(starts, starts, float(P), None, ALU.mult)
            v.drain()
            v.tensor_tensor(offm[:], bank_c[:, 0:EXPERTS * TB].rearrange("p (b e) -> p b e", b=TB),
                            per_expert[:, 4:5, :].to_broadcast((P, TB, EXPERTS)), ALU.add)
            v.drain()
            for n, hot in enumerate((first, second)):
                v.tensor_tensor(masked[:], hot[:], offm[:], ALU.mult)
                v.drain()
                v.tensor_reduce(slot_f[:, n, :], masked[:], AX.X, ALU.add)
                v.drain()
            v.tensor_copy(slots[:], slot_f[:]).then_inc(slots_ready, 1)
            v.tensor_tensor(compare[:], per_expert[0:1, 3:4, :].to_broadcast((1, BLOCKS, EXPERTS)),
                            const[0:1, C_BLOCK:C_BLOCK + BLOCKS].rearrange("p (j a) -> p j a", a=1).to_broadcast((1, BLOCKS, EXPERTS)), ALU.is_le)
            v.drain()
            v.tensor_reduce(eid_f[:], compare[:], AX.X, ALU.add)
            v.drain()
            v.tensor_scalar(eid_f[:], eid_f[:], float(EXPERTS - 1), None, ALU.min)
            v.drain()
            v.tensor_copy(eid[:], eid_f[:])


def run_experts(nc, d, keep):
    with ExitStack() as ctx:
        sb = lambda name, shape, dt=F32: ctx.enter_context(nc.sbuf_tensor(name, shape, dt))
        pb = lambda name: ctx.enter_context(nc.psum_tensor(name, [P, 512], F32))
        sem = lambda name: ctx.enter_context(nc.semaphore("e_" + name))
        const, eid = keep["const"], keep["eid"]
        ident = const[:, C_ID:C_ID + P]
        up_raw, down_raw = sb("up_raw", [P, 2, KT, 512]), sb("down_raw", [P, 2, 2, D])
        up_hi, up_lo = sb("up_hi", [P, KT, 512], F32R), sb("up_lo", [P, KT, 512], F32R)
        down_hi, down_lo = sb("down_hi", [P, 2, D], F32R), sb("down_lo", [P, 2, D], F32R)
        rows = sb("rows", [P, 2, D])
        xT_hi, xT_lo = sb("xT_hi", [P, KT, P], F32R), sb("xT_lo", [P, KT, P], F32R)
        silu, act_rows = sb("silu", [P, DE]), sb("act_rows", [P, DE])
        aT_hi, aT_lo = sb("aT_hi", [P, 2, P], F32R), sb("aT_lo", [P, 2, P], F32R)
        y_rows = sb("y_rows", [P, 2, D])
        slot_token = sb("slot_token_sb", [P, BLOCKS], U32)
        bank_g = [pb("bank_g0"), pb("bank_g1")]
        bank_x = [pb("bank_x0"), pb("bank_x1")]
        bank_a = pb("bank_a")
        bank_d = [pb("bank_d0"), pb("bank_d1")]
        two = lambda n: [sem(n + "0"), sem(n + "1")]
        up_in, down_in, rows_in, y_stored = two("up_in"), two("down_in"), two("rows_in"), two("y_stored")
        (tokens_in, up_hi_done, up_lo_done, up_used, down_hi_done, down_lo_done, down_used, x_turned, x_hi_done, x_lo_done,
         silu_done, act_done, a_turned, a_hi_done, a_lo_done, y_left, y_right) = (sem(n) for n in (
             "tokens_in", "up_hi_done", "up_lo_done", "up_used", "down_hi_done", "down_lo_done", "down_used", "x_turned", "x_hi_done",
             "x_lo_done", "silu_done", "act_done", "a_turned", "a_hi_done", "a_lo_done", "y_left", "y_right"))
        block = ctx.enter_context(nc.Block())
        LAST = BLOCKS - 1

        def turns(eng, body):
            for j in range(3):
                body(j, j // 2, j % 2, j == 0, False)
            pairs = (BLOCKS - 4) // 2
            with eng.Fori(1, pairs + 1) as i:
                body(2 * i + 1, i, 1, False, False)
                body(2 * i + 2, i + 1, 0, False, False)
            for j in range(2 * pairs + 3, BLOCKS):
                body(j, j // 2, j % 2, False, j == LAST)

        @block.sync
        def _(sp):
            def body(j, n, par, first, last):
                e = sp.value_load(eid[0:1, bass.ds(j, 1)], min_val=0, max_val=EXPERTS - 1)
                up = d["w_gate_up"][0, bass.ds(e, 1)].rearrange("a (k p) n -> p (a k) n", p=P)
                down = d["w_down"][0, bass.ds(e, 1)].rearrange("a (k p) n -> p (a k) n", p=P)
                wait(sp, up_lo_done, 4 * j - 4)
                sp.dma_start(up_raw[:, par], up).then_inc(up_in[par], 16)
                wait(sp, down_lo_done, 2 * j - 2)
                sp.dma_start(down_raw[:, par], down).then_inc(down_in[par], 16)

            turns(sp, body)

        @block.gpsimd
        def _(g):
            with nc.allow_non_contiguous_dma(reason="a column of token numbers for each block"):
                g.dma_start(slot_token[:], d["slot_token"].rearrange("(b p) a -> p (b a)", p=P)).then_inc(tokens_in, 16)
            g.wait_ge(tokens_in, 16)
            for j in range(BLOCKS):
                wait(g, x_turned, 2 * (j - 1))
                g.indirect_dma_start(out=rows[:, j % 2, :], out_offset=None, in_=d["h_rows"],
                                     in_offset=bass.IndirectOffsetOnAxis(ap=slot_token[:, j:j + 1], axis=0)).then_inc(rows_in[j % 2], 16)

        @block.tensor
        def _(pe):
            def turn_rows(j, n, par):
                pe.wait_ge(rows_in[par], 16 * (n + 1))
                for half in range(2):
                    wait(pe, x_lo_done, 2 * j - 1 + half)
                    for k in range(4):
                        kk = 4 * half + k
                        last = pe.transpose(bank_x[half][:, P * k:P * (k + 1)], rows[:, par, P * kk:P * (kk + 1)], ident)
                    last.then_inc(x_turned, 1)

            def gate_up(j, par):
                pe.wait_ge(x_lo_done, 2 * j + 2)
                wait(pe, act_done, j - 1)
                for k in range(KT):
                    if k % 2 == 0:
                        pe.wait_ge(up_lo_done, 4 * j + k // 2 + 1)
                    pe.matmul(bank_g[par][:], xT_hi[:, k, :], up_hi[:, k, :], start=(k == 0), stop=False)
                    pe.matmul(bank_g[par][:], xT_hi[:, k, :], up_lo[:, k, :], start=False, stop=False)
                    last = pe.matmul(bank_g[par][:], xT_lo[:, k, :], up_hi[:, k, :], start=False, stop=(k == KT - 1))
                    if k % 2 == 1:
                        last.then_inc(up_used, 1)

            def turn_act(j):
                pe.wait_ge(act_done, j + 1)
                wait(pe, a_lo_done, j)
                for k in range(2):
                    last = pe.transpose(bank_a[:, P * k:P * (k + 1)], act_rows[:, P * k:P * (k + 1)], ident)
                last.then_inc(a_turned, 1)

            def down(j):
                pe.wait_ge(a_lo_done, j + 1)
                wait(pe, y_left, j)
                wait(pe, y_right, j)
                for k in range(2):
                    pe.wait_ge(down_lo_done, 2 * j + k + 1)
                    for strip in range(2):
                        cols = slice(512 * strip, 512 * (strip + 1))
                        pe.matmul(bank_d[strip][:], aT_hi[:, k, :], down_hi[:, k, cols], start=(k == 0), stop=False)
                        pe.matmul(bank_d[strip][:], aT_hi[:, k, :], down_lo[:, k, cols], start=False, stop=False)
                        last = pe.matmul(bank_d[strip][:], aT_lo[:, k, :], down_hi[:, k, cols], start=False, stop=(k == 1))
                    last.then_inc(down_used, 1)

            def body(j, n, par, first, last):
                gate_up(j, par)
                if not first:
                    down(j - 1)
                if not last:
                    turn_rows(j + 1, n + 1 if par else n, 1 - par)
                turn_act(j)

            turn_rows(0, 0, 0)
            turns(pe, body)
            down(LAST)

        @block.scalar
        def _(act):
            def split_up(j, n, par):
                act.wait_ge(up_in[par], 16 * (n + 1))
                for x in range(4):
                    wait(act, up_used, 4 * j - 3 + x)
                    act.copy(up_hi[:, 2 * x:2 * x + 2, :], up_raw[:, par, 2 * x:2 * x + 2, :]).then_inc(up_hi_done, 1)

            def split_down(j, n, par):
                act.wait_ge(down_in[par], 16 * (n + 1))
                for x in range(2):
                    wait(act, down_used, 2 * j - 1 + x)
                    act.copy(down_hi[:, x, :], down_raw[:, par, x, :]).then_inc(down_hi_done, 1)

            def take_rows(j):
                for half in range(2):
                    act.wait_ge(x_turned, 2 * j + half + 1)
                    act.copy(xT_hi[:, 4 * half:4 * half + 4, :], bank_x[half][:].rearrange("p (k c) -> p k c", k=4)).then_inc(x_hi_done, 1)

            def store(j, par, n):
                act.wait_ge(down_used, 2 * j + 2)
                wait(act, y_stored[par], 16 * n)
                act.copy(y_rows[:, par, 0:512], bank_d[0][:]).then_inc(y_left, 1)
                act.wait_ge(y_left, j + 1)
                act.wait_ge(y_right, j + 1)
                act.dma_start(d["y_slots"][bass.ds(j, 1)].rearrange("a p n -> (a p) n"), y_rows[:, par, :]).then_inc(y_stored[par], 16)

            def body(j, n, par, first, last):
                after = (j + 1, n + 1 if par else n, 1 - par)
                if not last:
                    split_up(*after)
                act.wait_ge(up_used, 4 * j + 4)
                wait(act, act_done, j)
                act.activation(silu[:], bank_g[par][:, 0:DE], ACT.Silu).then_inc(silu_done, 1)
                if not first:
                    store(j - 1, 1 - par, n if par else n - 1)
                split_down(j, n, par)
                if not last:
                    take_rows(j + 1)
                act.wait_ge(a_turned, j + 1)
                act.copy(aT_hi[:], bank_a[:, 0:2 * P].rearrange("p (k c) -> p k c", k=2)).then_inc(a_hi_done, 1)

            split_up(0, 0, 0)
            take_rows(0)
            turns(act, body)
            store(LAST, LAST % 2, LAST // 2)
            act.wait_ge(y_stored[0], 16 * ((BLOCKS + 1) // 2))
            act.wait_ge(y_stored[1], 16 * (BLOCKS // 2))

        @block.vector
        def _(v):
            def split_up(j, par):
                for x in range(4):
                    v.wait_ge(up_hi_done, 4 * j + x + 1)
                    s = slice(2 * x, 2 * x + 2)
                    v.tensor_tensor(up_lo[:, s, :], up_raw[:, par, s, :], up_hi[:, s, :].bitcast(F32), ALU.subtract).then_inc(up_lo_done, 1)

            def take_rows(j):
                for half in range(2):
                    v.wait_ge(x_hi_done, 2 * j + half + 1)
                    s = slice(4 * half, 4 * half + 4)
                    v.tensor_tensor(xT_lo[:, s, :], bank_x[half][:].rearrange("p (k c) -> p k c", k=4), xT_hi[:, s, :].bitcast(F32),
                                    ALU.subtract).then_inc(x_lo_done, 1)

            def store(j, par, n):
                v.wait_ge(down_used, 2 * j + 2)
                wait(v, y_stored[par], 16 * n)
                v.tensor_copy(y_rows[:, par, 512:D], bank_d[1][:]).then_inc(y_right, 1)

            def body(j, n, par, first, last):
                if not last:
                    split_up(j + 1, 1 - par)
                v.wait_ge(silu_done, j + 1)
                wait(v, a_turned, j)
                v.tensor_tensor(act_rows[:], silu[:], bank_g[par][:, DE:2 * DE], ALU.mult).then_inc(act_done, 1)
                if not first:
                    store(j - 1, 1 - par, n if par else n - 1)
                for x in range(2):
                    v.wait_ge(down_hi_done, 2 * j + x + 1)
                    v.tensor_tensor(down_lo[:, x, :], down_raw[:, par, x, :], down_hi[:, x, :].bitcast(F32), ALU.subtract).then_inc(down_lo_done, 1)
                if not last:
                    take_rows(j + 1)
                v.wait_ge(a_hi_done, j + 1)
                v.tensor_tensor(aT_lo[:], bank_a[:, 0:2 * P].rearrange("p (k c) -> p k c", k=2), aT_hi[:].bitcast(F32), ALU.subtract).then_inc(a_lo_done, 1)

            split_up(0, 0)
            take_rows(0)
            turns(v, body)
            store(LAST, LAST % 2, LAST // 2)


def combine(nc, d, keep):
    with ExitStack() as ctx:
        sb = lambda name, shape, dt=F32: ctx.enter_context(nc.sbuf_tensor(name, shape, dt))
        sem = lambda name: ctx.enter_context(nc.semaphore("c_" + name))
        h, slots, weights = keep["h"], keep["slots"], keep["weights"]
        ln_g, ln_b = sb("ln2_g_sb", [P, D]), sb("ln2_b_sb", [P, D])
        picked = sb("picked", [P, TB, 2, D])
        stats, mv, root, eps = sb("stats2", [P, 12]), sb("mv2", [P, 2]), sb("root2", [P, 2]), sb("eps2", [P, 1])
        picked_in = [sem(f"picked_in{b}") for b in range(TB)]
        small_in, var_ready, root_done, y_ready, y_stored, consts_done = (sem(n) for n in ("small_in", "var_ready", "root_done", "y_ready", "y_stored", "consts_done"))
        block = ctx.enter_context(nc.Block())

        @block.gpsimd
        def _(g):
            for b in range(TB):
                for n in range(2):
                    g.indirect_dma_start(out=picked[:, b, n, :], out_offset=None, in_=d["y_slots"].rearrange("b p n -> (b p) n"),
                                         in_offset=bass.IndirectOffsetOnAxis(ap=slots[:, n, b:b + 1], axis=0)).then_inc(picked_in[b], 16)

        @block.sync
        def _(sp):
            sp.dma_start(ln_g[:], d["ln2_g"].to_broadcast((P, D))).then_inc(small_in, 16)
            sp.dma_start(ln_b[:], d["ln2_b"].to_broadcast((P, D))).then_inc(small_in, 16)
            for b in range(TB):
                sp.wait_ge(y_ready, b + 1)
                out = d["y_prompt"][0, P * b:P * (b + 1), :] if b < QB else d["y_sample"].rearrange("s q d -> (s q) d")
                sp.dma_start(out, picked[:, b, 0, :]).then_inc(y_stored, 16)
            sp.wait_ge(y_stored, 16 * TB)

        @block.scalar
        def _(act):
            act.wait_ge(consts_done, 1)
            for b in range(TB):
                act.wait_ge(var_ready, b + 1)
                act.activation(root[:, 0:1], mv[:, 1:2], ACT.Sqrt, bias=eps[:, 0:1], scale=1.0).then_inc(root_done, 1)

        @block.vector
        def _(v):
            v.memset(eps[:], EPS).then_inc(consts_done, 1)
            v.wait_ge(small_in, 32)
            for b in range(TB):
                y = picked[:, b, 0, :]
                v.wait_ge(picked_in[b], 32)
                v.tensor_scalar(y, y, weights[:, 0, b:b + 1], None, ALU.mult)
                v.drain()
                v.scalar_tensor_tensor(y, picked[:, b, 1, :], weights[:, 1, b:b + 1], y, ALU.mult, ALU.add)
                v.drain()
                v.scalar_tensor_tensor(y, h[:, b, :], ALPHA, y, ALU.mult, ALU.add)
                v.drain()
                layer_norm_steps(v, y, stats, mv[:], var_ready, root_done, b + 1)
                v.reciprocal(root[:, 1:2], root[:, 0:1])
                v.drain()
                v.tensor_scalar(y, y, mv[:, 0:1], root[:, 1:2], ALU.subtract, ALU.mult)
                v.drain()
                v.tensor_tensor(y, y, ln_g[:], ALU.mult)
                v.drain()
                v.tensor_tensor(y, y, ln_b[:], ALU.add).then_inc(y_ready, 1)


def program(nc, d):
    with ExitStack() as ctx:
        sb = lambda name, shape, dt=F32: ctx.enter_context(nc.sbuf_tensor(name, shape, dt))
        keep = {"const": sb("const_sb", [P, C_END]), "yc": sb("yc", [P, KT, TOK]), "ya": sb("ya", [P, KT, TOK]),
                "slots": sb("slots", [P, 2, TB], U32), "weights": sb("weights", [P, 2, TB]), "eid": sb("eid", [1, BLOCKS], I32)}
        keep["h"] = keep["yc"][:].rearrange("p k t -> p (k t)").rearrange("p (b n) -> p b n", n=D)
        d["gates"] = nc.dram_tensor("gates", [2, KT, P, TOK], F32).ap()
        d["h_rows"] = nc.dram_tensor("h_rows", [TOK, D], F32).ap()
        d["slot_token"] = nc.dram_tensor("slot_token", [BLOCKS * P, 1], U32).ap()
        d["y_slots"] = nc.dram_tensor("y_slots", [BLOCKS, P, D], F32).ap()
        project_and_attend(nc, d, keep)
        merge_branches(nc, d, keep)
        route(nc, d, keep)
        run_experts(nc, d, keep)
        combine(nc, d, keep)


INPUTS = ["x_prompt", "x_sample", "cache_k", "cache_v", "state_conv", "meta_tokens", "w_in", "conv_w", "lambda_qk", "subln_g",
          "w_branch", "w_out", "ln1_g", "ln1_b", "w_group", "b_group", "w_router", "b_router", "w_gate_up", "w_down", "ln2_g", "ln2_b"]
OUTPUTS = {
    "y_prompt": (1, SEQ, D), "y_sample": (STREAMS, NEW, D),
    "new_k_prompt": (1, 1, META + SEQ, HEADS, P), "new_v_prompt": (1, 1, META + SEQ, HEADS, P), "new_conv_prompt": (1, 1, 2, D),
    "new_k_sample": (1, STREAMS, NEW, HEADS, P), "new_v_sample": (1, STREAMS, NEW, HEADS, P), "new_conv_sample": (1, STREAMS, 2, D),
}


def kernel(**inputs):
    import concourse.bacc as bacc
    from concourse.bass_utils import run_bass_kernel_spmd

    nc = bacc.Bacc("TRN2", target_bir_lowering=False, num_devices=1)
    arrays = {name: np.ascontiguousarray(inputs[name]) for name in INPUTS}
    arrays["const"] = constants()
    d = {name: nc.dram_tensor("in_" + name, a.shape, F32, kind="ExternalInput").ap() for name, a in arrays.items()}
    for name, shape in OUTPUTS.items():
        d[name] = nc.dram_tensor("out_" + name, shape, F32, kind="ExternalOutput").ap()
    program(nc, d)
    result = run_bass_kernel_spmd(nc, [{"in_" + n: a for n, a in arrays.items()}], core_ids=[0])
    return tuple(result.results[0]["out_" + name] for name in OUTPUTS)
```

```python
from contextlib import ExitStack

import concourse.bass as bass
import numpy as np
from concourse import mybir

F32 = mybir.dt.float32
F32R = mybir.dt.float32r
U32 = mybir.dt.uint32
I32 = mybir.dt.int32
ALU = mybir.AluOpType
ACT = mybir.ActivationFunctionType
AX = mybir.AxisListType

P = 128
D = 1024
KT = D // P
META, SEQ, STREAMS, NEW, PAST = 16, 512, 8, 16, 256
SAMPLE = STREAMS * NEW
T = META + SEQ + SAMPLE
TOK = SEQ + SAMPLE
HALF = T // 2
TB = TOK // P
QB = SEQ // P
CHUNK = 64
HEADS = 8
CACHED = META + PAST
OWN = 2
LAM_INIT = 0.2
ALPHA = 2.0 ** 0.25
EPS = 1e-5
SCALE = 64 ** -0.5
MASKED = -1e30
EXPERTS, PER_GROUP, GROUPS = 32, 8, 4
DE = 256
SPARE = (2 * TOK) // (P + 1)
BLOCKS = EXPERTS + SPARE
NONE = 1 << 15
COL = {"h": 0, "bg": D, "cg": 2 * D, "q": 3 * D, "k": 4 * D, "v": 5 * D, "gc": 6 * D, "ga": 7 * D}
UNITS = ["h", "cg", "bg", "gc", "ga", "k", "v", "q"]
NU = len(UNITS)

C_ID, C_SPREAD, C_MASK, C_UPPER = 0, 128, 384, 640
C_GROUP, C_EXPERT, C_BLOCK, C_FIRST, C_SIGN, C_TOKEN, C_END = 768, 800, 832, 848, 880, 881, 892


def constants():
    c = np.zeros((P, C_END), np.float32)
    row = np.arange(P)
    c[:, C_ID:C_ID + P] = np.eye(P)
    for g in range(2):
        for r in range(P):
            s, q = 4 * g + r // 32, r % 16
            c[r, C_SPREAD + P * g + 16 * s + q] = 1.0
            c[r, C_MASK + P * g:C_MASK + P * (g + 1)] = np.where(row // 16 == s, 0.0, MASKED)
    c[:, C_UPPER:C_UPPER + P] = row[:, None] < row[None, :]
    c[:, C_GROUP:C_GROUP + EXPERTS] = np.arange(EXPERTS) // PER_GROUP
    c[:, C_EXPERT:C_EXPERT + EXPERTS] = np.arange(EXPERTS)
    c[:, C_BLOCK:C_BLOCK + SPARE] = np.arange(SPARE)
    c[:, C_FIRST:C_FIRST + EXPERTS] = np.arange(EXPERTS) * P
    c[:, C_SIGN] = (row // 16) % 2
    for n in range(2 * TB):
        c[:, C_TOKEN + n] = P * n + row
    return c


def wait(eng, sem, value):
    if not isinstance(value, int) or value > 0:
        eng.wait_ge(sem, value)


def project_and_attend(nc, d, keep):
    with ExitStack() as ctx:
        sb = lambda name, shape, dt=F32: ctx.enter_context(nc.sbuf_tensor(name, shape, dt))
        pb = lambda name, shape: ctx.enter_context(nc.psum_tensor(name, shape, F32))
        sem = lambda name: ctx.enter_context(nc.semaphore(name))
        yc, ya, const = keep["yc"], keep["ya"], keep["const"]

        x_hi, x_lo = sb("x_hi", [P, KT, T], F32R), sb("x_lo", [P, KT, T], F32R)
        w_raw = sb("w_raw", [P, 2, KT, P])
        w_hi, w_lo = sb("w_hi", [P, 2, KT, P], F32R), sb("w_lo", [P, 2, KT, P], F32R)
        h_buf, u_buf, conv = sb("h_buf", [P, T]), sb("u_buf", [P, T]), sb("conv", [P, TOK])
        u_hist = sb("u_hist", [P, STREAMS, NEW + 2])
        u_last = sb("u_last", [P, KT, 18])
        hist_T = sb("hist_T", [P, KT, 16])
        taps = sb("taps", [P, KT, 3])
        gate = sb("gate", [P, 2, TOK])
        kT, vT, qT = sb("kT", [P, T]), sb("vT", [P, T]), sb("qT", [P, TOK])
        q_maps = sb("q_maps", [P, STREAMS, 32])
        q_pad = sb("q_pad", [P, STREAMS * P + P])
        k_rows, v_rows = sb("k_rows", [P, 6, P]), sb("v_rows", [P, 6, P])
        k_cache, v_cache = sb("k_cache", [P, 17, P]), sb("v_cache", [P, 17, P])
        kcT = sb("kcT", [P, 17 * P])
        prob = sb("prob", [P, 2, META + SEQ])
        mix = sb("mix", [P, 2, META + SEQ])
        mixT, mixT_meta = sb("mixT", [P, QB, SEQ]), sb("mixT_meta", [META, SEQ])
        own_T = sb("own_T", [P, OWN, STREAMS * P + P])
        shared_T = sb("shared_T", [P, 2, P])
        spread = sb("spread", [P, 2, P])
        neg_max, row_sum = sb("neg_max", [P, 2]), sb("row_sum", [P, 2])
        inv = sb("inv", [P, 4])
        lam = sb("lam", [P, 8])
        lam_in, lam_tmp = sb("lam_in", [P, 256]), sb("lam_tmp", [P, 64])
        x_rows = [k_cache[:, 0:8, :].rearrange("p a b -> p (a b)"), v_cache[:, 0:8, :].rearrange("p a b -> p (a b)")]
        meta_rows = kcT[0:META, 0:D]
        state_rows = mixT[0:16, 0:2, :].rearrange("p a b -> p (a b)")
        last_rows = mixT[0:18, 0:2, :].rearrange("p a b -> p (a b)")

        bank_u = [pb("bank_u0", [P, 512]), pb("bank_u1", [P, 512])]
        bank_s = [pb("bank_s0", [P, 1024]), pb("bank_s1", [P, 1024])]
        bank_t, bank_o = pb("bank_t", [P, 512]), pb("bank_o", [P, 512])
        meta_T = bank_t[0:META, 384:512]
        ident = const[:, C_ID:C_ID + P]

        names = ["const_in", "meta_in", "state_in", "taps_in", "lam_in_sem", "zeroed", "lam_ready", "lam_sums", "lam_exp",
                 "turned", "turned_hi", "turned_lo", "hist_done", "split_hi", "split_lo", "half_done", "hist_ready",
                 "k_cache_in", "v_cache_in", "t_full", "t_free", "o_full", "o_free", 
                 "max_ready0", "max_ready1", "exp_done0", "exp_done1", "scores0", "scores1", "mix_ready", "spread_ready",
                 "q_maps_ready", "kv_stored", "last_stored"]
        s = {n: sem("a_" + n) for n in names}
        x_in = [sem("a_x_in0"), sem("a_x_in1")]
        w_in_sem = [sem("a_w_in0"), sem("a_w_in1")]
        gate_stored = [sem("a_gate_stored0"), sem("a_gate_stored1")]
        evicted = [sem("a_evicted0"), sem("a_evicted1")]
        scores = [s["scores0"], s["scores1"]]
        max_ready = [s["max_ready0"], s["max_ready1"]]
        exp_done = [s["exp_done0"], s["exp_done1"]]
        block = ctx.enter_context(nc.Block())

        fill_t = lambda i, n: 11 * i - 9 + n
        fill_o = lambda i, n: 6 * i - 4 + n
        fill_s = lambda i, n: 5 * (i - 1) + n
        T_SAMPLE, T_PROMPT, T_META, T_ROWS, O_SAMPLE, O_PROMPT, O_ROWS = 3, 4, 8, 9, 2, 3, 4

        def turns(eng, body):
            body(0, True, False, True)
            with eng.Fori(1, HEADS - 1) as i:
                body(i, True, True, True)
            body(HEADS - 1, True, True, False)
            body(HEADS, False, True, False)

        w_view = d["w_in"][0].rearrange("(k p) n -> p k n", p=P)
        keys = lambda b: META + P * (b + 1)

        @block.sync
        def _(sp):
            sp.dma_start(const[:], d["const"]).then_inc(s["const_in"], 16)
            sp.dma_start(meta_rows, d["meta_tokens"]).then_inc(s["meta_in"], 16)
            for b in range(TB):
                wait(sp, s["turned"], 2 * (b - 1))
                src = d["x_prompt"][0, P * b:P * (b + 1), :] if b < QB else d["x_sample"].rearrange("s q d -> (s q) d")
                sp.dma_start(x_rows[b % 2], src).then_inc(x_in[b % 2], 16)
                if b == 0:
                    sp.dma_start(state_rows, d["state_conv"][0].rearrange("s j d -> (s j) d")).then_inc(s["state_in"], 16)
                    sp.dma_start(lam_in[:], d["lambda_qk"].rearrange("l a b -> l (a b)").to_broadcast((P, 256))).then_inc(s["lam_in_sem"], 16)
                    with nc.allow_non_contiguous_dma(reason="three taps of each channel, once"):
                        for k in range(KT):
                            sp.dma_start(taps[:, k, :], d["conv_w"][0, :, P * k:P * (k + 1)].rearrange("w p -> p w")).then_inc(s["taps_in"], 16)

            def body(i, units, attend, more):
                if not units:
                    return
                for u, name in enumerate(UNITS):
                    n = NU * i + u
                    src = w_view[:, :, bass.ds(sp.snap(i * P + COL[name]) if not isinstance(i, int) else i * P + COL[name], P)]
                    wait(sp, s["split_lo"], n - 1)
                    sp.dma_start(w_raw[:, u % 2], src).then_inc(w_in_sem[u % 2], 16)
                    if u == 6:
                        for name, buf, done in (("cache_k", k_cache, "k_cache_in"), ("cache_v", v_cache, "v_cache_in")):
                            srcs = [d[name][0, :, P * t:P * (t + 1), bass.ds(sp.snap(i + 0) if not isinstance(i, int) else i, 1), :]
                                    .rearrange("s p h d -> p s (h d)") for t in range(OWN)]
                            srcs.append(d[name][0, :, OWN * P:CACHED, bass.ds(sp.snap(i + 0) if not isinstance(i, int) else i, 1), :])
                            if isinstance(i, int):
                                sp.wait_ge(s["turned"], 2 * TB + 3)
                            else:
                                sp.wait_ge(s["o_full"], fill_o(i, O_SAMPLE) + 1)
                            for t in range(OWN):
                                sp.dma_start(buf[:, t:OWN * STREAMS:OWN, :], srcs[t]).then_inc(s[done], 16)
                            sp.dma_start(buf[:, 16, :], srcs[OWN]).then_inc(s[done], 16)

            turns(sp, body)

        @block.tensor
        def _(pe):
            pe.wait_ge(s["const_in"], 16)
            for f in range(2 * TB + 2):
                b, half = divmod(f, 2)
                rows, w = (x_rows[b % 2], P) if b < TB else (meta_rows, META)
                if b < TB:
                    pe.wait_ge(x_in[b % 2], 16 * (b // 2 + 1))
                else:
                    pe.wait_ge(s["meta_in"], 16)
                wait(pe, s["turned_lo"], f - 1)
                bank = (bank_t, bank_o)[f % 2][:].rearrange("p (k c) -> p k c", k=4)
                for k in range(4):
                    kk = 4 * half + k
                    last = pe.transpose(bank[:, k, 0:w], rows[:, P * kk:P * (kk + 1)], ident[0:w, 0:w])
                last.then_inc(s["turned"], 1)
            pe.wait_ge(s["state_in"], 16)
            pe.wait_ge(s["turned_lo"], 2 * TB + 1)
            for k in range(KT):
                last = pe.transpose(bank_t[:, 16 * k:16 * k + 16], state_rows[:, P * k:P * (k + 1)], ident[0:16, 0:16])
            last.then_inc(s["turned"], 1)
            pe.wait_ge(s["hist_done"], 1)

            def unit(i, u):
                n = NU * i + u
                pe.wait_ge(s["split_lo"], n + 1)
                for half in range(2):
                    wait(pe, evicted[half], n)
                    out = bank_u[half][:, 0:HALF]
                    cols = slice(HALF * half, HALF * (half + 1))
                    for k in range(KT):
                        pe.matmul(out, w_hi[:, u % 2, k, :], x_hi[:, k, cols], start=(k == 0), stop=False)
                        pe.matmul(out, w_hi[:, u % 2, k, :], x_lo[:, k, cols], start=False, stop=False)
                        last = pe.matmul(out, w_lo[:, u % 2, k, :], x_hi[:, k, cols], start=False, stop=(k == KT - 1))
                    last.then_inc(s["half_done"], 1)

            def turn_cache(i):
                pe.wait_ge(s["k_cache_in"], 48 * i)
                for f in range(5):
                    if f % 2 == 0:
                        bank, full, free, n = bank_t, "t_full", "t_free", fill_t(i, f // 2)
                    else:
                        bank, full, free, n = bank_o, "o_full", "o_free", fill_o(i, f // 2)
                    pe.wait_ge(s[free], n)
                    for k in range(4 * f, min(4 * f + 4, 17)):
                        last = pe.transpose(bank[:, P * (k % 4):P * (k % 4) + P], k_cache[:, k, :], ident)
                    last.then_inc(s[full], 1)

            def sample_scores(i):
                pe.wait_ge(s["q_maps_ready"], i)
                pe.wait_ge(s["t_free"], fill_t(i, 3))
                pe.wait_ge(s["o_free"], fill_o(i, 2))
                for g in range(2):
                    for j in range(4):
                        st = 4 * g + j
                        pe.matmul(bank_s[g][:, 0:2 * P], q_pad[:, P * st:P * (st + 1)], kcT[:, 2 * P * st:2 * P * (st + 1)],
                                  start=(j == 0), stop=(j == 3))
                    q_all = q_maps[:, 4 * g:4 * g + 4, :].rearrange("p s c -> p (s c)")
                    pe.matmul(bank_s[g][:, 2 * P:3 * P], q_all, kcT[:, 16 * P:17 * P], start=True, stop=True)
                    pe.matmul(bank_s[g][:, 3 * P:4 * P], q_all, kT[:, META + SEQ:T], start=True, stop=True).then_inc(scores[g], 1)

            def sample_mix(i):
                pe.wait_ge(s["spread_ready"], i)
                pe.wait_ge(s["t_free"], fill_t(i, T_SAMPLE))
                for t in range(4):
                    for g in range(2):
                        last = pe.matmul(bank_t[:, P * t:P * (t + 1)], prob[:, g, P * t:P * (t + 1)], spread[:, g, :],
                                         start=(g == 0), stop=(g == 1))
                last.then_inc(s["t_full"], 1)

            def sample_values(i):
                pe.wait_ge(s["v_cache_in"], 48 * i)
                pe.wait_ge(s["t_free"], fill_t(i, T_SAMPLE) + 1)
                pe.wait_ge(s["o_free"], fill_o(i, O_SAMPLE))
                out = bank_o[:, 0:P]
                for st in range(STREAMS):
                    for t in range(OWN):
                        pe.matmul(out, v_cache[:, OWN * st + t, :], own_T[:, t, P * st:P * (st + 1)],
                                  start=(st == 0 and t == 0), stop=False)
                pe.matmul(out, v_cache[:, 16, :], shared_T[:, 0, :], start=False, stop=False)
                pe.matmul(out, v_rows[:, 4, :], shared_T[:, 1, :], start=False, stop=True).then_inc(s["o_full"], 1)

            def prompt_scores(i, b):
                for m in range(2):
                    wait(pe, exp_done[m], fill_s(i, 1 + b))
                    r = slice(64 * m, 64 * m + 64)
                    w = keys(b)
                    last = pe.matmul(bank_s[m][:, 0:min(w, 512)], qT[r, P * b:P * (b + 1)], kT[r, 0:min(w, 512)], start=True, stop=True)
                    if w > 512:
                        last = pe.matmul(bank_s[m][:, 512:w], qT[r, P * b:P * (b + 1)], kT[r, 512:w], start=True, stop=True)
                    last.then_inc(scores[m], 1)

            def prompt_turn(i, b):
                pe.wait_ge(s["mix_ready"], 4 * (i - 1) + b + 1)
                pe.wait_ge(s["t_free"], fill_t(i, T_PROMPT + b))
                for t in range(b + 1):
                    last = pe.transpose(bank_t[:, P * t:P * (t + 1)], mix[:, b % 2, META + P * t:META + P * (t + 1)], ident)
                if b == QB - 1:
                    last.then_inc(s["t_full"], 1)
                    pe.wait_ge(s["t_free"], fill_t(i, T_META))
                pe.transpose(meta_T, mix[:, b % 2, 0:META], ident).then_inc(s["t_full"], 1)

            def prompt_values(i):
                pe.wait_ge(s["t_free"], fill_t(i, T_META) + 1)
                pe.wait_ge(s["o_free"], fill_o(i, O_PROMPT))
                pe.matmul(bank_o[:], v_rows[0:META, 5, :], mixT_meta[:], start=True, stop=False)
                for t in range(QB):
                    last = pe.matmul(bank_o[:, P * t:SEQ], v_rows[:, t, :], mixT[:, t, P * t:SEQ], start=False, stop=(t == QB - 1))
                last.then_inc(s["o_full"], 1)

            def turn_rows(i, n):
                for src, u in (((kT, 5), (vT, 6))[n],):
                    for half in range(2):
                        pe.wait_ge(evicted[half], NU * i + u + 1)
                    wait(pe, s["t_free"], fill_t(i, T_ROWS + n))
                    for t in range(QB):
                        last = pe.transpose(bank_t[:, P * t:P * (t + 1)], src[:, META + P * t:META + P * (t + 1)], ident)
                    last.then_inc(s["t_full"], 1)
                    wait(pe, s["o_free"], fill_o(i, O_ROWS + n))
                    pe.transpose(bank_o[:, 0:P], src[:, META + SEQ:T], ident)
                    pe.transpose(bank_o[0:META, P:2 * P], src[:, 0:META], ident).then_inc(s["o_full"], 1)

            def body(i, units, attend, more):
                for u in range(NU):
                    if units:
                        unit(i, u)
                    if attend:
                        if u == 0:
                            turn_cache(i)
                            sample_scores(i)
                        if u == 1:
                            sample_mix(i)
                            prompt_scores(i, 0)
                        if u == 2:
                            sample_values(i)
                        if 2 <= u <= 5:
                            prompt_turn(i, u - 2)
                        if 2 <= u <= 4:
                            prompt_scores(i, u - 1)
                        if u == 6:
                            prompt_values(i)
                    if units and u >= 6:
                        turn_rows(i, u - 6)

            turns(pe, body)
            pe.wait_ge(s["hist_ready"], KT)
            pe.wait_ge(s["t_free"], fill_t(HEADS, T_ROWS))
            for k in range(4):
                last = pe.transpose(bank_t[0:18, P * k:P * (k + 1)], u_last[:, k, :], ident)
            last.then_inc(s["t_full"], 1)
            pe.wait_ge(s["o_free"], fill_o(HEADS, O_ROWS))
            for k in range(4):
                last = pe.transpose(bank_o[0:18, P * k:P * (k + 1)], u_last[:, 4 + k, :], ident)
            last.then_inc(s["o_full"], 1)

        @block.scalar
        def _(act):
            act.wait_ge(s["lam_sums"], 1)
            act.activation(lam[:, 2:4], lam[:, 0:2], ACT.Exp).then_inc(s["lam_exp"], 1)
            for f in range(2 * TB + 2):
                b, half = divmod(f, 2)
                w, at = (P, META + P * b) if b < TB else (META, 0)
                bank = (bank_t, bank_o)[f % 2][:].rearrange("p (k c) -> p k c", k=4)
                act.wait_ge(s["turned"], f + 1)
                act.copy(x_hi[:, 4 * half:4 * half + 4, at:at + w], bank[:, :, 0:w]).then_inc(s["turned_hi"], 1)
            act.wait_ge(s["turned"], 2 * TB + 3)
            act.copy(hist_T[:], bank_t[:, 0:P].rearrange("p (k c) -> p k c", k=KT)).then_inc(s["hist_done"], 1)

            def split(i, u):
                n = NU * i + u
                act.wait_ge(w_in_sem[u % 2], 16 * ((NU // 2) * i + u // 2 + 1))
                wait(act, s["half_done"], 2 * (n - 1))
                act.copy(w_hi[:, u % 2], w_raw[:, u % 2]).then_inc(s["split_hi"], 1)

            def evict(i, u):
                n = NU * i + u
                name = UNITS[u]
                for half in range(2):
                    lo, hi = HALF * half, HALF * (half + 1)
                    skip = META if half == 0 else 0
                    if name in ("gc", "ga") and half == 0:
                        wait(act, gate_stored[name == "ga"], 16 * i)
                    if name == "h" and half == 0:
                        for x in range(2):
                            wait(act, evicted[x], NU * (i - 1) + 2)
                    if name in ("k", "q") and half == 0 and not isinstance(i, int):
                        act.wait_ge(s["scores1"], fill_s(i, 4) + 1)
                    if name == "q" and half == 0:
                        wait(act, s["q_maps_ready"], i)
                    act.wait_ge(s["half_done"], 2 * n + half + 1)
                    src = bank_u[half][:, 0:HALF]
                    if name == "h":
                        ins = act.copy(h_buf[:, lo:hi], src)
                    elif name in ("gc", "ga"):
                        ins = act.copy(gate[:, int(name == "ga"), lo + skip - META:hi - META], src[:, skip:])
                    elif name in ("k", "v"):
                        ins = act.copy((kT if name == "k" else vT)[:, lo:hi], src)
                    elif name == "q":
                        ins = act.copy(qT[:, lo + skip - META:hi - META], src[:, skip:])
                    ins.then_inc(evicted[half], 1)
                if name in ("gc", "ga"):
                    for half in range(2):
                        act.wait_ge(evicted[half], n + 1)
                    act.dma_start(d["gates"][int(name == "ga"), bass.ds(i, 1)].rearrange("a p t -> p (a t)"),
                                  gate[:, int(name == "ga"), :]).then_inc(gate_stored[name == "ga"], 16)

            def take_cache(i):
                for f in range(0, 5, 2):
                    act.wait_ge(s["t_full"], fill_t(i, f // 2) + 1)
                    w = P * min(4, 17 - 4 * f)
                    act.copy(kcT[:, 4 * P * f:4 * P * f + w], bank_t[:, 0:w]).then_inc(s["t_free"], 1)

            def exponent(i, n, w):
                for m in range(2):
                    act.wait_ge(max_ready[m], fill_s(i, n) + 1)
                    if n > 1:
                        act.wait_ge(s["mix_ready"], 4 * (i - 1) + n - 1)
                    act.activation(prob[:, m, 0:w], bank_s[m][:, 0:w], ACT.Exp, bias=neg_max[:, m:m + 1], scale=SCALE,
                                   accum_out=row_sum[:, m:m + 1]).then_inc(exp_done[m], 1)

            def take_turned(i, b):
                act.wait_ge(s["t_full"], fill_t(i, T_PROMPT + b) + 1)
                ins = act.copy(mixT[:, 0:b + 1, P * b:P * (b + 1)], bank_t[:, 0:P * (b + 1)].rearrange("p (t q) -> p t q", q=P))
                if b == QB - 1:
                    ins.then_inc(s["t_free"], 1)
                    act.wait_ge(s["t_full"], fill_t(i, T_META) + 1)
                act.copy(mixT_meta[:, P * b:P * (b + 1)], meta_T).then_inc(s["t_free"], 1)

            def take_output(i, n, first, w):
                act.wait_ge(s["o_full"], fill_o(i, n) + 1)
                act.copy(ya[:, bass.ds(i - 1, 1), first:first + w].rearrange("p a t -> p (a t)"), bank_o[:, 0:w]).then_inc(s["o_free"], 1)

            def take_rows(i, n):
                if n == 0:
                    wait(act, s["kv_stored"], 96 * i)
                for rows in ((k_rows, v_rows)[n],):
                    act.wait_ge(s["t_full"], fill_t(i, T_ROWS + n) + 1)
                    act.copy(rows[:, 0:QB, :], bank_t[:].rearrange("p (t c) -> p t c", c=P)).then_inc(s["t_free"], 1)
                    act.wait_ge(s["o_full"], fill_o(i, O_ROWS + n) + 1)
                    act.copy(rows[:, 4, :], bank_o[:, 0:P])
                    act.copy(rows[0:META, 5, :], bank_o[0:META, P:2 * P]).then_inc(s["o_free"], 1)
                act.wait_ge(s["t_free"], fill_t(i, T_ROWS + n) + 1)
                act.wait_ge(s["o_free"], fill_o(i, O_ROWS + n) + 1)
                for which, rows in ((("k", k_rows), ("v", v_rows))[n],):
                    out = d["new_" + which + "_prompt"][0, 0, :, bass.ds(i, 1), :].rearrange("t a c -> t (a c)")
                    act.dma_start(out[0:META, :], rows[0:META, 5, :]).then_inc(s["kv_stored"], 16)
                    act.dma_start(out[META:META + SEQ, :].rearrange("(b p) c -> p b c", p=P), rows[:, 0:QB, :]).then_inc(s["kv_stored"], 16)
                    out = d["new_" + which + "_sample"][0, :, :, bass.ds(i, 1), :].rearrange("s q a c -> (s q) (a c)")
                    act.dma_start(out, rows[:, 4, :]).then_inc(s["kv_stored"], 16)

            def body(i, units, attend, more):
                for u in range(NU):
                    if units:
                        if u + 1 < NU:
                            split(i, u + 1)
                        elif more:
                            split(i + 1, 0)
                        if UNITS[u] not in ("cg", "bg"):
                            evict(i, u)
                    if attend:
                        if u == 0:
                            take_cache(i)
                            exponent(i, 0, 4 * P)
                        if 1 <= u <= 4:
                            if u == 2:
                                take_output(i, O_SAMPLE, SEQ, P)
                            if u >= 2:
                                take_turned(i, u - 2)
                            exponent(i, u, keys(u - 1))
                        if u == 5:
                            take_turned(i, 3)
                        if u == 6:
                            take_output(i, O_PROMPT, 0, SEQ)
                    if units and u >= 6:
                        take_rows(i, u - 6)

            split(0, 0)
            turns(act, body)
            act.wait_ge(s["t_full"], fill_t(HEADS, T_ROWS) + 1)
            act.copy(last_rows[:, 0:512], bank_t[0:18, :])
            act.wait_ge(s["o_full"], fill_o(HEADS, O_ROWS) + 1)
            act.copy(last_rows[:, 512:1024], bank_o[0:18, :]).then_inc(s["t_free"], 1)
            act.wait_ge(s["t_free"], fill_t(HEADS, T_ROWS) + 1)
            act.dma_start(d["new_conv_prompt"][0, 0], last_rows[0:2, :]).then_inc(s["last_stored"], 16)
            act.dma_start(d["new_conv_sample"][0].rearrange("s j c -> (s j) c"), last_rows[2:18, :]).then_inc(s["last_stored"], 16)
            act.wait_ge(s["last_stored"], 32)
            act.wait_ge(s["kv_stored"], 96 * HEADS)
            for x in range(2):
                act.wait_ge(gate_stored[x], 16 * KT)

        @block.vector
        def _(v):
            v.memset(q_maps[:], 0.0)
            v.memset(q_pad[:], 0.0)
            v.memset(own_T[:], 0.0)
            v.wait_ge(s["lam_in_sem"], 16)
            for x in range(2):
                v.tensor_tensor_reduce(lam_tmp[:], lam_in[:, 128 * x:128 * x + 64], lam_in[:, 128 * x + 64:128 * x + 128],
                                       1.0, 0.0, ALU.mult, ALU.add, lam[:, x:x + 1])
                v.drain()
            v.sem_inc(s["lam_sums"], 1)
            v.wait_ge(s["lam_exp"], 1)
            v.scalar_tensor_tensor(lam[:, 4:5], lam[:, 3:4], -LAM_INIT, lam[:, 2:3], ALU.add, ALU.subtract)
            v.drain()
            v.wait_ge(s["const_in"], 16)
            v.tensor_scalar(lam[:, 6:7], lam[:, 4:5], -1.0, None, ALU.add)
            v.drain()
            v.tensor_scalar(lam[:, 5:6], lam[:, 6:7], const[:, C_SIGN:C_SIGN + 1], 1.0, ALU.mult, ALU.add)
            for f in range(2 * TB + 2):
                b, half = divmod(f, 2)
                w, at = (P, META + P * b) if b < TB else (META, 0)
                bank = (bank_t, bank_o)[f % 2][:].rearrange("p (k c) -> p k c", k=4)
                v.wait_ge(s["turned_hi"], f + 1)
                v.tensor_tensor(x_lo[:, 4 * half:4 * half + 4, at:at + w], bank[:, :, 0:w],
                                x_hi[:, 4 * half:4 * half + 4, at:at + w].bitcast(F32), ALU.subtract).then_inc(s["turned_lo"], 1)
            v.wait_ge(s["taps_in"], 16 * KT)
            v.wait_ge(s["hist_done"], 1)

            def split(i, u):
                n = NU * i + u
                v.wait_ge(s["split_hi"], n + 1)
                v.tensor_tensor(w_lo[:, u % 2], w_raw[:, u % 2], w_hi[:, u % 2].bitcast(F32), ALU.subtract).then_inc(s["split_lo"], 1)

            def evict_cg(i):
                n = NU * i + 1
                for half in range(2):
                    lo, hi = HALF * half, HALF * (half + 1)
                    v.wait_ge(evicted[half], n)
                    v.wait_ge(s["half_done"], 2 * n + half + 1)
                    v.tensor_tensor(u_buf[:, lo:hi], bank_u[half][:, 0:HALF], h_buf[:, lo:hi], ALU.mult).then_inc(evicted[half], 1)
                v.drain()
                v.tensor_copy(u_hist[:, :, 2:NEW + 2], u_buf[:, META + SEQ:T].rearrange("p (s q) -> p s q", q=NEW))
                v.tensor_copy(u_hist[:, :, 0:2], hist_T[:, bass.ds(i, 1), :].rearrange("p a (s j) -> p (a s) j", j=2))
                v.tensor_copy(u_last[:, bass.ds(i, 1), 0:2].rearrange("p a c -> p (a c)"), u_buf[:, META + SEQ - 2:META + SEQ])
                v.drain()
                v.tensor_copy(u_last[:, bass.ds(i, 1), 2:18].rearrange("p a (s j) -> p (a s) j", j=2), u_hist[:, :, NEW:NEW + 2]).then_inc(s["hist_ready"], 1)
                for t in (2, 1, 0):
                    tap = taps[:, bass.ds(i, 1), t:t + 1].rearrange("p a b -> p (a b)")
                    to = conv[:, SEQ:TOK].rearrange("p (s q) -> p s q", q=NEW)
                    prompt, sample = u_buf[:, META - 2 + t:META - 2 + t + SEQ], u_hist[:, :, t:t + NEW]
                    if t == 2:
                        v.tensor_scalar(conv[:, 0:SEQ], prompt, tap, None, ALU.mult)
                        v.tensor_scalar(to, sample, tap, None, ALU.mult)
                    else:
                        v.scalar_tensor_tensor(conv[:, 0:SEQ], prompt, tap, conv[:, 0:SEQ], ALU.mult, ALU.add)
                        v.scalar_tensor_tensor(to, sample, tap, to, ALU.mult, ALU.add)
                    v.drain()

            def evict_bg(i):
                n = NU * i + 2
                for half in range(2):
                    lo, hi = HALF * half, HALF * (half + 1)
                    skip = META if half == 0 else 0
                    v.wait_ge(s["half_done"], 2 * n + half + 1)
                    v.tensor_tensor(yc[:, bass.ds(i, 1), lo + skip - META:hi - META].rearrange("p a t -> p (a t)"),
                                    bank_u[half][:, skip:HALF], conv[:, lo + skip - META:hi - META], ALU.mult).then_inc(evicted[half], 1)

            def take_cache(i):
                for f in (1, 3):
                    v.wait_ge(s["o_full"], fill_o(i, f // 2) + 1)
                    v.tensor_copy(kcT[:, 4 * P * f:4 * P * (f + 1)], bank_o[:]).then_inc(s["o_free"], 1)

            def maximum(i, n, w):
                for m in range(2):
                    v.wait_ge(scores[m], fill_s(i, n) + 1)
                    if n == 0:
                        v.tensor_tensor(bank_s[m][:, 2 * P:4 * P].rearrange("p (x c) -> p x c", x=2),
                                        bank_s[m][:, 2 * P:4 * P].rearrange("p (x c) -> p x c", x=2),
                                        const[:, C_MASK + P * m:C_MASK + P * (m + 1)].rearrange("p (x c) -> p x c", x=1).to_broadcast((P, 2, P)), ALU.add)
                    else:
                        v.memset(bank_s[m][0:CHUNK, w - CHUNK:w], MASKED)
                    v.drain()
                    v.tensor_reduce(neg_max[:, m:m + 1], bank_s[m][:, 0:w], AX.X, ALU.max)
                    v.drain()
                    v.tensor_scalar(neg_max[:, m:m + 1], neg_max[:, m:m + 1], -SCALE, None, ALU.mult).then_inc(max_ready[m], 1)

            def spread_rows(i):
                for g in range(2):
                    v.wait_ge(exp_done[g], fill_s(i, 0) + 1)
                    v.reciprocal(inv[:, g:g + 1], row_sum[:, g:g + 1])
                    v.drain()
                    v.tensor_scalar(spread[:, g, :], const[:, C_SPREAD + P * g:C_SPREAD + P * (g + 1)], inv[:, g:g + 1], lam[:, 5:6],
                                    ALU.mult, ALU.mult)
                v.drain()
                v.sem_inc(s["spread_ready"], 1)

            def take_sample_mix(i):
                v.wait_ge(s["t_full"], fill_t(i, T_SAMPLE) + 1)
                for t in range(OWN):
                    to = own_T[:, t, :].rearrange("p (s c) -> p s c", c=P + NEW)[:, 0:STREAMS, 0:NEW]
                    v.tensor_copy(to, bank_t[:, P * t:P * (t + 1)].rearrange("p (s q) -> p s q", q=NEW))
                v.tensor_copy(shared_T[:], bank_t[:, 2 * P:4 * P].rearrange("p (t c) -> p t c", c=P)).then_inc(s["t_free"], 1)

            def combine_maps(i, b):
                w = keys(b)
                v.wait_ge(exp_done[0], fill_s(i, 1 + b) + 1)
                v.wait_ge(exp_done[1], fill_s(i, 1 + b) + 1)
                v.reciprocal(inv[:, 0:2], row_sum[:])
                v.drain()
                v.tensor_scalar(mix[:, b % 2, 0:w], prob[:, 0, 0:w], inv[:, 0:1], None, ALU.mult)
                v.tensor_scalar(inv[:, 2:3], inv[:, 1:2], lam[:, 4:5], None, ALU.mult)
                v.drain()
                v.scalar_tensor_tensor(mix[:, b % 2, 0:w], prob[:, 1, 0:w], inv[:, 2:3], mix[:, b % 2, 0:w], ALU.mult, ALU.add).then_inc(s["mix_ready"], 1)

            def lay_out_q(i):
                for half in range(2):
                    v.wait_ge(evicted[half], NU * i + 8)
                for m in range(2):
                    r = slice(64 * m, 64 * m + 64)
                    q = qT[r, SEQ:TOK].rearrange("p (s q) -> p s q", q=NEW)
                    v.tensor_copy(q_maps[r, :, NEW * m:NEW * (m + 1)], q)
                    for g in range(2):
                        to = q_pad[r, 4 * P * g:4 * P * g + 640].rearrange("p (s c) -> p s c", c=P + 32)
                        last = v.tensor_copy(to[:, :, NEW * m:NEW * (m + 1)], q[:, 4 * g:4 * g + 4, :])
                last.then_inc(s["q_maps_ready"], 1)

            def body(i, units, attend, more):
                for u in range(NU):
                    if units:
                        if u + 1 < NU:
                            split(i, u + 1)
                        elif more:
                            split(i + 1, 0)
                        if UNITS[u] == "cg":
                            evict_cg(i)
                        if UNITS[u] == "bg":
                            evict_bg(i)
                    if attend:
                        if u == 0:
                            take_cache(i)
                            maximum(i, 0, 4 * P)
                            spread_rows(i)
                        if u == 1:
                            take_sample_mix(i)
                        if 1 <= u <= 4:
                            maximum(i, u, keys(u - 1))
                            combine_maps(i, u - 1)
                if units:
                    lay_out_q(i)

            split(0, 0)
            turns(v, body)


def merge_branches(nc, d, keep):
    with ExitStack() as ctx:
        sb = lambda name, shape, dt=F32: ctx.enter_context(nc.sbuf_tensor(name, shape, dt))
        pb = lambda name: ctx.enter_context(nc.psum_tensor(name, [P, 512], F32))
        sem = lambda name: ctx.enter_context(nc.semaphore("m_" + name))
        yc, ya = keep["yc"], keep["ya"]
        H = TOK // 2
        w_raw = sb("mw_raw", [P, 2, KT, P])
        w_hi, w_lo = sb("mw_hi", [P, 2, KT, P], F32R), sb("mw_lo", [P, 2, KT, P], F32R)
        y_hi = [sb("yc_hi", [P, KT, TOK], F32R), sb("ya_hi", [P, KT, TOK], F32R)]
        y_lo = [sb("yc_lo", [P, KT, TOK], F32R), sb("ya_lo", [P, KT, TOK], F32R)]
        merged = sb("merged", [P, KT, TOK])
        gate_a = yc
        square, root, normed, gated = (sb(n, [P, TOK]) for n in ("square", "root", "normed", "gated"))
        ones, gain, eps = sb("ones", [P, P]), sb("gain", [P, 2]), sb("eps", [P, 1])
        bank_u = [pb("mbank_u0"), pb("mbank_u1")]
        bank_r = [pb("bank_r0"), pb("bank_r1")]
        w_loaded = [sem("w_loaded0"), sem("w_loaded1")]
        evicted = [sem("evicted0"), sem("evicted1")]
        gc_in, ga_in, gain_in, yc_hi_done, yc_lo_done, gate_ready = (sem(n) for n in ("gc_in", "ga_in", "gain_in", "yc_hi_done", "yc_lo_done", "gate_ready"))
        split_hi, split_lo, half_done, consts_done = (sem(n) for n in ("split_hi", "split_lo", "half_done", "consts_done"))
        squared, summed, rooted, norm_done, ya_hi_done, ya_lo_done, gated_sem = (sem(n) for n in ("squared", "summed", "rooted", "norm_done", "ya_hi_done", "ya_lo_done", "gated_sem"))
        block = ctx.enter_context(nc.Block())

        @block.sync
        def _(sp):
            sp.dma_start(merged[:], d["gates"][0].rearrange("k p t -> p k t")).then_inc(gc_in, 16)
            with nc.allow_non_contiguous_dma(reason="one value a partition"):
                sp.dma_start(gain[:, 0:1], d["subln_g"].rearrange("l p -> p l")).then_inc(gain_in, 16)

            def body(i, u, br):
                n = 2 * i + u
                view = d["w_branch"][0, br].rearrange("(k p) n -> p k n", p=P)
                col = (i - 4 * br) * 2 * P + u * P
                src = view[:, :, bass.ds(col if isinstance(i, int) else sp.snap(col), P)]
                wait(sp, split_lo, n - 1)
                sp.dma_start(w_raw[:, u], src).then_inc(w_loaded[u], 16)

            for u in range(2):
                body(0, u, 0)
            sp.wait_ge(yc_lo_done, KT)
            sp.dma_start(gate_a[:], d["gates"][1].rearrange("k p t -> p k t")).then_inc(ga_in, 16)
            with sp.Fori(1, 4) as i:
                for u in range(2):
                    body(i, u, 0)
            with sp.Fori(4, 8) as i:
                for u in range(2):
                    body(i, u, 1)

        def turns(eng, body):
            for u in range(2):
                body(0, u, 0)
            with eng.Fori(1, 4) as i:
                for u in range(2):
                    body(i, u, 0)
            with eng.Fori(4, 8) as i:
                for u in range(2):
                    body(i, u, 1)

        @block.tensor
        def _(pe):
            pe.wait_ge(consts_done, 1)

            def body(i, u, br):
                n = 2 * i + u
                if br == 0 and isinstance(i, int) and u == 0:
                    pe.wait_ge(yc_lo_done, KT)
                if br == 1 and u == 0:
                    pe.wait_ge(ya_lo_done, KT)
                pe.wait_ge(split_lo, n + 1)
                for half in range(2):
                    wait(pe, evicted[half], n)
                    out, cols = bank_u[half][:, 0:H], slice(H * half, H * (half + 1))
                    for k in range(KT):
                        pe.matmul(out, w_hi[:, u, k, :], y_hi[br][:, k, cols], start=(k == 0), stop=False)
                        pe.matmul(out, w_hi[:, u, k, :], y_lo[br][:, k, cols], start=False, stop=False)
                        last = pe.matmul(out, w_lo[:, u, k, :], y_hi[br][:, k, cols], start=False, stop=(k == KT - 1))
                    last.then_inc(half_done, 1)
                if br == 0:
                    pe.wait_ge(squared, n + 1)
                    wait(pe, rooted, n)
                    for half in range(2):
                        last = pe.matmul(bank_r[half][:, 0:H], ones[:], square[:, H * half:H * (half + 1)], start=True, stop=True)
                    last.then_inc(summed, 1)

            turns(pe, body)

        @block.scalar
        def _(act):
            for k in range(KT):
                act.copy(y_hi[0][:, k], yc[:, k]).then_inc(yc_hi_done, 1)

            def body(i, u, br):
                n = 2 * i + u
                act.wait_ge(w_loaded[u], 16 * (i + 1))
                wait(act, half_done, 2 * (n - 1))
                act.copy(w_hi[:, u], w_raw[:, u]).then_inc(split_hi, 1)
                if br == 0:
                    if isinstance(i, int) and u == 0:
                        act.wait_ge(gc_in, 16)
                        act.activation(merged[:], merged[:], ACT.Sigmoid).then_inc(gate_ready, 1)
                    wait(act, summed, n)
                    act.activation(square[:], ya[:, bass.ds(n, 1), :].rearrange("p a t -> p (a t)"), ACT.Square).then_inc(squared, 1)
                    act.wait_ge(summed, n + 1)
                    wait(act, norm_done, n)
                    act.activation(root[:, 0:H], bank_r[0][:, 0:H], ACT.Sqrt, bias=eps[:, 0:1], scale=1.0 / P)
                    act.activation(root[:, H:TOK], bank_r[1][:, 0:H], ACT.Sqrt, bias=eps[:, 0:1], scale=1.0 / P).then_inc(rooted, 1)
                    act.wait_ge(norm_done, n + 1)
                    act.copy(y_hi[1][:, bass.ds(n, 1), :].rearrange("p a t -> p (a t)"), normed[:]).then_inc(ya_hi_done, 1)

            act.wait_ge(consts_done, 1)
            for u in range(2):
                body(0, u, 0)
            with act.Fori(1, 4) as i:
                for u in range(2):
                    body(i, u, 0)
            act.wait_ge(ga_in, 16)
            act.activation(gate_a[:], gate_a[:], ACT.Sigmoid).then_inc(gate_ready, 1)
            with act.Fori(4, 8) as i:
                for u in range(2):
                    body(i, u, 1)

        @block.vector
        def _(v):
            v.memset(ones[:], 1.0)
            v.memset(eps[:], EPS).then_inc(consts_done, 1)
            v.wait_ge(gain_in, 16)
            v.tensor_scalar(gain[:, 1:2], gain[:, 0:1], 1.0 - LAM_INIT, None, ALU.mult)
            for k in range(KT):
                v.wait_ge(yc_hi_done, k + 1)
                v.tensor_tensor(y_lo[0][:, k], yc[:, k], y_hi[0][:, k].bitcast(F32), ALU.subtract).then_inc(yc_lo_done, 1)

            def body(i, u, br):
                n = 2 * i + u
                v.wait_ge(split_hi, n + 1)
                v.tensor_tensor(w_lo[:, u], w_raw[:, u], w_hi[:, u].bitcast(F32), ALU.subtract).then_inc(split_lo, 1)
                one = lambda t, x: t[:, bass.ds(x, 1), :].rearrange("p a t -> p (a t)")
                if br == 0:
                    v.wait_ge(rooted, n + 1)
                    wait(v, ya_hi_done, n)
                    v.tensor_scalar(normed[:], one(ya, n), gain[:, 1:2], None, ALU.mult)
                    v.reciprocal(root[:], root[:])
                    v.drain()
                    v.tensor_tensor(normed[:], normed[:], root[:], ALU.mult).then_inc(norm_done, 1)
                    v.wait_ge(ya_hi_done, n + 1)
                    v.tensor_tensor(one(y_lo[1], n), normed[:], one(y_hi[1], n).bitcast(F32), ALU.subtract).then_inc(ya_lo_done, 1)
                v.wait_ge(gate_ready, 1 + br)
                for half in range(2):
                    cols = slice(H * half, H * (half + 1))
                    pick = lambda t, x: t[:, bass.ds(x, 1), cols].rearrange("p a t -> p (a t)")
                    v.wait_ge(half_done, 2 * n + half + 1)
                    if br == 0:
                        v.tensor_tensor(pick(merged, n), bank_u[half][:, 0:H], pick(merged, n), ALU.mult).then_inc(evicted[half], 1)
                    else:
                        m = n - KT
                        v.tensor_tensor(gated[:, cols], bank_u[half][:, 0:H], pick(gate_a, m), ALU.mult).then_inc(evicted[half], 1)
                        v.drain()
                        v.tensor_tensor(pick(ya, m), gated[:, cols], pick(merged, m), ALU.add)

            turns(v, body)


def layer_norm_steps(v, pre, stats, mv, act_root, root_done, n):
    for half in range(2):
        v.bn_stats(stats[:, 6 * half:6 * half + 6], pre[:, 512 * half:512 * (half + 1)])
    v.drain()
    v.bn_aggr(mv, stats[:, 0:12]).then_inc(act_root, 1)
    v.wait_ge(root_done, n)


def route(nc, d, keep):
    with ExitStack() as ctx:
        sb = lambda name, shape, dt=F32: ctx.enter_context(nc.sbuf_tensor(name, shape, dt))
        pb = lambda name: ctx.enter_context(nc.psum_tensor(name, [P, 512], F32))
        sem = lambda name: ctx.enter_context(nc.semaphore("r_" + name))
        merged, const, h = keep["ya"], keep["const"], keep["h"]
        slots, weights, eid = keep["slots"], keep["weights"], keep["eid"]
        ident = const[:, C_ID:C_ID + P]
        w_raw = sb("wo_raw", [P, 2, D])
        w_hi, w_lo = sb("wo_hi", [P, KT, D], F32R), sb("wo_lo", [P, KT, D], F32R)
        m_hi, m_lo = sb("m_hi", [P, KT, TOK], F32R), sb("m_lo", [P, KT, TOK], F32R)
        x_rows, pre = sb("rx_rows", [P, 2, D]), sb("pre", [P, 2, D])
        hT = sb("hT", [P, KT, P])
        ln_g, ln_b = sb("ln1_g_sb", [P, D]), sb("ln1_b_sb", [P, D])
        w_router, b_router = sb("w_router_sb", [P, KT, 36]), sb("b_router_sb", [P, 36])
        stats, mv, root, eps = sb("stats", [P, 12]), sb("mv", [P, 2]), sb("root1", [P, 2]), sb("eps1", [P, 1])
        logits = sb("logits", [P, TB, 36])
        group8, top8, idx8 = sb("group8", [P, TB, 8]), sb("top8", [P, TB, 8]), sb("idx8", [P, TB, 8], U32)
        pick_f = sb("pick_f", [P, 4, TB])
        masked, offm = sb("masked", [P, TB, EXPERTS]), sb("offm", [P, TB, EXPERTS])
        first, second, both = (sb(n, [P, TB, EXPERTS]) for n in ("first", "second", "both"))
        shifted, expd = sb("shifted", [P, TB, 8]), sb("expd", [P, TB, 8])
        soft = sb("soft", [P, 6, TB])
        ones, zeros = sb("ones1", [P, P]), sb("zeros1", [P, EXPERTS])
        per_expert = sb("per_expert", [P, 6, EXPERTS])
        compare = sb("compare", [1, SPARE, EXPERTS])
        eid_f = sb("eid_f", [1, SPARE + 1])
        choices = sb("choices", [P, 2 * TB], U32)
        over = sb("over", [P, TB, EXPERTS])
        empty = sb("empty", [BLOCKS, P], U32)
        slot_f = sb("slot_f", [P, 2, TB])

        bank = [[pb(f"rbank{a}{b}") for b in range(2)] for a in range(2)]
        bank_h = [pb("bank_h0"), pb("bank_h1")]
        bank_l, bank_c = pb("bank_l"), pb("bank_c")
        w_loaded, x_loaded, h_stored = ([sem(f"{n}{x}") for x in range(2)] for n in ("w_loaded", "x_loaded", "h_stored"))
        small_in, split_hi, split_lo, m_hi_done, m_lo_done, out_done, taken = (sem(n) for n in ("small_in", "split_hi", "split_lo", "m_hi_done", "m_lo_done", "out_done", "taken"))
        var_ready, root_done, h_ready, h_turned, h_taken, logits_done = (sem(n) for n in ("var_ready", "root_done", "h_ready", "h_turned", "h_taken", "logits_done"))
        shifted_ready, exp_ready, both_ready, counted, slots_ready, empty_ready, table_sem, consts_done = (sem(n) for n in ("shifted_ready", "exp_ready", "both_ready", "counted", "slots_ready", "empty_ready", "table_sem", "consts_done"))
        block = ctx.enter_context(nc.Block())
        SMALL = 16 * 6

        @block.sync
        def _(sp):
            for k in range(KT):
                wait(sp, split_lo, k - 1)
                sp.dma_start(w_raw[:, k % 2], d["w_out"][0, P * k:P * (k + 1), :]).then_inc(w_loaded[k % 2], 16)
                if k < 2:
                    sp.dma_start(x_rows[:, k], d["x_prompt"][0, P * k:P * (k + 1), :]).then_inc(x_loaded[k], 16)
                if k == 1:
                    sp.dma_start(ln_g[:], d["ln1_g"].to_broadcast((P, D))).then_inc(small_in, 16)
                    sp.dma_start(ln_b[:], d["ln1_b"].to_broadcast((P, D))).then_inc(small_in, 16)
                    sp.dma_start(b_router[:, 0:4], d["b_group"].to_broadcast((P, 4))).then_inc(small_in, 16)
                    sp.dma_start(b_router[:, 4:36], d["b_router"].to_broadcast((P, 32))).then_inc(small_in, 16)
                    sp.dma_start(w_router[:, :, 0:4], d["w_group"][0].rearrange("(k p) n -> p k n", p=P)).then_inc(small_in, 16)
                    sp.dma_start(w_router[:, :, 4:36], d["w_router"][0].rearrange("(k p) n -> p k n", p=P)).then_inc(small_in, 16)
            for b in range(2, TB):
                src = d["x_prompt"][0, P * b:P * (b + 1), :] if b < QB else d["x_sample"].rearrange("s q d -> (s q) d")
                sp.wait_ge(taken, b - 1)
                sp.dma_start(x_rows[:, b % 2], src).then_inc(x_loaded[b % 2], 16)
            for b in range(TB):
                sp.wait_ge(h_ready, b + 1)
                sp.dma_start(d["h_rows"][P * b:P * (b + 1), :], h[:, b, :]).then_inc(h_stored[b % 2], 16)
            sp.wait_ge(h_stored[0], 48)
            sp.wait_ge(h_stored[1], 32)

        @block.tensor
        def _(pe):
            def out_rows(b):
                wait(pe, taken, b - 1)
                pe.wait_ge(m_lo_done, KT)
                for k in range(KT):
                    pe.wait_ge(split_lo, k + 1)
                    rows = slice(P * b, P * (b + 1))
                    for strip in range(2):
                        out, cols = bank[b % 2][strip][:], slice(512 * strip, 512 * (strip + 1))
                        pe.matmul(out, m_hi[:, k, rows], w_hi[:, k, cols], start=(k == 0), stop=False)
                        pe.matmul(out, m_hi[:, k, rows], w_lo[:, k, cols], start=False, stop=False)
                        last = pe.matmul(out, m_lo[:, k, rows], w_hi[:, k, cols], start=False, stop=(k == KT - 1))
                last.then_inc(out_done, 1)

            def router(b):
                pe.wait_ge(h_ready, b + 1)
                wait(pe, h_taken, 2 * b)
                for k in range(KT):
                    last = pe.transpose(bank_h[k // 4][:, P * (k % 4):P * (k % 4 + 1)], h[:, b, P * k:P * (k + 1)], ident)
                    if k % 4 == 3:
                        last.then_inc(h_turned, 1)
                pe.wait_ge(h_taken, 2 * b + 2)
                if b == 0:
                    pe.wait_ge(small_in, SMALL)
                for k in range(KT):
                    last = pe.matmul(bank_l[:, 64 * b:64 * b + 36], hT[:, k, :], w_router[:, k, :], start=(k == 0), stop=(k == KT - 1))
                last.then_inc(logits_done, 1)

            for b in range(TB + 1):
                if b < TB:
                    out_rows(b)
                if b > 0:
                    router(b - 1)
            pe.wait_ge(both_ready, 1)
            pe.wait_ge(consts_done, 1)
            for b in range(TB):
                out = bank_c[:, EXPERTS * b:EXPERTS * (b + 1)]
                for a in range(b):
                    pe.matmul(out, ones[:], both[:, a, :], start=(a == 0), stop=False)
                pe.matmul(out, const[:, C_UPPER:C_UPPER + P], both[:, b, :], start=(b == 0), stop=True)
            for b in range(TB):
                last = pe.matmul(bank_c[:, EXPERTS * TB:EXPERTS * (TB + 1)], ones[:], both[:, b, :], start=(b == 0), stop=(b == TB - 1))
            last.then_inc(counted, 1)

        @block.scalar
        def _(act):
            for k in range(KT):
                act.copy(m_hi[:, k], merged[:, k]).then_inc(m_hi_done, 1)
                act.wait_ge(w_loaded[k % 2], 16 * (k // 2 + 1))
                act.copy(w_hi[:, k], w_raw[:, k % 2]).then_inc(split_hi, 1)
            act.wait_ge(consts_done, 1)
            for b in range(TB):
                act.wait_ge(var_ready, b + 1)
                act.activation(root[:, 0:1], mv[:, 1:2], ACT.Sqrt, bias=eps[:, 0:1], scale=1.0).then_inc(root_done, 1)
                for half in range(2):
                    act.wait_ge(h_turned, 2 * b + half + 1)
                    wait(act, logits_done, b)
                    act.copy(hT[:, 4 * half:4 * half + 4, :], bank_h[half][:].rearrange("p (k c) -> p k c", k=4)).then_inc(h_taken, 1)
            act.wait_ge(shifted_ready, 1)
            act.activation(expd[:], shifted[:], ACT.Exp).then_inc(exp_ready, 1)

        @block.gpsimd
        def _(g):
            g.wait_ge(empty_ready, 1)
            g.dma_start(d["slot_choice"].rearrange("(b p) a -> b (p a)", p=P), empty[:]).then_inc(table_sem, 16)
            g.wait_ge(table_sem, 16)
            g.wait_ge(slots_ready, 1)
            for n in range(2):
                for b in range(TB):
                    g.indirect_dma_start(out=d["slot_choice"], out_offset=bass.IndirectOffsetOnAxis(ap=slots[:, n, b:b + 1], axis=0),
                                         in_=choices[:, TB * n + b:TB * n + b + 1], in_offset=None).then_inc(table_sem, 16)
            g.wait_ge(table_sem, 16 * (1 + 2 * TB))

        @block.vector
        def _(v):
            v.memset(ones[:], 1.0)
            v.memset(zeros[:], 0.0)
            v.memset(eps[:], EPS).then_inc(consts_done, 1)
            v.tensor_copy(choices[:], const[:, C_TOKEN:C_TOKEN + 2 * TB])
            v.tensor_scalar(empty[:], const[0:BLOCKS, 0:P], 0.0, float(NONE), ALU.mult, ALU.add).then_inc(empty_ready, 1)
            v.memset(group8[:], MASKED)
            for k in range(KT):
                v.wait_ge(m_hi_done, k + 1)
                v.tensor_tensor(m_lo[:, k], merged[:, k], m_hi[:, k].bitcast(F32), ALU.subtract).then_inc(m_lo_done, 1)
                v.wait_ge(split_hi, k + 1)
                v.tensor_tensor(w_lo[:, k], w_raw[:, k % 2], w_hi[:, k].bitcast(F32), ALU.subtract).then_inc(split_lo, 1)
            v.wait_ge(small_in, SMALL)
            for b in range(TB):
                v.wait_ge(out_done, b + 1)
                v.wait_ge(x_loaded[b % 2], 16 * (b // 2 + 1))
                p = pre[:, b % 2, :]
                for strip in range(2):
                    cols = slice(512 * strip, 512 * (strip + 1))
                    last = v.scalar_tensor_tensor(p[:, cols], x_rows[:, b % 2, cols], ALPHA, bank[b % 2][strip][:], ALU.mult, ALU.add)
                last.then_inc(taken, 1)
                v.drain()
                layer_norm_steps(v, p, stats, mv[:], var_ready, root_done, b + 1)
                v.reciprocal(root[:, 1:2], root[:, 0:1])
                v.drain()
                v.tensor_scalar(p, p, mv[:, 0:1], root[:, 1:2], ALU.subtract, ALU.mult)
                v.drain()
                v.tensor_tensor(p, p, ln_g[:], ALU.mult)
                v.drain()
                v.tensor_tensor(h[:, b, :], p, ln_b[:], ALU.add).then_inc(h_ready, 1)

            v.wait_ge(logits_done, TB)
            v.tensor_tensor(logits[:], bank_l[:, 0:64 * TB].rearrange("p (b c) -> p b c", b=TB)[:, :, 0:36],
                            b_router[:].rearrange("p (a c) -> p a c", a=1).to_broadcast((P, TB, 36)), ALU.add)
            v.drain()
            v.tensor_copy(group8[:, :, 0:GROUPS], logits[:, :, 0:GROUPS])
            v.drain()
            for b in range(TB):
                v.max(top8[:, b, :], group8[:, b, :])
            v.drain()
            for b in range(TB):
                v.max_index(idx8[:, b, :], top8[:, b, :], group8[:, b, :])
            v.drain()
            v.tensor_copy(pick_f[:, 0, :], idx8[:, :, 0])
            v.tensor_tensor(shifted[:, :, 0:GROUPS], logits[:, :, 0:GROUPS], top8[:, :, 0:1].to_broadcast((P, TB, GROUPS)), ALU.subtract)
            v.drain()
            for b in range(TB):
                v.tensor_scalar(masked[:, b, :], const[:, C_GROUP:C_GROUP + EXPERTS], pick_f[:, 0, b:b + 1], None, ALU.is_equal)
            v.drain()
            v.tensor_scalar(offm[:], masked[:], -MASKED, MASKED, ALU.mult, ALU.add)
            v.tensor_tensor(masked[:], masked[:], logits[:, :, GROUPS:GROUPS + EXPERTS], ALU.mult)
            v.drain()
            v.tensor_tensor(masked[:], masked[:], offm[:], ALU.add)
            v.drain()
            for b in range(TB):
                v.max(top8[:, b, :], masked[:, b, :])
            v.drain()
            for b in range(TB):
                v.max_index(idx8[:, b, :], top8[:, b, :], masked[:, b, :])
            v.drain()
            v.tensor_copy(pick_f[:, 1, :], idx8[:, :, 0])
            v.tensor_copy(pick_f[:, 2, :], idx8[:, :, 1])
            v.memset(shifted[:, :, 5:8], 0.0)
            v.tensor_tensor(shifted[:, :, 4:5], top8[:, :, 1:2], top8[:, :, 0:1], ALU.subtract).then_inc(shifted_ready, 1)
            v.drain()
            for n, hot in enumerate((first, second)):
                for b in range(TB):
                    v.tensor_scalar(hot[:, b, :], const[:, C_EXPERT:C_EXPERT + EXPERTS], pick_f[:, 1 + n, b:b + 1], None, ALU.is_equal)
            v.drain()
            v.tensor_tensor(both[:], first[:], second[:], ALU.add).then_inc(both_ready, 1)
            v.wait_ge(exp_ready, 1)
            v.tensor_reduce(soft[:, 0, :], expd[:, :, 0:GROUPS], AX.X, ALU.add)
            v.tensor_scalar(soft[:, 1, :], expd[:, :, 4], 1.0, None, ALU.add)
            v.drain()
            v.tensor_tensor(soft[:, 2, :], soft[:, 0, :], soft[:, 1, :], ALU.mult)
            v.drain()
            v.reciprocal(weights[:, 0, :], soft[:, 2, :])
            v.drain()
            v.tensor_tensor(weights[:, 1, :], weights[:, 0, :], expd[:, :, 4], ALU.mult)
            v.wait_ge(counted, 1)
            counts, n_blocks, tmp, ends, starts = (per_expert[:, x, :] for x in range(5))
            v.tensor_copy(counts, bank_c[:, EXPERTS * TB:EXPERTS * (TB + 1)])
            v.tensor_scalar(n_blocks, bank_c[:, EXPERTS * TB:EXPERTS * (TB + 1)], float(P), None, ALU.is_gt)
            v.tensor_copy(over[:], bank_c[:, 0:EXPERTS * TB].rearrange("p (b e) -> p b e", b=TB))
            v.drain()
            for x in range(2, TB):
                v.scalar_tensor_tensor(n_blocks, counts, float(P * x), n_blocks, ALU.is_gt, ALU.add)
                v.drain()
            v.tensor_tensor_scan(ends, n_blocks, zeros[:], 0.0, ALU.add, ALU.add)
            v.drain()
            v.tensor_tensor(starts, ends, n_blocks, ALU.subtract)
            v.drain()
            v.scalar_tensor_tensor(tmp, starts, float(EXPERTS - 1), const[:, C_EXPERT:C_EXPERT + EXPERTS], ALU.add, ALU.subtract)
            v.tensor_scalar(offm[:], over[:], float(P), float(P), ALU.is_ge, ALU.mult)
            v.drain()
            v.tensor_tensor(offm[:], offm[:], per_expert[:, 2:3, :].to_broadcast((P, TB, EXPERTS)), ALU.mult)
            v.tensor_tensor(over[:], over[:], const[:, C_FIRST:C_FIRST + EXPERTS].rearrange("p (a e) -> p a e", a=1).to_broadcast((P, TB, EXPERTS)), ALU.add)
            v.drain()
            v.tensor_tensor(offm[:], offm[:], over[:], ALU.add)
            v.drain()
            for n, hot in enumerate((first, second)):
                v.tensor_tensor(masked[:], hot[:], offm[:], ALU.mult)
                v.drain()
                v.tensor_reduce(slot_f[:, n, :], masked[:], AX.X, ALU.add)
                v.drain()
            v.tensor_copy(slots[:], slot_f[:]).then_inc(slots_ready, 1)
            v.tensor_tensor(compare[:], per_expert[0:1, 3:4, :].to_broadcast((1, SPARE, EXPERTS)),
                            const[0:1, C_BLOCK:C_BLOCK + SPARE].rearrange("p (j a) -> p j a", a=1).to_broadcast((1, SPARE, EXPERTS)), ALU.is_le)
            v.drain()
            v.tensor_reduce(eid_f[:, 0:SPARE], compare[:], AX.X, ALU.add)
            v.drain()
            v.tensor_scalar(eid_f[:, 0:SPARE], eid_f[:, 0:SPARE], float(EXPERTS - 1), None, ALU.min)
            v.tensor_copy(eid_f[:, SPARE:SPARE + 1], per_expert[0:1, 3, EXPERTS - 1:EXPERTS])
            v.drain()
            v.tensor_copy(eid[:], eid_f[:])


def run_experts(nc, d, keep):
    with ExitStack() as ctx:
        sb = lambda name, shape, dt=F32: ctx.enter_context(nc.sbuf_tensor(name, shape, dt))
        pb = lambda name: ctx.enter_context(nc.psum_tensor(name, [P, 512], F32))
        sem = lambda name: ctx.enter_context(nc.semaphore("e_" + name))
        const, eid = keep["const"], keep["eid"]
        ident = const[:, C_ID:C_ID + P]
        up_raw, down_raw = sb("up_raw", [P, 2, KT, 512]), sb("down_raw", [P, 2, 2, D])
        up_hi, up_lo = sb("up_hi", [P, KT, 512], F32R), sb("up_lo", [P, KT, 512], F32R)
        down_hi, down_lo = sb("down_hi", [P, 2, 2, D], F32R), sb("down_lo", [P, 2, 2, D], F32R)
        rows = sb("rows", [P, 2, D])
        xT_hi, xT_lo = sb("xT_hi", [P, 2, KT, P], F32R), sb("xT_lo", [P, 2, KT, P], F32R)
        silu, act_rows = sb("silu", [P, DE]), sb("act_rows", [P, DE])
        aT_hi, aT_lo = sb("aT_hi", [P, 2, P], F32R), sb("aT_lo", [P, 2, P], F32R)
        y_rows = sb("y_rows", [P, 2, D])
        choice = sb("choice", [P, BLOCKS], U32)
        choice_f, above = sb("choice_f", [P, BLOCKS]), sb("above", [P, BLOCKS])
        token = sb("token", [P, BLOCKS], U32)
        bank_g = [pb("bank_g0"), pb("bank_g1")]
        bank_x = [pb("bank_x0"), pb("bank_x1")]
        bank_a = pb("bank_a")
        bank_d = [pb("bank_d0"), pb("bank_d1")]
        two = lambda n: [sem(n + "0"), sem(n + "1")]
        up_in, down_in, rows_in, y_stored = two("up_in"), two("down_in"), two("rows_in"), two("y_stored")
        (choice_in, token_ready, up_hi_done, up_lo_done, up_used, down_hi_done, down_lo_done, down_used, x_turned, x_hi_done, x_lo_done,
         silu_done, act_done, a_turned, a_hi_done, a_lo_done, y_left, y_right) = (sem(n) for n in (
             "choice_in", "token_ready", "up_hi_done", "up_lo_done", "up_used", "down_hi_done", "down_lo_done", "down_used", "x_turned",
             "x_hi_done", "x_lo_done", "silu_done", "act_done", "a_turned", "a_hi_done", "a_lo_done", "y_left", "y_right"))
        block = ctx.enter_context(nc.Block())

        def run(eng, body, j0, j1):
            j = j0
            while j < j1 and (j < 3 or j == j0):
                body(j, j // 2, j % 2, j == j0, j == j1 - 1)
                j += 1
            pairs = (j1 - 1 - j) // 2
            with eng.Fori(j // 2, j // 2 + pairs) as i:
                body(2 * i + 1, i, 1, False, False)
                body(2 * i + 2, i + 1, 0, False, False)
            for j in range(j + 2 * pairs, j1):
                body(j, j // 2, j % 2, False, j == j1 - 1)

        def all_blocks(eng, stretch):
            stretch(0, EXPERTS)
            spare = eng.value_load(eid[0:1, SPARE:SPARE + 1], min_val=0, max_val=SPARE)
            with eng.If(spare > 0):
                stretch(EXPERTS, BLOCKS)

        @block.sync
        def _(sp):
            def body(j, n, par, first, last):
                if not isinstance(j, int) and keep["spare"]:
                    e = sp.value_load(eid[0:1, bass.ds(j - EXPERTS, 1)], min_val=0, max_val=EXPERTS - 1)
                elif keep["spare"]:
                    e = sp.value_load(eid[0:1, j - EXPERTS:j - EXPERTS + 1], min_val=0, max_val=EXPERTS - 1)
                else:
                    e = j if isinstance(j, int) else sp.snap(j)
                up = d["w_gate_up"][0, bass.ds(e, 1)].rearrange("a (k p) n -> p (a k) n", p=P)
                down = d["w_down"][0, bass.ds(e, 1)].rearrange("a (k p) n -> p (a k) n", p=P)
                wait(sp, up_lo_done, 4 * j - 4)
                sp.dma_start(up_raw[:, par], up).then_inc(up_in[par], 16)
                wait(sp, down_lo_done, 2 * j - 2)
                sp.dma_start(down_raw[:, par], down).then_inc(down_in[par], 16)

            def stretch(j0, j1):
                keep["spare"] = j0 > 0
                run(sp, body, j0, j1)

            all_blocks(sp, stretch)

        @block.gpsimd
        def _(g):
            with nc.allow_non_contiguous_dma(reason="a column of slots for each block"):
                g.dma_start(choice[:], d["slot_choice"].rearrange("(b p) a -> p (b a)", p=P)).then_inc(choice_in, 16)
            g.wait_ge(token_ready, 1)

            def gather(j):
                wait(g, x_turned, 2 * (j - 1))
                g.indirect_dma_start(out=rows[:, j % 2, :], out_offset=None, in_=d["h_rows"],
                                     in_offset=bass.IndirectOffsetOnAxis(ap=token[:, j:j + 1], axis=0),
                                     bounds_check=TOK - 1, oob_is_err=False).then_inc(rows_in[j % 2], 16)

            def scatter(j):
                g.wait_ge(y_left, j + 1)
                g.wait_ge(y_right, j + 1)
                g.indirect_dma_start(out=d["y_choice"], out_offset=bass.IndirectOffsetOnAxis(ap=choice[:, j:j + 1], axis=0),
                                     in_=y_rows[:, j % 2, :], in_offset=None,
                                     bounds_check=2 * TOK - 1, oob_is_err=False).then_inc(y_stored[j % 2], 16)

            def stretch(j0, j1):
                gather(j0)
                gather(j0 + 1)
                for j in range(j0, j1):
                    if j + 2 < j1:
                        gather(j + 2)
                    if j > j0:
                        scatter(j - 1)
                scatter(j1 - 1)
                g.wait_ge(y_stored[0], 16 * ((j1 + 1) // 2))
                g.wait_ge(y_stored[1], 16 * (j1 // 2))

            all_blocks(g, stretch)

        @block.tensor
        def _(pe):
            def turn_rows(j, n, par):
                pe.wait_ge(rows_in[par], 16 * (n + 1))
                for half in range(2):
                    wait(pe, x_lo_done, 2 * j - 1 + half)
                    for k in range(4):
                        kk = 4 * half + k
                        last = pe.transpose(bank_x[half][:, P * k:P * (k + 1)], rows[:, par, P * kk:P * (kk + 1)], ident)
                    last.then_inc(x_turned, 1)

            def gate_up(j, par):
                pe.wait_ge(x_lo_done, 2 * j + 2)
                wait(pe, act_done, j - 1)
                for k in range(KT):
                    if k % 2 == 0:
                        pe.wait_ge(up_lo_done, 4 * j + k // 2 + 1)
                    pe.matmul(bank_g[par][:], xT_hi[:, par, k, :], up_hi[:, k, :], start=(k == 0), stop=False)
                    pe.matmul(bank_g[par][:], xT_hi[:, par, k, :], up_lo[:, k, :], start=False, stop=False)
                    last = pe.matmul(bank_g[par][:], xT_lo[:, par, k, :], up_hi[:, k, :], start=False, stop=(k == KT - 1))
                    if k % 2 == 1:
                        last.then_inc(up_used, 1)

            def turn_act(j):
                pe.wait_ge(act_done, j + 1)
                wait(pe, a_lo_done, j)
                for k in range(2):
                    last = pe.transpose(bank_a[:, P * k:P * (k + 1)], act_rows[:, P * k:P * (k + 1)], ident)
                last.then_inc(a_turned, 1)

            def down(j, par):
                pe.wait_ge(a_lo_done, j + 1)
                wait(pe, y_left, j)
                wait(pe, y_right, j)
                for k in range(2):
                    pe.wait_ge(down_lo_done, 2 * j + k + 1)
                    for strip in range(2):
                        cols = slice(512 * strip, 512 * (strip + 1))
                        pe.matmul(bank_d[strip][:], aT_hi[:, k, :], down_hi[:, par, k, cols], start=(k == 0), stop=False)
                        pe.matmul(bank_d[strip][:], aT_hi[:, k, :], down_lo[:, par, k, cols], start=False, stop=False)
                        last = pe.matmul(bank_d[strip][:], aT_lo[:, k, :], down_hi[:, par, k, cols], start=False, stop=(k == 1))
                    last.then_inc(down_used, 1)

            def body(j, n, par, first, last):
                if not last:
                    turn_rows(j + 1, n + 1 if par else n, 1 - par)
                gate_up(j, par)
                if not first:
                    down(j - 1, 1 - par)
                turn_act(j)

            def stretch(j0, j1):
                turn_rows(j0, j0 // 2, 0)
                run(pe, body, j0, j1)
                down(j1 - 1, (j1 - 1) % 2)

            all_blocks(pe, stretch)

        @block.scalar
        def _(act):
            def split_up(j, n, par):
                act.wait_ge(up_in[par], 16 * (n + 1))
                for x in range(4):
                    wait(act, up_used, 4 * j - 3 + x)
                    act.copy(up_hi[:, 2 * x:2 * x + 2, :], up_raw[:, par, 2 * x:2 * x + 2, :]).then_inc(up_hi_done, 1)

            def split_down(j, n, par):
                act.wait_ge(down_in[par], 16 * (n + 1))
                for x in range(2):
                    wait(act, down_used, 2 * j - 3 + x)
                    act.copy(down_hi[:, par, x, :], down_raw[:, par, x, :]).then_inc(down_hi_done, 1)

            def take_rows(j, par):
                for half in range(2):
                    act.wait_ge(x_turned, 2 * j + half + 1)
                    act.copy(xT_hi[:, par, 4 * half:4 * half + 4, :], bank_x[half][:].rearrange("p (k c) -> p k c", k=4)).then_inc(x_hi_done, 1)

            def store(j, par, n):
                act.wait_ge(down_used, 2 * j + 2)
                wait(act, y_stored[par], 16 * n)
                act.copy(y_rows[:, par, 0:512], bank_d[0][:]).then_inc(y_left, 1)

            def body(j, n, par, first, last):
                if not last:
                    take_rows(j + 1, 1 - par)
                split_down(j, n, par)
                if not last:
                    split_up(j + 1, n + 1 if par else n, 1 - par)
                act.wait_ge(up_used, 4 * j + 4)
                wait(act, act_done, j)
                act.activation(silu[:], bank_g[par][:, 0:DE], ACT.Silu).then_inc(silu_done, 1)
                if not first:
                    store(j - 1, 1 - par, n if par else n - 1)
                act.wait_ge(a_turned, j + 1)
                act.copy(aT_hi[:], bank_a[:, 0:2 * P].rearrange("p (k c) -> p k c", k=2)).then_inc(a_hi_done, 1)

            def stretch(j0, j1):
                split_up(j0, j0 // 2, 0)
                take_rows(j0, 0)
                run(act, body, j0, j1)
                store(j1 - 1, (j1 - 1) % 2, (j1 - 1) // 2)

            all_blocks(act, stretch)

        @block.vector
        def _(v):
            v.memset(rows[:], 0.0)
            v.wait_ge(choice_in, 16)
            v.tensor_copy(choice_f[:], choice[:])
            v.drain()
            v.tensor_scalar(above[:], choice_f[:], float(TOK), -float(TOK), ALU.is_ge, ALU.mult)
            v.drain()
            v.tensor_tensor(choice_f[:], choice_f[:], above[:], ALU.add)
            v.drain()
            v.tensor_copy(token[:], choice_f[:]).then_inc(token_ready, 1)

            def split_up(j, par):
                for x in range(4):
                    v.wait_ge(up_hi_done, 4 * j + x + 1)
                    s = slice(2 * x, 2 * x + 2)
                    v.tensor_tensor(up_lo[:, s, :], up_raw[:, par, s, :], up_hi[:, s, :].bitcast(F32), ALU.subtract).then_inc(up_lo_done, 1)

            def take_rows(j, par):
                for half in range(2):
                    v.wait_ge(x_hi_done, 2 * j + half + 1)
                    s = slice(4 * half, 4 * half + 4)
                    v.tensor_tensor(xT_lo[:, par, s, :], bank_x[half][:].rearrange("p (k c) -> p k c", k=4), xT_hi[:, par, s, :].bitcast(F32),
                                    ALU.subtract).then_inc(x_lo_done, 1)

            def store(j, par, n):
                v.wait_ge(down_used, 2 * j + 2)
                wait(v, y_stored[par], 16 * n)
                v.tensor_copy(y_rows[:, par, 512:D], bank_d[1][:]).then_inc(y_right, 1)

            def body(j, n, par, first, last):
                if not last:
                    take_rows(j + 1, 1 - par)
                for x in range(2):
                    v.wait_ge(down_hi_done, 2 * j + x + 1)
                    v.tensor_tensor(down_lo[:, par, x, :], down_raw[:, par, x, :], down_hi[:, par, x, :].bitcast(F32), ALU.subtract).then_inc(down_lo_done, 1)
                if not last:
                    split_up(j + 1, 1 - par)
                v.wait_ge(silu_done, j + 1)
                wait(v, a_turned, j)
                v.tensor_tensor(act_rows[:], silu[:], bank_g[par][:, DE:2 * DE], ALU.mult).then_inc(act_done, 1)
                if not first:
                    store(j - 1, 1 - par, n if par else n - 1)
                v.wait_ge(a_hi_done, j + 1)
                v.tensor_tensor(aT_lo[:], bank_a[:, 0:2 * P].rearrange("p (k c) -> p k c", k=2), aT_hi[:].bitcast(F32), ALU.subtract).then_inc(a_lo_done, 1)

            def stretch(j0, j1):
                split_up(j0, 0)
                take_rows(j0, 0)
                run(v, body, j0, j1)
                store(j1 - 1, (j1 - 1) % 2, (j1 - 1) // 2)

            all_blocks(v, stretch)


def combine(nc, d, keep):
    with ExitStack() as ctx:
        sb = lambda name, shape, dt=F32: ctx.enter_context(nc.sbuf_tensor(name, shape, dt))
        sem = lambda name: ctx.enter_context(nc.semaphore("c_" + name))
        h, slots, weights = keep["h"], keep["slots"], keep["weights"]
        ln_g, ln_b = sb("ln2_g_sb", [P, D]), sb("ln2_b_sb", [P, D])
        picked = sb("picked", [P, TB, 2, D])
        stats, mv, root, eps = sb("stats2", [P, 12]), sb("mv2", [P, 2]), sb("root2", [P, 2]), sb("eps2", [P, 1])
        picked_in = [sem(f"picked_in{b}") for b in range(TB)]
        small_in, var_ready, root_done, y_ready, y_stored, consts_done = (sem(n) for n in ("small_in", "var_ready", "root_done", "y_ready", "y_stored", "consts_done"))
        block = ctx.enter_context(nc.Block())

        @block.sync
        def _(sp):
            for b in range(TB):
                for n in range(2):
                    sp.dma_start(picked[:, b, n, :], d["y_choice"][TOK * n + P * b:TOK * n + P * (b + 1), :]).then_inc(picked_in[b], 16)
            sp.dma_start(ln_g[:], d["ln2_g"].to_broadcast((P, D))).then_inc(small_in, 16)
            sp.dma_start(ln_b[:], d["ln2_b"].to_broadcast((P, D))).then_inc(small_in, 16)
            for b in range(TB):
                sp.wait_ge(y_ready, b + 1)
                out = d["y_prompt"][0, P * b:P * (b + 1), :] if b < QB else d["y_sample"].rearrange("s q d -> (s q) d")
                sp.dma_start(out, picked[:, b, 0, :]).then_inc(y_stored, 16)
            sp.wait_ge(y_stored, 16 * TB)

        @block.scalar
        def _(act):
            act.wait_ge(consts_done, 1)
            for b in range(TB):
                act.wait_ge(var_ready, b + 1)
                act.activation(root[:, 0:1], mv[:, 1:2], ACT.Sqrt, bias=eps[:, 0:1], scale=1.0).then_inc(root_done, 1)

        @block.vector
        def _(v):
            v.memset(eps[:], EPS).then_inc(consts_done, 1)
            for b in range(TB):
                y = picked[:, b, 0, :]
                v.wait_ge(picked_in[b], 32)
                v.tensor_scalar(y, y, weights[:, 0, b:b + 1], None, ALU.mult)
                v.drain()
                v.scalar_tensor_tensor(y, picked[:, b, 1, :], weights[:, 1, b:b + 1], y, ALU.mult, ALU.add)
                v.drain()
                v.scalar_tensor_tensor(y, h[:, b, :], ALPHA, y, ALU.mult, ALU.add)
                v.drain()
                layer_norm_steps(v, y, stats, mv[:], var_ready, root_done, b + 1)
                v.reciprocal(root[:, 1:2], root[:, 0:1])
                v.drain()
                v.tensor_scalar(y, y, mv[:, 0:1], root[:, 1:2], ALU.subtract, ALU.mult)
                v.drain()
                if b == 0:
                    v.wait_ge(small_in, 32)
                v.tensor_tensor(y, y, ln_g[:], ALU.mult)
                v.drain()
                v.tensor_tensor(y, y, ln_b[:], ALU.add).then_inc(y_ready, 1)


def program(nc, d):
    with ExitStack() as ctx:
        sb = lambda name, shape, dt=F32: ctx.enter_context(nc.sbuf_tensor(name, shape, dt))
        keep = {"const": sb("const_sb", [P, C_END]), "yc": sb("yc", [P, KT, TOK]), "ya": sb("ya", [P, KT, TOK]),
                "slots": sb("slots", [P, 2, TB], U32), "weights": sb("weights", [P, 2, TB]), "eid": sb("eid", [1, SPARE + 1], I32)}
        keep["h"] = keep["yc"][:].rearrange("p k t -> p (k t)").rearrange("p (b n) -> p b n", n=D)
        d["gates"] = nc.dram_tensor("gates", [2, KT, P, TOK], F32).ap()
        d["h_rows"] = nc.dram_tensor("h_rows", [TOK, D], F32).ap()
        d["slot_choice"] = nc.dram_tensor("slot_choice", [BLOCKS * P, 1], U32).ap()
        d["y_choice"] = nc.dram_tensor("y_choice", [2 * TOK, D], F32).ap()
        project_and_attend(nc, d, keep)
        merge_branches(nc, d, keep)
        route(nc, d, keep)
        run_experts(nc, d, keep)
        combine(nc, d, keep)


INPUTS = ["x_prompt", "x_sample", "cache_k", "cache_v", "state_conv", "meta_tokens", "w_in", "conv_w", "lambda_qk", "subln_g",
          "w_branch", "w_out", "ln1_g", "ln1_b", "w_group", "b_group", "w_router", "b_router", "w_gate_up", "w_down", "ln2_g", "ln2_b"]
OUTPUTS = {
    "y_prompt": (1, SEQ, D), "y_sample": (STREAMS, NEW, D),
    "new_k_prompt": (1, 1, META + SEQ, HEADS, P), "new_v_prompt": (1, 1, META + SEQ, HEADS, P), "new_conv_prompt": (1, 1, 2, D),
    "new_k_sample": (1, STREAMS, NEW, HEADS, P), "new_v_sample": (1, STREAMS, NEW, HEADS, P), "new_conv_sample": (1, STREAMS, 2, D),
}


def kernel(**inputs):
    import concourse.bacc as bacc
    from concourse.bass_utils import run_bass_kernel_spmd

    nc = bacc.Bacc("TRN2", target_bir_lowering=False, num_devices=1)
    arrays = {name: np.ascontiguousarray(inputs[name]) for name in INPUTS}
    arrays["const"] = constants()
    d = {name: nc.dram_tensor("in_" + name, a.shape, F32, kind="ExternalInput").ap() for name, a in arrays.items()}
    for name, shape in OUTPUTS.items():
        d[name] = nc.dram_tensor("out_" + name, shape, F32, kind="ExternalOutput").ap()
    program(nc, d)
    result = run_bass_kernel_spmd(nc, [{"in_" + n: a for n, a in arrays.items()}], core_ids=[0])
    return tuple(result.results[0]["out_" + name] for name in OUTPUTS)
```

```python
from contextlib import ExitStack

import concourse.bass as bass
import numpy as np
from concourse import mybir

F32 = mybir.dt.float32
F32R = mybir.dt.float32r
U32 = mybir.dt.uint32
I32 = mybir.dt.int32
ALU = mybir.AluOpType
ACT = mybir.ActivationFunctionType
AX = mybir.AxisListType

P = 128
D = 1024
KT = D // P
META, SEQ, STREAMS, NEW, PAST = 16, 512, 8, 16, 256
SAMPLE = STREAMS * NEW
T = META + SEQ + SAMPLE
TOK = SEQ + SAMPLE
HALF = T // 2
TB = TOK // P
QB = SEQ // P
CHUNK = 64
HEADS = 8
CACHED = META + PAST
OWN = 2
LAM_INIT = 0.2
ALPHA = 2.0 ** 0.25
EPS = 1e-5
SCALE = 64 ** -0.5
MASKED = -1e30
EXPERTS, PER_GROUP, GROUPS = 32, 8, 4
DE = 256
SPARE = (2 * TOK) // (P + 1)
BLOCKS = EXPERTS + SPARE
ROUND = 1.5 * 2 ** 23
NONE = 1 << 15
COL = {"h": 0, "bg": D, "cg": 2 * D, "q": 3 * D, "k": 4 * D, "v": 5 * D, "gc": 6 * D, "ga": 7 * D}
UNITS = ["h", "cg", "bg", "gc", "ga", "k", "v", "q"]
NU = len(UNITS)

C_ID, C_SPREAD, C_MASK, C_UPPER = 0, 128, 384, 640
C_GROUP, C_EXPERT, C_BLOCK, C_FIRST, C_SIGN, C_TOKEN, C_COLUMN = 768, 800, 832, 848, 880, 881, 892
C_END = C_COLUMN + P


def constants():
    c = np.zeros((P, C_END), np.float32)
    row = np.arange(P)
    c[:, C_ID:C_ID + P] = np.eye(P)
    for g in range(2):
        for r in range(P):
            s, q = 4 * g + r // 32, r % 16
            c[r, C_SPREAD + P * g + 16 * s + q] = 1.0
            c[r, C_MASK + P * g:C_MASK + P * (g + 1)] = np.where(row // 16 == s, 0.0, MASKED)
    c[:, C_UPPER:C_UPPER + P] = row[:, None] < row[None, :]
    c[:, C_GROUP:C_GROUP + EXPERTS] = np.arange(EXPERTS) // PER_GROUP
    c[:, C_EXPERT:C_EXPERT + EXPERTS] = np.arange(EXPERTS)
    c[:, C_BLOCK:C_BLOCK + SPARE] = np.arange(SPARE)
    c[:, C_FIRST:C_FIRST + EXPERTS] = np.arange(EXPERTS) * P
    c[:, C_SIGN] = (row // 16) % 2
    for n in range(2 * TB):
        c[:, C_TOKEN + n] = P * n + row
    c[:, C_COLUMN:C_END] = row
    return c


def wait(eng, sem, value):
    if not isinstance(value, int) or value > 0:
        eng.wait_ge(sem, value)


def slab(nc, ctx, name, floats):
    base = (nc.sbuf_base + 31) // 32 * 32
    ctx.enter_context(nc.sbuf_tensor(name, [P, floats], F32))
    return lambda name, shape, dt, at: nc.alloc_sbuf_tensor_at(name, shape, dt, offset=base + 4 * at)


def project_and_attend(nc, d, keep):
    with ExitStack() as ctx:
        sb = lambda name, shape, dt=F32: ctx.enter_context(nc.sbuf_tensor(name, shape, dt))
        pb = lambda name, shape: ctx.enter_context(nc.psum_tensor(name, shape, F32))
        sem = lambda name: ctx.enter_context(nc.semaphore(name))
        yc, ya, const = keep["yc"], keep["ya"], keep["const"]

        x_hi, x_lo = keep["x_hi"], keep["x_lo"]
        w_raw = sb("w_raw", [P, 2, KT, P])
        w_hi, w_lo = sb("w_hi", [P, 2, KT, P], F32R), sb("w_lo", [P, 2, KT, P], F32R)
        hi_place, lo_place = slab(nc, ctx, "hi_slab", 3 * 17 * P), slab(nc, ctx, "lo_slab", (OWN + 1) * (STREAMS * P + P) + 2 * T + TOK)
        ya_hi, ya_lo = hi_place("ya_hi", [P, KT, TOK], F32R, 0), lo_place("ya_lo", [P, KT, TOK], F32R, 0)
        k_cache, v_cache = hi_place("k_cache", [P, 17, P], F32, 0), hi_place("v_cache", [P, 17, P], F32, 17 * P)
        kcT = hi_place("kcT", [P, 17 * P], F32, 34 * P)
        own_T = lo_place("own_T", [P, OWN, STREAMS * P + P], F32, 0)
        q_pad = lo_place("q_pad", [P, STREAMS * P + P], F32, OWN * (STREAMS * P + P))
        at = (OWN + 1) * (STREAMS * P + P)
        h_buf, u_buf, conv = (lo_place(*x) for x in (("h_buf", [P, T], F32, at), ("u_buf", [P, T], F32, at + T), ("conv", [P, TOK], F32, at + 2 * T)))
        u_hist = sb("u_hist", [P, STREAMS, NEW + 2])
        u_last = sb("u_last", [P, KT, 18])
        hist_T = sb("hist_T", [P, KT, 16])
        taps = sb("taps", [P, KT, 3])
        gate = sb("gate", [P, 2, TOK])
        kT, vT, qT = sb("kT", [P, T]), sb("vT", [P, T]), sb("qT", [P, TOK])
        q_maps = sb("q_maps", [P, STREAMS, 32])
        k_rows, v_rows = sb("k_rows", [P, 6, P]), sb("v_rows", [P, 6, P])
        prob = sb("prob", [P, 2, META + SEQ])
        mix = sb("mix", [P, 2, META + SEQ])
        mixT, mixT_meta = keep["w_out_raw"][:].rearrange("p a b -> p (a b)").rearrange("p (t q) -> p t q", t=QB), sb("mixT_meta", [META, SEQ])
        shared_T = sb("shared_T", [P, 2, P])
        spread = sb("spread", [P, 2, P])
        neg_max, row_sum = sb("neg_max", [P, 2]), sb("row_sum", [P, 2])
        inv = sb("inv", [P, 4])
        lam = sb("lam", [P, 8])
        lam_in, lam_tmp = sb("lam_in", [P, 256]), sb("lam_tmp", [P, 64])
        x_rows = [buf[:, 8 * n:8 * n + 8, :].rearrange("p a b -> p (a b)") for buf in (k_cache, v_cache) for n in range(2)]
        x_rows.append(kcT[:, 0:D])
        meta_rows = kcT[0:META, D:2 * D]
        state_rows = mixT[0:16, 0:2, :].rearrange("p a b -> p (a b)")
        last_rows = mixT[0:18, 0:2, :].rearrange("p a b -> p (a b)")
        gated = kT[:, 0:TOK]
        square, root, ones, eps, gain = sb("square", [P, TOK]), sb("root", [P, TOK]), sb("ones", [P, P]), sb("eps", [P, 1]), sb("gain", [P, 2])

        bank_u = [pb("bank_u0", [P, 512]), pb("bank_u1", [P, 512])]
        bank_s = [pb("bank_s0", [P, 1024]), pb("bank_s1", [P, 1024])]
        bank_t, bank_o = pb("bank_t", [P, 512]), pb("bank_o", [P, 512])
        meta_T = [bank_t[0:META, 384:512]] * (QB - 1) + [bank_s[0][0:META, 768:896]]
        bank_r = bank_s[1][:, 640:896]
        bank_n = bank_s[0][:, 640:768]
        turn_banks = [bank_t, bank_o] + bank_u
        ident = const[:, C_ID:C_ID + P]

        names = ["ident_in", "const_in", "meta_in", "state_in", "taps_in", "lam_in_sem", "lam_sums", "lam_exp",
                 "turned", "turned_hi", "turned_lo", "hist_done", "split_hi", "split_lo", "half_done", "hist_ready",
                 "k_cache_in", "v_cache_in", "t_full", "t_free", "o_full", "o_free", "r_full", "r_free",
                 "max_ready0", "max_ready1", "exp_done0", "exp_done1", "scores0", "scores1", "mix_ready", "spread_ready",
                 "q_maps_ready", "kv_stored", "last_stored", "last_turned", "gain_in", "rows_copied",
                 "yc_hi_done", "yc_lo_done", "ya_hi_done", "ya_lo_done", "normed", "gate_ready", "merged_done", "merged_hi"]
        s = {n: sem("a_" + n) for n in names}
        x_in = [sem(f"a_x_in{b}") for b in range(TB)]
        w_in_sem = [sem("a_w_in0"), sem("a_w_in1")]
        gate_stored = [sem("a_gate_stored0"), sem("a_gate_stored1")]
        gate_in = [sem("a_gate_in0"), sem("a_gate_in1")]
        evicted = [sem("a_evicted0"), sem("a_evicted1")]
        scores = [s["scores0"], s["scores1"]]
        max_ready = [s["max_ready0"], s["max_ready1"]]
        exp_done = [s["exp_done0"], s["exp_done1"]]
        block = ctx.enter_context(nc.Block())

        fill_t = lambda i, n: 10 * i - 8 + n
        fill_o = lambda i, n: 5 * i - 5 + n
        rows_t = lambda i, n: n if isinstance(i, int) and i == 0 else fill_t(i, T_ROWS + n)
        fill_s = lambda i, n: 5 * (i - 1) + n
        T_SAMPLE, T_PROMPT, T_ROWS, O_SAMPLE, O_PROMPT, O_NORM = 3, 4, 8, 2, 3, 4

        def turns(eng, body, second_branch):
            body(0, True, False)
            with eng.Fori(1, HEADS) as i:
                body(i, True, True)
            body(HEADS, False, True)
            second_branch(0, 0, False)
            second_branch(0, 1, False)
            with eng.Fori(1, KT // 2 - 1) as q:
                second_branch(q, 0, False)
                second_branch(q, 1, False)
            second_branch(KT // 2 - 1, 0, False)
            second_branch(KT // 2 - 1, 1, True)

        BRANCH = [NU * HEADS, NU * HEADS + KT]
        one = lambda t, x, cols=slice(0, TOK): t[:, bass.ds(x, 1), cols].rearrange("p a t -> p (a t)")

        def columns(u, half):
            first, w = (0, HALF) if UNITS[u] in ("h", "cg", "k", "v") else (META, TOK // 2)
            return slice(first + w * half, first + w * (half + 1))

        w_view = d["w_in"][0].rearrange("(k p) n -> p k n", p=P)
        keys = lambda b: META + P * (b + 1)

        @block.sync
        def _(sp):
            sp.dma_start(const[:, C_ID:C_ID + P], d["const"][:, C_ID:C_ID + P]).then_inc(s["ident_in"], 16)
            for b in range(TB):
                src = d["x_prompt"][0, P * b:P * (b + 1), :] if b < QB else d["x_sample"].rearrange("s q d -> (s q) d")
                sp.dma_start(x_rows[b], src).then_inc(x_in[b], 16)
                if b == 1:
                    sp.dma_start(meta_rows, d["meta_tokens"]).then_inc(s["meta_in"], 16)

            def load_branch(br, m, par):
                n = BRANCH[br] + m
                view = d["w_branch"][0, br].rearrange("(k p) n -> p k n", p=P)
                src = view[:, :, P * m:P * m + P] if isinstance(m, int) else view[:, :, bass.ds(sp.snap(P * m), P)]
                gate_src = d["gates"][br, bass.ds(m if isinstance(m, int) else sp.snap(m), 1)].rearrange("a p t -> p (a t)")
                sp.wait_ge(s["split_lo"], n - 1)
                sp.dma_start(w_raw[:, par], src).then_inc(w_in_sem[par], 16)
                if isinstance(m, int) and m < 2 and br == 0:
                    sp.wait_ge(gate_stored[0], 16 * KT)
                    sp.wait_ge(gate_stored[1], 16 * KT)
                else:
                    sp.wait_ge(evicted[0], n - 1)
                    sp.wait_ge(evicted[1], n - 1)
                sp.dma_start(gate[:, par, :], gate_src).then_inc(gate_in[par], 16)

            def body(i, units, attend):
                if not units:
                    for m in range(KT):
                        load_branch(0, m, m % 2)
                    return
                for u, name in enumerate(UNITS):
                    n = NU * i + u
                    src = w_view[:, :, bass.ds(sp.snap(i * P + COL[name]) if not isinstance(i, int) else i * P + COL[name], P)]
                    wait(sp, s["split_lo"], n - 1)
                    sp.dma_start(w_raw[:, u % 2], src).then_inc(w_in_sem[u % 2], 16)
                    if u == 6:
                        for name, buf, done in (("cache_k", k_cache, "k_cache_in"), ("cache_v", v_cache, "v_cache_in")):
                            srcs = [d[name][0, :, P * t:P * (t + 1), bass.ds(sp.snap(i + 0) if not isinstance(i, int) else i, 1), :]
                                    .rearrange("s p h d -> p s (h d)") for t in range(OWN)]
                            srcs.append(d[name][0, :, OWN * P:CACHED, bass.ds(sp.snap(i + 0) if not isinstance(i, int) else i, 1), :])
                            if isinstance(i, int):
                                sp.wait_ge(s["turned"], 2 * TB + 3)
                            else:
                                sp.wait_ge(s["o_full"], fill_o(i, O_SAMPLE) + 1)
                            for t in range(OWN):
                                sp.dma_start(buf[:, t:OWN * STREAMS:OWN, :], srcs[t]).then_inc(s[done], 16)
                            sp.dma_start(buf[:, 16, :], srcs[OWN]).then_inc(s[done], 16)

            turns(sp, body, lambda q, par, end: load_branch(1, 2 * q + par, par))
            sp.wait_ge(s["o_full"], fill_o(HEADS, O_PROMPT) + 1)
            for k in range(2):
                sp.dma_start(keep["w_out_raw"][:, k], d["w_out"][0, P * k:P * (k + 1), :]).then_inc(keep["w_out_in"][k], 16)

        @block.gpsimd
        def _(g):
            g.dma_start(lam_in[:], d["lambda_qk"].rearrange("l a b -> l (a b)").to_broadcast((P, 256))).then_inc(s["lam_in_sem"], 16)
            g.dma_start(state_rows, d["state_conv"][0].rearrange("s j d -> (s j) d")).then_inc(s["state_in"], 16)
            with nc.allow_non_contiguous_dma(reason="three taps of each channel, once"):
                g.dma_start(gain[:, 0:1], d["subln_g"].rearrange("l p -> p l")).then_inc(s["gain_in"], 16)
                for k in range(KT):
                    g.dma_start(taps[:, k, :], d["conv_w"][0, :, P * k:P * (k + 1)].rearrange("w p -> p w")).then_inc(s["taps_in"], 16)
            g.dma_start(const[:, P:C_COLUMN], d["const"][:, P:C_COLUMN]).then_inc(s["const_in"], 16)

        @block.tensor
        def _(pe):
            pe.wait_ge(s["ident_in"], 16)
            for f in range(2 * TB + 2):
                b, half = divmod(f, 2)
                rows, w = (x_rows[b], P) if b < TB else (meta_rows, META)
                if b < TB:
                    pe.wait_ge(x_in[b], 16)
                else:
                    pe.wait_ge(s["meta_in"], 16)
                wait(pe, s["turned_lo"], f - 3)
                bank = turn_banks[f % 4][:].rearrange("p (k c) -> p k c", k=4)
                for k in range(4):
                    kk = 4 * half + k
                    last = pe.transpose(bank[:, k, 0:w], rows[:, P * kk:P * (kk + 1)], ident[0:w, 0:w])
                last.then_inc(s["turned"], 1)
            pe.wait_ge(s["state_in"], 16)
            pe.wait_ge(s["turned_lo"], 2 * TB + 1)
            for k in range(KT):
                last = pe.transpose(bank_t[:, 16 * k:16 * k + 16], state_rows[:, P * k:P * (k + 1)], ident[0:16, 0:16])
            last.then_inc(s["turned"], 1)
            pe.wait_ge(s["hist_done"], 1)
            pe.wait_ge(s["turned_lo"], 2 * TB + 2)

            def unit(i, u):
                n = NU * i + u
                pe.wait_ge(s["split_lo"], n + 1)
                for half in range(2):
                    wait(pe, evicted[half], n)
                    cols = columns(u, half)
                    out = bank_u[half][:, 0:cols.stop - cols.start]
                    for k in range(KT):
                        pe.matmul(out, w_hi[:, u % 2, k, :], x_hi[:, k, cols], start=(k == 0), stop=False)
                        pe.matmul(out, w_hi[:, u % 2, k, :], x_lo[:, k, cols], start=False, stop=False)
                        last = pe.matmul(out, w_lo[:, u % 2, k, :], x_hi[:, k, cols], start=False, stop=(k == KT - 1))
                    last.then_inc(s["half_done"], 1)

            def branch_product(br, m, par):
                n = BRANCH[br] + m
                hi, lo, ready = ((x_hi, x_lo, s["yc_lo_done"]), (ya_hi, ya_lo, s["ya_lo_done"]))[br]
                pe.wait_ge(s["split_lo"], n + 1)

                def part(k, half):
                    cols = slice(TOK // 2 * half, TOK // 2 * (half + 1))
                    out = bank_u[half][:, 0:TOK // 2]
                    pe.matmul(out, w_hi[:, par, k, :], hi[:, k, cols], start=(k == 0), stop=False)
                    pe.matmul(out, w_hi[:, par, k, :], lo[:, k, cols], start=False, stop=False)
                    last = pe.matmul(out, w_lo[:, par, k, :], hi[:, k, cols], start=False, stop=(k == KT - 1))
                    if k == KT - 1:
                        last.then_inc(s["half_done"], 1)

                if isinstance(m, int) and m == 0:
                    pe.wait_ge(evicted[0], n)
                    pe.wait_ge(evicted[1], n)
                    for k in range(KT):
                        pe.wait_ge(ready, k + 1)
                        part(k, 0)
                        part(k, 1)
                else:
                    for half in range(2):
                        pe.wait_ge(evicted[half], n)
                        for k in range(KT):
                            part(k, half)

            def turn_cache(i):
                pe.wait_ge(s["k_cache_in"], 48 * i)
                for f in range(5):
                    if f % 2 == 0:
                        bank, full, free, n = bank_t, "t_full", "t_free", fill_t(i, f // 2)
                    else:
                        bank, full, free, n = bank_o, "o_full", "o_free", fill_o(i, f // 2) + 1
                    pe.wait_ge(s[free], n)
                    for k in range(4 * f, min(4 * f + 4, 17)):
                        last = pe.transpose(bank[:, P * (k % 4):P * (k % 4) + P], k_cache[:, k, :], ident)
                    last.then_inc(s[full], 1)

            def sample_scores(i):
                pe.wait_ge(s["q_maps_ready"], i)
                pe.wait_ge(s["t_free"], fill_t(i, 3))
                pe.wait_ge(s["o_free"], fill_o(i, 2) + 1)
                for g in range(2):
                    for j in range(4):
                        st = 4 * g + j
                        pe.matmul(bank_s[g][:, 0:2 * P], q_pad[:, P * st:P * (st + 1)], kcT[:, 2 * P * st:2 * P * (st + 1)],
                                  start=(j == 0), stop=(j == 3))
                    q_all = q_maps[:, 4 * g:4 * g + 4, :].rearrange("p s c -> p (s c)")
                    pe.matmul(bank_s[g][:, 2 * P:3 * P], q_all, kcT[:, 16 * P:17 * P], start=True, stop=True)
                    pe.matmul(bank_s[g][:, 3 * P:4 * P], q_all, kT[:, META + SEQ:T], start=True, stop=True).then_inc(scores[g], 1)

            def sample_mix(i):
                pe.wait_ge(s["r_free"], 2 * i)
                pe.wait_ge(s["spread_ready"], i)
                pe.wait_ge(s["t_free"], fill_t(i, T_SAMPLE))
                for t in range(4):
                    for g in range(2):
                        last = pe.matmul(bank_t[:, P * t:P * (t + 1)], prob[:, g, P * t:P * (t + 1)], spread[:, g, :],
                                         start=(g == 0), stop=(g == 1))
                last.then_inc(s["t_full"], 1)

            def sample_values(i):
                pe.wait_ge(s["v_cache_in"], 48 * i)
                pe.wait_ge(s["t_free"], fill_t(i, T_SAMPLE) + 1)
                pe.wait_ge(s["o_free"], fill_o(i, O_SAMPLE) + 1)
                out = bank_o[:, 0:P]
                for st in range(STREAMS):
                    for t in range(OWN):
                        pe.matmul(out, v_cache[:, OWN * st + t, :], own_T[:, t, P * st:P * (st + 1)],
                                  start=(st == 0 and t == 0), stop=False)
                pe.matmul(out, v_cache[:, 16, :], shared_T[:, 0, :], start=False, stop=False)
                pe.matmul(out, v_rows[:, 4, :], shared_T[:, 1, :], start=False, stop=True).then_inc(s["o_full"], 1)

            def prompt_scores(i, b):
                for m in range(2):
                    wait(pe, exp_done[m], fill_s(i, 1 + b))
                    r = slice(64 * m, 64 * m + 64)
                    w = keys(b)
                    last = pe.matmul(bank_s[m][:, 0:min(w, 512)], qT[r, P * b:P * (b + 1)], kT[r, 0:min(w, 512)], start=True, stop=True)
                    if w > 512:
                        last = pe.matmul(bank_s[m][:, 512:w], qT[r, P * b:P * (b + 1)], kT[r, 512:w], start=True, stop=True)
                    last.then_inc(scores[m], 1)

            def prompt_turn(i, b):
                pe.wait_ge(s["mix_ready"], 4 * (i - 1) + b + 1)
                pe.wait_ge(s["t_free"], fill_t(i, T_PROMPT + b))
                for t in range(b + 1):
                    last = pe.transpose(bank_t[:, P * t:P * (t + 1)], mix[:, b % 2, META + P * t:META + P * (t + 1)], ident)
                pe.transpose(meta_T[b], mix[:, b % 2, 0:META], ident).then_inc(s["t_full"], 1)

            def prompt_values(i):
                pe.wait_ge(s["t_free"], fill_t(i, T_PROMPT + QB - 1) + 1)
                pe.wait_ge(s["o_free"], fill_o(i, O_PROMPT) + 1)
                pe.matmul(bank_o[:], v_rows[0:META, 5, :], mixT_meta[:], start=True, stop=False)
                for t in range(QB):
                    last = pe.matmul(bank_o[:, P * t:SEQ], v_rows[:, t, :], mixT[:, t, P * t:SEQ], start=False, stop=(t == QB - 1))
                last.then_inc(s["o_full"], 1)

            def turn_rows(i, n):
                src, u = ((kT, 5), (vT, 6))[n]
                for half in range(2):
                    pe.wait_ge(evicted[half], NU * i + u + 1)
                wait(pe, s["t_free"], rows_t(i, n))
                for t in range(QB):
                    last = pe.transpose(bank_t[:, P * t:P * (t + 1)], src[:, META + P * t:META + P * (t + 1)], ident)
                last.then_inc(s["t_full"], 1)
                wait(pe, s["r_free"], 2 * i + n)
                pe.transpose(bank_r[:, 0:P], src[:, META + SEQ:T], ident)
                pe.transpose(bank_r[0:META, P:2 * P], src[:, 0:META], ident).then_inc(s["r_full"], 1)

            def sum_squares(i):
                pe.wait_ge(s["o_free"], fill_o(i, O_NORM) + 1)
                pe.matmul(bank_n, ones[:], square[:, SEQ:TOK], start=True, stop=True)
                pe.matmul(bank_o[:], ones[:], square[:, 0:SEQ], start=True, stop=True).then_inc(s["o_full"], 1)

            def turn_last():
                pe.wait_ge(s["hist_ready"], KT)
                for half in range(2):
                    pe.wait_ge(evicted[half], NU * HEADS)
                    for k in range(4):
                        last = pe.transpose(bank_u[half][0:18, P * k:P * (k + 1)], u_last[:, 4 * half + k, :], ident)
                last.then_inc(s["last_turned"], 1)

            def body(i, units, attend):
                if not units:
                    turn_last()
                for u in range(NU):
                    if units:
                        unit(i, u)
                    elif 1 <= u < 6:
                        branch_product(0, u, u % 2)
                    if attend:
                        if u == 0:
                            turn_cache(i)
                            sample_scores(i)
                            if not units:
                                pe.wait_ge(s["rows_copied"], 1)
                                branch_product(0, 0, 0)
                        if u == 1:
                            sample_mix(i)
                            prompt_scores(i, 0)
                        if u == 2:
                            sample_values(i)
                        if 2 <= u <= 5:
                            prompt_turn(i, u - 2)
                        if 2 <= u <= 4:
                            prompt_scores(i, u - 1)
                        if u == 6:
                            prompt_values(i)
                        if u == 7:
                            sum_squares(i)
                    if not units and u >= 6:
                        branch_product(0, u, u % 2)
                    if units and u >= 6:
                        turn_rows(i, u - 6)

            turns(pe, body, lambda q, par, end: branch_product(1, 2 * q + par, par))

        @block.scalar
        def _(act):
            def split(i, u, pair=None):
                n = NU * i + u if pair is None else 2 * pair + u
                act.wait_ge(w_in_sem[u % 2], 16 * ((NU // 2) * i + u // 2 + 1 if pair is None else pair + 1))
                wait(act, s["half_done"], 2 * (n - 1))
                act.copy(w_hi[:, u % 2], w_raw[:, u % 2]).then_inc(s["split_hi"], 1)

            for f in range(2 * TB + 2):
                b, half = divmod(f, 2)
                w, at = (P, META + P * b) if b < TB else (META, 0)
                bank = turn_banks[f % 4][:].rearrange("p (k c) -> p k c", k=4)
                act.wait_ge(s["turned"], f + 1)
                act.copy(x_hi[:, 4 * half:4 * half + 4, at:at + w], bank[:, :, 0:w]).then_inc(s["turned_hi"], 1)
                if f == 2 * TB - 1:
                    split(0, 0)
            act.wait_ge(s["turned"], 2 * TB + 3)
            act.copy(hist_T[:], bank_t[:, 0:P].rearrange("p (k c) -> p k c", k=KT)).then_inc(s["hist_done"], 1)

            def evict(i, u):
                n = NU * i + u
                name = UNITS[u]
                for half in range(2):
                    cols = columns(u, half)
                    lo, hi = cols.start, cols.stop
                    if name in ("gc", "ga") and half == 0:
                        wait(act, gate_stored[name == "ga"], 16 * i)
                    if name == "h" and half == 0:
                        for x in range(2):
                            wait(act, evicted[x], NU * (i - 1) + 2)
                    if name in ("k", "q") and half == 0 and not isinstance(i, int):
                        act.wait_ge(s["scores1"], fill_s(i, 4) + 1)
                    if name == "q" and half == 0:
                        wait(act, s["q_maps_ready"], i)
                    act.wait_ge(s["half_done"], 2 * n + half + 1)
                    src = bank_u[half][:, 0:hi - lo]
                    if name == "h":
                        ins = act.copy(h_buf[:, lo:hi], src)
                    elif name in ("gc", "ga"):
                        ins = act.copy(gate[:, int(name == "ga"), lo - META:hi - META], src)
                    elif name in ("k", "v"):
                        ins = act.copy((kT if name == "k" else vT)[:, lo:hi], src)
                    elif name == "q":
                        ins = act.copy(qT[:, lo - META:hi - META], src)
                    ins.then_inc(evicted[half], 1)
                if name in ("gc", "ga"):
                    for half in range(2):
                        act.wait_ge(evicted[half], n + 1)
                    act.dma_start(d["gates"][int(name == "ga"), bass.ds(i, 1)].rearrange("a p t -> p (a t)"),
                                  gate[:, int(name == "ga"), :]).then_inc(gate_stored[name == "ga"], 16)

            def take_cache(i):
                for f in range(0, 5, 2):
                    act.wait_ge(s["t_full"], fill_t(i, f // 2) + 1)
                    w = P * min(4, 17 - 4 * f)
                    act.copy(kcT[:, 4 * P * f:4 * P * f + w], bank_t[:, 0:w]).then_inc(s["t_free"], 1)

            def exponent(i, n, w):
                for m in range(2):
                    act.wait_ge(max_ready[m], fill_s(i, n) + 1)
                    if n > 1:
                        act.wait_ge(s["mix_ready"], 4 * (i - 1) + n - 1)
                    act.activation(prob[:, m, 0:w], bank_s[m][:, 0:w], ACT.Exp, bias=neg_max[:, m:m + 1], scale=SCALE,
                                   accum_out=row_sum[:, m:m + 1]).then_inc(exp_done[m], 1)

            def take_turned(i, b):
                act.wait_ge(s["t_full"], fill_t(i, T_PROMPT + b) + 1)
                act.copy(mixT[:, 0:b + 1, P * b:P * (b + 1)], bank_t[:, 0:P * (b + 1)].rearrange("p (t q) -> p t q", q=P))
                act.copy(mixT_meta[:, P * b:P * (b + 1)], meta_T[b]).then_inc(s["t_free"], 1)

            def take_output(i, n, first, w):
                act.wait_ge(s["o_full"], fill_o(i, n) + 1)
                act.copy(ya[:, bass.ds(i - 1, 1), first:first + w].rearrange("p a t -> p (a t)"), bank_o[:, 0:w])
                act.activation(square[:, first:first + w], bank_o[:, 0:w], ACT.Square).then_inc(s["o_free"], 1)

            def take_rows(i, n):
                if n == 0:
                    wait(act, s["kv_stored"], 96 * i)
                rows = (k_rows, v_rows)[n]
                act.wait_ge(s["t_full"], rows_t(i, n) + 1)
                act.copy(rows[:, 0:QB, :], bank_t[:].rearrange("p (t c) -> p t c", c=P)).then_inc(s["t_free"], 1)
                act.wait_ge(s["r_full"], 2 * i + n + 1)
                act.copy(rows[:, 4, :], bank_r[:, 0:P])
                act.copy(rows[0:META, 5, :], bank_r[0:META, P:2 * P]).then_inc(s["r_free"], 1)
                act.wait_ge(s["t_free"], rows_t(i, n) + 1)
                act.wait_ge(s["r_free"], 2 * i + n + 1)
                which = "kv"[n]
                out = d["new_" + which + "_prompt"][0, 0, :, bass.ds(i, 1), :].rearrange("t a c -> t (a c)")
                act.dma_start(out[0:META, :], rows[0:META, 5, :]).then_inc(s["kv_stored"], 16)
                act.dma_start(out[META:META + SEQ, :].rearrange("(b p) c -> p b c", p=P), rows[:, 0:QB, :]).then_inc(s["kv_stored"], 16)
                out = d["new_" + which + "_sample"][0, :, :, bass.ds(i, 1), :].rearrange("s q a c -> (s q) (a c)")
                act.dma_start(out, rows[:, 4, :]).then_inc(s["kv_stored"], 16)

            def take_roots(i):
                act.wait_ge(s["o_full"], fill_o(i, O_NORM) + 1)
                act.activation(root[:, SEQ:TOK], bank_n, ACT.Sqrt, bias=eps[:, 0:1], scale=1.0 / P)
                act.activation(root[:, 0:SEQ], bank_o[:], ACT.Sqrt, bias=eps[:, 0:1], scale=1.0 / P).then_inc(s["o_free"], 1)

            def store_last():
                act.wait_ge(s["last_turned"], 1)
                act.wait_ge(s["o_full"], fill_o(HEADS - 1, O_PROMPT) + 1)
                for half in range(2):
                    last = act.copy(last_rows[:, 512 * half:512 * (half + 1)], bank_u[half][0:18, :])
                last.then_inc(s["rows_copied"], 1)
                act.wait_ge(s["rows_copied"], 1)
                act.dma_start(d["new_conv_prompt"][0, 0], last_rows[0:2, :]).then_inc(s["last_stored"], 16)
                act.dma_start(d["new_conv_sample"][0].rearrange("s j c -> (s j) c"), last_rows[2:18, :]).then_inc(s["last_stored"], 16)

            def split_conv():
                act.wait_ge(s["half_done"], 2 * NU * HEADS)
                act.wait_ge(evicted[0], NU * HEADS)
                act.wait_ge(evicted[1], NU * HEADS)
                for k in range(KT):
                    act.copy(x_hi[:, k, 0:TOK], yc[:, k]).then_inc(s["yc_hi_done"], 1)

            def split_head(k):
                act.copy(ya_hi[:, k], ya[:, k]).then_inc(s["ya_hi_done"], 1)

            def open_gate(br, m, par):
                act.wait_ge(gate_in[par], 16 * (KT // 2 * br + 1) + (16 * (m // 2) if isinstance(m, int) else 8 * (m - par)))
                act.activation(gate[:, par, :], gate[:, par, :], ACT.Sigmoid).then_inc(s["gate_ready"], 1)

            def body(i, units, attend):
                if not units:
                    store_last()
                for u in range(NU):
                    if u + 1 < NU:
                        split(i, u + 1)
                    else:
                        split(i + 1, 0)
                    if units and UNITS[u] not in ("cg", "bg"):
                        evict(i, u)
                    if not units and u > 0:
                        open_gate(0, u, u % 2)
                    if attend:
                        if u == 0:
                            take_cache(i)
                            if not units:
                                split_conv()
                            exponent(i, 0, 4 * P)
                        if 1 <= u <= 4:
                            if u == 2:
                                take_output(i, O_SAMPLE, SEQ, P)
                                if not units:
                                    act.wait_ge(s["last_stored"], 32)
                            if u >= 2:
                                take_turned(i, u - 2)
                            exponent(i, u, keys(u - 1))
                        if u == 5:
                            take_turned(i, 3)
                        if u == 6:
                            take_output(i, O_PROMPT, 0, SEQ)
                        if u == 7:
                            take_roots(i)
                    if not units:
                        if u == 0:
                            open_gate(0, 0, 0)
                        if u == 3:
                            act.wait_ge(s["q_maps_ready"], HEADS)
                        for k in {3: (0,), 4: (1,), 5: (2, 3), 6: (4, 5), 7: (6,)}.get(u, ()):
                            split_head(k)
                    if units and u >= 6:
                        take_rows(i, u - 6)

            def second_branch(q, par, end):
                m = 2 * q + par
                if isinstance(q, int) and q == 0 and par == 0:
                    act.wait_ge(s["normed"], 1)
                    split_head(KT - 1)
                if not end:
                    split(0, 1 - par, BRANCH[1] // 2 + q + par)
                open_gate(1, m, par)
                act.wait_ge(s["merged_done"], m + 1)
                act.copy(one(x_hi, m), one(yc, m)).then_inc(s["merged_hi"], 1)

            act.wait_ge(s["lam_sums"], 1)
            act.activation(lam[:, 2:4], lam[:, 0:2], ACT.Exp).then_inc(s["lam_exp"], 1)
            turns(act, body, second_branch)
            act.wait_ge(s["kv_stored"], 96 * HEADS)

        @block.vector
        def _(v):
            def split(i, u, pair=None):
                n = NU * i + u if pair is None else 2 * pair + u
                v.wait_ge(s["split_hi"], n + 1)
                v.tensor_tensor(w_lo[:, u % 2], w_raw[:, u % 2], w_hi[:, u % 2].bitcast(F32), ALU.subtract).then_inc(s["split_lo"], 1)

            for f in range(2 * TB + 2):
                b, half = divmod(f, 2)
                w, at = (P, META + P * b) if b < TB else (META, 0)
                bank = turn_banks[f % 4][:].rearrange("p (k c) -> p k c", k=4)
                v.wait_ge(s["turned_hi"], f + 1)
                v.tensor_tensor(x_lo[:, 4 * half:4 * half + 4, at:at + w], bank[:, :, 0:w],
                                x_hi[:, 4 * half:4 * half + 4, at:at + w].bitcast(F32), ALU.subtract).then_inc(s["turned_lo"], 1)
                if f == 2 * TB - 1:
                    split(0, 0)
            v.drain()
            v.sem_inc(s["o_free"], 1)
            v.wait_ge(s["taps_in"], 16 * KT)
            v.wait_ge(s["hist_done"], 1)

            def evict_cg(i):
                n = NU * i + 1
                for half in range(2):
                    lo, hi = HALF * half, HALF * (half + 1)
                    v.wait_ge(evicted[half], n)
                    v.wait_ge(s["half_done"], 2 * n + half + 1)
                    v.tensor_tensor(u_buf[:, lo:hi], bank_u[half][:, 0:HALF], h_buf[:, lo:hi], ALU.mult).then_inc(evicted[half], 1)
                v.drain()
                v.tensor_copy(u_hist[:, :, 2:NEW + 2], u_buf[:, META + SEQ:T].rearrange("p (s q) -> p s q", q=NEW))
                v.tensor_copy(u_hist[:, :, 0:2], hist_T[:, bass.ds(i, 1), :].rearrange("p a (s j) -> p (a s) j", j=2))
                v.tensor_copy(u_last[:, bass.ds(i, 1), 0:2].rearrange("p a c -> p (a c)"), u_buf[:, META + SEQ - 2:META + SEQ])
                v.drain()
                v.tensor_copy(u_last[:, bass.ds(i, 1), 2:18].rearrange("p a (s j) -> p (a s) j", j=2), u_hist[:, :, NEW:NEW + 2]).then_inc(s["hist_ready"], 1)
                for t in (2, 1, 0):
                    tap = taps[:, bass.ds(i, 1), t:t + 1].rearrange("p a b -> p (a b)")
                    to = conv[:, SEQ:TOK].rearrange("p (s q) -> p s q", q=NEW)
                    prompt, sample = u_buf[:, META - 2 + t:META - 2 + t + SEQ], u_hist[:, :, t:t + NEW]
                    if t == 2:
                        v.tensor_scalar(conv[:, 0:SEQ], prompt, tap, None, ALU.mult)
                        v.tensor_scalar(to, sample, tap, None, ALU.mult)
                    else:
                        v.scalar_tensor_tensor(conv[:, 0:SEQ], prompt, tap, conv[:, 0:SEQ], ALU.mult, ALU.add)
                        v.scalar_tensor_tensor(to, sample, tap, to, ALU.mult, ALU.add)
                    v.drain()

            def evict_bg(i):
                n = NU * i + 2
                for half in range(2):
                    w = TOK // 2
                    v.wait_ge(s["half_done"], 2 * n + half + 1)
                    v.tensor_tensor(yc[:, bass.ds(i, 1), w * half:w * (half + 1)].rearrange("p a t -> p (a t)"),
                                    bank_u[half][:, 0:w], conv[:, w * half:w * (half + 1)], ALU.mult).then_inc(evicted[half], 1)

            def take_cache(i):
                for f in (1, 3):
                    v.wait_ge(s["o_full"], fill_o(i, f // 2) + 1)
                    v.tensor_copy(kcT[:, 4 * P * f:4 * P * (f + 1)], bank_o[:]).then_inc(s["o_free"], 1)

            def maximum(i, n, w):
                for m in range(2):
                    v.wait_ge(scores[m], fill_s(i, n) + 1)
                    if n == 0:
                        v.tensor_tensor(bank_s[m][:, 2 * P:4 * P].rearrange("p (x c) -> p x c", x=2),
                                        bank_s[m][:, 2 * P:4 * P].rearrange("p (x c) -> p x c", x=2),
                                        const[:, C_MASK + P * m:C_MASK + P * (m + 1)].rearrange("p (x c) -> p x c", x=1).to_broadcast((P, 2, P)), ALU.add)
                    else:
                        v.memset(bank_s[m][0:CHUNK, w - CHUNK:w], MASKED)
                    v.drain()
                    v.tensor_reduce(neg_max[:, m:m + 1], bank_s[m][:, 0:w], AX.X, ALU.max)
                    v.drain()
                    v.tensor_scalar(neg_max[:, m:m + 1], neg_max[:, m:m + 1], -SCALE, None, ALU.mult).then_inc(max_ready[m], 1)

            def spread_rows(i):
                for g in range(2):
                    v.wait_ge(exp_done[g], fill_s(i, 0) + 1)
                    v.reciprocal(inv[:, g:g + 1], row_sum[:, g:g + 1])
                    v.drain()
                    v.tensor_scalar(spread[:, g, :], const[:, C_SPREAD + P * g:C_SPREAD + P * (g + 1)], inv[:, g:g + 1], lam[:, 5:6],
                                    ALU.mult, ALU.mult)
                v.drain()
                v.sem_inc(s["spread_ready"], 1)

            def take_sample_mix(i):
                v.wait_ge(s["t_full"], fill_t(i, T_SAMPLE) + 1)
                for t in range(OWN):
                    to = own_T[:, t, :].rearrange("p (s c) -> p s c", c=P + NEW)[:, 0:STREAMS, 0:NEW]
                    v.tensor_copy(to, bank_t[:, P * t:P * (t + 1)].rearrange("p (s q) -> p s q", q=NEW))
                v.tensor_copy(shared_T[:], bank_t[:, 2 * P:4 * P].rearrange("p (t c) -> p t c", c=P)).then_inc(s["t_free"], 1)

            def combine_maps(i, b):
                w = keys(b)
                v.wait_ge(exp_done[0], fill_s(i, 1 + b) + 1)
                v.wait_ge(exp_done[1], fill_s(i, 1 + b) + 1)
                v.reciprocal(inv[:, 0:2], row_sum[:])
                v.drain()
                v.tensor_scalar(mix[:, b % 2, 0:w], prob[:, 0, 0:w], inv[:, 0:1], None, ALU.mult)
                v.tensor_scalar(inv[:, 2:3], inv[:, 1:2], lam[:, 4:5], None, ALU.mult)
                v.drain()
                v.scalar_tensor_tensor(mix[:, b % 2, 0:w], prob[:, 1, 0:w], inv[:, 2:3], mix[:, b % 2, 0:w], ALU.mult, ALU.add).then_inc(s["mix_ready"], 1)

            def norm(i):
                v.wait_ge(s["o_free"], fill_o(i, O_NORM) + 2)
                v.reciprocal(root[:], root[:])
                v.drain()
                y = ya[:, bass.ds(i - 1, 1), :].rearrange("p a t -> p (a t)")
                last = v.scalar_tensor_tensor(y, y, gain[:, 1:2], root[:], ALU.mult, ALU.mult)
                if isinstance(i, int) and i == HEADS:
                    last.then_inc(s["normed"], 1)

            def split_conv():
                for k in range(KT):
                    v.wait_ge(s["yc_hi_done"], k + 1)
                    v.tensor_tensor(x_lo[:, k, 0:TOK], yc[:, k], x_hi[:, k, 0:TOK].bitcast(F32), ALU.subtract).then_inc(s["yc_lo_done"], 1)

            def split_head(k):
                v.wait_ge(s["ya_hi_done"], k + 1)
                v.tensor_tensor(ya_lo[:, k], ya[:, k], ya_hi[:, k].bitcast(F32), ALU.subtract).then_inc(s["ya_lo_done"], 1)

            def evict_branch(br, m, par):
                n = BRANCH[br] + m
                v.wait_ge(s["gate_ready"], KT * br + m + 1)
                for half in range(2):
                    cols = slice(TOK // 2 * half, TOK // 2 * (half + 1))
                    v.wait_ge(s["half_done"], 2 * n + half + 1)
                    to = one(yc, m, cols) if br == 0 else gated[:, cols]
                    v.tensor_tensor(to, bank_u[half][:, 0:TOK // 2], gate[:, par, cols], ALU.mult).then_inc(evicted[half], 1)

            def lay_out_q(i):
                for half in range(2):
                    v.wait_ge(evicted[half], NU * i + 8)
                for m in range(2):
                    r = slice(64 * m, 64 * m + 64)
                    q = qT[r, SEQ:TOK].rearrange("p (s q) -> p s q", q=NEW)
                    v.tensor_copy(q_maps[r, :, NEW * m:NEW * (m + 1)], q)
                    for g in range(2):
                        to = q_pad[r, 4 * P * g:4 * P * g + 640].rearrange("p (s c) -> p s c", c=P + 32)
                        last = v.tensor_copy(to[:, :, NEW * m:NEW * (m + 1)], q[:, 4 * g:4 * g + 4, :])
                last.then_inc(s["q_maps_ready"], 1)

            def body(i, units, attend):
                for u in range(NU):
                    if u + 1 < NU:
                        split(i, u + 1)
                    else:
                        split(i + 1, 0)
                    if units and UNITS[u] == "cg":
                        evict_cg(i)
                    if units and UNITS[u] == "bg":
                        evict_bg(i)
                    if not units and u == NU - 1:
                        norm(i)
                    if not units and u > 0:
                        evict_branch(0, u, u % 2)
                    if attend:
                        if u == 0:
                            take_cache(i)
                            if not units:
                                split_conv()
                            maximum(i, 0, 4 * P)
                            spread_rows(i)
                            if not units:
                                evict_branch(0, 0, 0)
                        if u == 1:
                            take_sample_mix(i)
                        if 1 <= u <= 4:
                            maximum(i, u, keys(u - 1))
                            combine_maps(i, u - 1)
                    if not units:
                        for k in {3: (0,), 4: (1,), 5: (2, 3), 6: (4, 5), 7: (6,)}.get(u, ()):
                            split_head(k)
                if units and attend:
                    norm(i)
                if units:
                    lay_out_q(i)

            def second_branch(q, par, end):
                m = 2 * q + par
                if isinstance(q, int) and q == 0 and par == 0:
                    split_head(KT - 1)
                if not end:
                    split(0, 1 - par, BRANCH[1] // 2 + q + par)
                evict_branch(1, m, par)
                v.drain()
                v.tensor_tensor(one(yc, m), gated, one(yc, m), ALU.add).then_inc(s["merged_done"], 1)
                v.wait_ge(s["merged_hi"], m + 1)
                v.tensor_tensor(one(x_lo, m), one(yc, m), one(x_hi, m).bitcast(F32), ALU.subtract)

            v.memset(ones[:], 1.0)
            v.memset(eps[:], EPS)
            v.memset(q_maps[:], 0.0)
            v.wait_ge(s["gain_in"], 16)
            v.tensor_scalar(gain[:, 1:2], gain[:, 0:1], 1.0 - LAM_INIT, None, ALU.mult)
            v.memset(q_pad[:], 0.0)
            v.memset(own_T[:], 0.0)
            v.wait_ge(s["lam_in_sem"], 16)
            for x in range(2):
                v.tensor_tensor_reduce(lam_tmp[:], lam_in[:, 128 * x:128 * x + 64], lam_in[:, 128 * x + 64:128 * x + 128],
                                       1.0, 0.0, ALU.mult, ALU.add, lam[:, x:x + 1])
                v.drain()
            v.sem_inc(s["lam_sums"], 1)
            v.wait_ge(s["lam_exp"], 1)
            v.scalar_tensor_tensor(lam[:, 4:5], lam[:, 3:4], -LAM_INIT, lam[:, 2:3], ALU.add, ALU.subtract)
            v.drain()
            v.wait_ge(s["const_in"], 16)
            v.tensor_scalar(lam[:, 6:7], lam[:, 4:5], -1.0, None, ALU.add)
            v.drain()
            v.tensor_scalar(lam[:, 5:6], lam[:, 6:7], const[:, C_SIGN:C_SIGN + 1], 1.0, ALU.mult, ALU.add)
            turns(v, body, second_branch)


def center(act, out, pre, mv, scratch, eps, n, steps):
    var_ready, centered = steps
    act.wait_ge(var_ready, n)
    act.activation(scratch[:, 0:1], mv[:, 1:2], ACT.Sqrt, bias=eps[:, 0:1], scale=1.0)
    act.activation(out, pre, ACT.Identity, bias=scratch[:, 2:3], scale=1.0).then_inc(centered, 1)


def moments(v, pre, stats, mv, scratch, steps):
    for half in range(2):
        v.bn_stats(stats[:, 6 * half:6 * half + 6], pre[:, 512 * half:512 * (half + 1)])
    v.drain()
    v.bn_aggr(mv, stats[:, 0:12])
    v.drain()
    v.tensor_scalar(scratch[:, 2:3], mv[:, 0:1], -1.0, None, ALU.mult).then_inc(steps[0], 1)


def scale_shift(v, out, centered_rows, scratch, gain, shift, n, steps):
    v.wait_ge(steps[1], n)
    v.reciprocal(scratch[:, 1:2], scratch[:, 0:1])
    v.drain()
    v.scalar_tensor_tensor(centered_rows, centered_rows, scratch[:, 1:2], gain, ALU.mult, ALU.mult)
    v.drain()
    return v.tensor_tensor(out, centered_rows, shift, ALU.add)


def route(nc, d, keep):
    with ExitStack() as ctx:
        sb = lambda name, shape, dt=F32: ctx.enter_context(nc.sbuf_tensor(name, shape, dt))
        pb = lambda name: ctx.enter_context(nc.psum_tensor(name, [P, 512], F32))
        sem = lambda name: ctx.enter_context(nc.semaphore("r_" + name))
        m_hi, m_lo, const, h = keep["x_hi"], keep["x_lo"], keep["const"], keep["h"]
        weights, eid = keep["weights"], keep["eid"]
        ident = const[:, C_ID:C_ID + P]
        up, down = keep["up_raw"][0], keep["down_raw"][0]
        w_raw = [keep["w_out_raw"][:, k, :] for k in range(2)]
        w_raw += [up[:, 2 * k:2 * k + 2, :].rearrange("p a n -> p (a n)") for k in range(4)] + [down[:, k, :] for k in range(2)]
        w_hi, w_lo = (keep[n][:].rearrange("p (k n) -> p k n", n=D) for n in ("w_hi_space", "w_lo_space"))
        x_rows = sb("rx_rows", [P, 2, D])
        free = keep["ya"][:].rearrange("p k t -> p (k t)")
        pre, hT = free[:, 0:2 * D].rearrange("p (b n) -> p b n", n=D), free[:, 2 * D:3 * D].rearrange("p (k c) -> p k c", k=KT)
        ln_g, ln_b = free[:, 3 * D:4 * D], free[:, 4 * D:5 * D]
        w_router, b_router = sb("w_router_sb", [P, KT, 36]), sb("b_router_sb", [P, 36])
        stats, mv, scratch, eps = sb("stats", [P, 12]), sb("mv", [P, 2]), sb("scratch1", [P, 4]), sb("eps1", [P, 1])
        logits = sb("logits", [P, TB, 36])
        group8, top8, idx8 = sb("group8", [P, TB, 8]), sb("top8", [P, TB, 8]), sb("idx8", [P, TB, 8], U32)
        pick_f = sb("pick_f", [P, 4, TB])
        masked, offm = sb("masked", [P, TB, EXPERTS]), sb("offm", [P, TB, EXPERTS])
        first, second, both = (sb(n, [P, TB, EXPERTS]) for n in ("first", "second", "both"))
        shifted, expd = sb("shifted", [P, TB, 8]), sb("expd", [P, TB, 8])
        soft = sb("soft", [P, 6, TB])
        ones, zeros = sb("ones1", [P, P]), sb("zeros1", [P, EXPERTS])
        per_expert = sb("per_expert", [P, 6, EXPERTS])
        compare = sb("compare", [1, SPARE, EXPERTS])
        eid_f = sb("eid_f", [1, SPARE + 1])
        above_count = sb("above_count", [P, EXPERTS, TB - 1])
        column, choice_id = sb("column", [P, P]), sb("choice_id", [P, 2 * TB])
        place, of_block = sb("place", [P, 2 * TB, P]), sb("of_block", [P, 2 * TB, BLOCKS])
        place_f, block_f = sb("place_f", [P, 2 * TB]), sb("block_f", [P, 2 * TB])
        over = sb("over", [P, TB, EXPERTS])
        ahead = sb("ahead", [P, TB + 1, EXPERTS])
        choice_f, above = sb("choice_f", [P, BLOCKS]), sb("above", [P, BLOCKS])
        choice, token = keep["choice"], keep["token"]
        slot_f = sb("slot_f", [P, 2, TB])

        bank = [[pb(f"rbank{a}{b}") for b in range(2)] for a in range(2)]
        bank_h = [pb("bank_h0"), pb("bank_h1")]
        bank_l, bank_c = pb("bank_l"), pb("bank_c")
        tile_logits = lambda b, n: (bank_l[:, 64 * b:64 * (b + n)] if b + n < TB else bank_c[:, 448:512]).rearrange("p (b c) -> p b c", b=n)
        w_loaded = keep["w_out_in"]
        x_loaded, h_stored = ([sem(f"{n}{x}") for x in range(2)] for n in ("x_loaded", "h_stored"))
        small_in, split_hi, split_lo, out_done, taken = (sem(n) for n in ("small_in", "split_hi", "split_lo", "out_done", "taken"))
        var_ready, root_done, h_ready, h_turned, h_taken, logits_done = (sem(n) for n in ("var_ready", "root_done", "h_ready", "h_turned", "h_taken", "logits_done"))
        shifted_ready, exp_ready, both_ready, counted, slots_ready, placed, blocks_placed, table_done, consts_done = (sem(n) for n in ("shifted_ready", "exp_ready", "both_ready", "counted", "slots_ready", "placed", "blocks_placed", "table_done", "consts_done"))
        block = ctx.enter_context(nc.Block())
        SMALL = 16 * 7

        @block.sync
        def _(sp):
            for k in range(2, KT):
                sp.dma_start(w_raw[k], d["w_out"][0, P * k:P * (k + 1), :]).then_inc(w_loaded[k], 16)
            for k in range(2, 4):
                sp.dma_start(x_rows[:, k - 2], d["x_prompt"][0, P * (k - 2):P * (k - 1), :]).then_inc(x_loaded[k - 2], 16)
            sp.dma_start(column[:], d["const"][:, C_COLUMN:C_END]).then_inc(small_in, 16)
            sp.dma_start(ln_g, d["ln1_g"].to_broadcast((P, D))).then_inc(small_in, 16)
            sp.dma_start(ln_b, d["ln1_b"].to_broadcast((P, D))).then_inc(small_in, 16)
            sp.dma_start(b_router[:, 0:4], d["b_group"].to_broadcast((P, 4))).then_inc(small_in, 16)
            sp.dma_start(b_router[:, 4:36], d["b_router"].to_broadcast((P, 32))).then_inc(small_in, 16)
            sp.dma_start(w_router[:, :, 0:4], d["w_group"][0].rearrange("(k p) n -> p k n", p=P)).then_inc(small_in, 16)
            sp.dma_start(w_router[:, :, 4:36], d["w_router"][0].rearrange("(k p) n -> p k n", p=P)).then_inc(small_in, 16)

            def load_expert(e, par):
                if e == 0:
                    sp.wait_ge(split_lo, KT)
                if e > 1:
                    sp.wait_ge(keep["up_lo_done"], 4 * (e - 1))
                sp.dma_start(keep["up_raw"][par][:], d["w_gate_up"][0, e].rearrange("(k p) n -> p k n", p=P)).then_inc(keep["up_in"][par], 16)
                if e > 1:
                    sp.wait_ge(keep["down_lo_done"], 2 * (e - 1))
                sp.dma_start(keep["down_raw"][par][:], d["w_down"][0, e].rearrange("(k p) n -> p k n", p=P)).then_inc(keep["down_in"][par], 16)

            load_expert(0, 0)
            for b in range(2, TB):
                src = d["x_prompt"][0, P * b:P * (b + 1), :] if b < QB else d["x_sample"].rearrange("s q d -> (s q) d")
                sp.wait_ge(taken, b - 1)
                sp.dma_start(x_rows[:, b % 2], src).then_inc(x_loaded[b % 2], 16)
            for b in range(TB):
                sp.wait_ge(h_ready, b + 1)
                sp.dma_start(d["h_rows"][P * b:P * (b + 1), :], h[:, b, :]).then_inc(h_stored[b % 2], 16)
            sp.wait_ge(out_done, TB)
            load_expert(1, 1)
            sp.dma_start(keep["ln2_g"], d["ln2_g"].to_broadcast((P, D))).then_inc(keep["ln2_in"], 16)
            sp.dma_start(keep["ln2_b"], d["ln2_b"].to_broadcast((P, D))).then_inc(keep["ln2_in"], 16)
            load_expert(2, 0)
            sp.wait_ge(h_stored[0], 48)
            sp.wait_ge(h_stored[1], 32)

        @block.tensor
        def _(pe):
            def out_rows(b):
                wait(pe, taken, b - 1)
                for k in range(KT):
                    pe.wait_ge(split_lo, k + 1)
                    rows = slice(P * b, P * (b + 1))
                    for strip in range(2):
                        out, cols = bank[b % 2][strip][:], slice(512 * strip, 512 * (strip + 1))
                        pe.matmul(out, m_hi[:, k, rows], w_hi[:, k, cols], start=(k == 0), stop=False)
                        pe.matmul(out, m_hi[:, k, rows], w_lo[:, k, cols], start=False, stop=False)
                        last = pe.matmul(out, m_lo[:, k, rows], w_hi[:, k, cols], start=False, stop=(k == KT - 1))
                last.then_inc(out_done, 1)

            def turn_h(b):
                pe.wait_ge(h_ready, b + 1)
                wait(pe, h_taken, 2 * b)
                for k in range(KT):
                    last = pe.transpose(bank_h[k // 4][:, P * (k % 4):P * (k % 4 + 1)], h[:, b, P * k:P * (k + 1)], ident)
                    if k % 4 == 3:
                        last.then_inc(h_turned, 1)

            def router(b):
                pe.wait_ge(h_taken, 2 * b + 2)
                if b == 0:
                    pe.wait_ge(small_in, SMALL)
                for k in range(KT):
                    last = pe.matmul(tile_logits(b, 1)[:, 0, 0:36], hT[:, k, :], w_router[:, k, :], start=(k == 0), stop=(k == KT - 1))
                last.then_inc(logits_done, 1)

            for b in range(TB):
                out_rows(b)
                if b > 1:
                    router(b - 2)
                if b > 0:
                    turn_h(b - 1)
            router(TB - 2)
            turn_h(TB - 1)
            router(TB - 1)
            pe.wait_ge(both_ready, 2)
            pe.wait_ge(consts_done, 1)
            flat = both[:].rearrange("p b e -> p (b e)")
            pe.matmul(bank_c[:, 0:EXPERTS * TB], const[:, C_UPPER:C_UPPER + P], flat, start=True, stop=True)
            last = pe.matmul(bank_c[:, 256:256 + EXPERTS * TB], ones[:], flat, start=True, stop=True)
            last.then_inc(counted, 1)
            for c in range(2 * TB):
                pe.wait_ge(placed, c + 1)
                if c % 2 == 0:
                    pe.wait_ge(blocks_placed, c // 2 + 1)
                last = pe.matmul(bank_h[0][:, 0:BLOCKS], place[:, c, :], of_block[:, c, :], start=(c == 0), stop=(c == 2 * TB - 1))
            last.then_inc(table_done, 1)

        @block.scalar
        def _(act):
            for k in range(KT):
                act.wait_ge(w_loaded[k], 16)
                act.copy(w_hi[:, k], w_raw[k]).then_inc(split_hi, 1)
            act.wait_ge(consts_done, 1)
            for b in range(TB):
                center(act, pre[:, b % 2, :], pre[:, b % 2, :], mv, scratch, eps, b + 1, (var_ready, root_done))
                for half in range(2):
                    act.wait_ge(h_turned, 2 * b + half + 1)
                    wait(act, logits_done, b)
                    act.copy(hT[:, 4 * half:4 * half + 4, :], bank_h[half][:].rearrange("p (k c) -> p k c", k=4)).then_inc(h_taken, 1)
            up_raw, down_raw, (up_hi, _), (down_hi, _) = keep["up_raw"][0], keep["down_raw"][0], keep["up_parts"], keep["down_parts"]
            act.wait_ge(out_done, TB)
            act.wait_ge(keep["up_in"][0], 16)
            for x in range(4):
                act.copy(up_hi[:, 2 * x:2 * x + 2, :], up_raw[:, 2 * x:2 * x + 2, :]).then_inc(keep["up_hi_done"], 1)
            act.wait_ge(keep["down_in"][0], 16)
            for x in range(2):
                act.copy(down_hi[:, 0, x, :], down_raw[:, x, :]).then_inc(keep["down_hi_done"], 1)
            act.wait_ge(shifted_ready, 2)
            act.activation(expd[:], shifted[:], ACT.Exp).then_inc(exp_ready, 1)

        @block.gpsimd
        def _(g):
            g.wait_ge(out_done, TB)
            g.memset(keep["rows"][:], 0.0)
            (up_hi, up_lo), (down_hi, down_lo) = keep["up_parts"], keep["down_parts"]
            for x in range(4):
                t = slice(2 * x, 2 * x + 2)
                g.wait_ge(keep["up_hi_done"], x + 1)
                g.tensor_tensor(up_lo[:, t, :], keep["up_raw"][0][:, t, :], up_hi[:, t, :].bitcast(F32), ALU.subtract).then_inc(keep["up_lo_done"], 1)

            def down_part(x):
                g.wait_ge(keep["down_hi_done"], x + 1)
                g.tensor_tensor(down_lo[:, 0, x, :], keep["down_raw"][0][:, x, :], down_hi[:, 0, x, :].bitcast(F32), ALU.subtract).then_inc(keep["down_lo_done"], 1)

            down_part(0)
            g.wait_ge(slots_ready, 1)
            for c in range(0, 2 * TB, 2):
                g.tensor_scalar(of_block[:, c, :], column[:, 0:BLOCKS], block_f[:, c:c + 1], choice_id[:, c:c + 1],
                                ALU.is_equal, ALU.mult).then_inc(blocks_placed, 1)
            down_part(1)

        @block.vector
        def _(v):
            v.memset(ones[:], 1.0)
            v.memset(zeros[:], 0.0)
            v.memset(eps[:], EPS).then_inc(consts_done, 1)
            v.tensor_scalar(choice_id[:], const[:, C_TOKEN:C_TOKEN + 2 * TB], 1.0, None, ALU.add)
            v.memset(group8[:], MASKED)
            v.memset(shifted[:, :, 5:8], 0.0)
            for k in range(KT):
                v.wait_ge(split_hi, k + 1)
                v.tensor_tensor(w_lo[:, k], w_raw[k], w_hi[:, k].bitcast(F32), ALU.subtract).then_inc(split_lo, 1)
            v.wait_ge(small_in, SMALL)
            for b in range(TB):
                v.wait_ge(out_done, b + 1)
                v.wait_ge(x_loaded[b % 2], 16 * (b // 2 + 1))
                p = pre[:, b % 2, :]
                for strip in range(2):
                    cols = slice(512 * strip, 512 * (strip + 1))
                    last = v.scalar_tensor_tensor(p[:, cols], x_rows[:, b % 2, cols], ALPHA, bank[b % 2][strip][:], ALU.mult, ALU.add)
                last.then_inc(taken, 1)
                v.drain()
                moments(v, p, stats, mv[:], scratch, (var_ready, root_done))
                scale_shift(v, h[:, b, :], p, scratch, ln_g, ln_b, b + 1, (var_ready, root_done)).then_inc(h_ready, 1)

            def pick(b0, b1):
                n, at = b1 - b0, slice(b0, b1)
                v.wait_ge(logits_done, b1)
                v.tensor_tensor(logits[:, at, :], tile_logits(b0, n)[:, :, 0:36],
                                b_router[:].rearrange("p (a c) -> p a c", a=1).to_broadcast((P, n, 36)), ALU.add)
                v.drain()
                v.tensor_copy(group8[:, at, 0:GROUPS], logits[:, at, 0:GROUPS])
                v.drain()
                for b in range(b0, b1):
                    v.max(top8[:, b, :], group8[:, b, :])
                v.drain()
                for b in range(b0, b1):
                    v.max_index(idx8[:, b, :], top8[:, b, :], group8[:, b, :])
                v.drain()
                v.tensor_copy(pick_f[:, 0, at], idx8[:, at, 0])
                v.tensor_tensor(shifted[:, at, 0:GROUPS], logits[:, at, 0:GROUPS], top8[:, at, 0:1].to_broadcast((P, n, GROUPS)), ALU.subtract)
                v.drain()
                for b in range(b0, b1):
                    v.tensor_scalar(masked[:, b, :], const[:, C_GROUP:C_GROUP + EXPERTS], pick_f[:, 0, b:b + 1], None, ALU.is_equal)
                v.drain()
                v.tensor_scalar(offm[:, at, :], masked[:, at, :], -MASKED, MASKED, ALU.mult, ALU.add)
                v.tensor_tensor(masked[:, at, :], masked[:, at, :], logits[:, at, GROUPS:GROUPS + EXPERTS], ALU.mult)
                v.drain()
                v.tensor_tensor(masked[:, at, :], masked[:, at, :], offm[:, at, :], ALU.add)
                v.drain()
                for b in range(b0, b1):
                    v.max(top8[:, b, :], masked[:, b, :])
                v.drain()
                for b in range(b0, b1):
                    v.max_index(idx8[:, b, :], top8[:, b, :], masked[:, b, :])
                v.drain()
                v.tensor_copy(pick_f[:, 1, at], idx8[:, at, 0])
                v.tensor_copy(pick_f[:, 2, at], idx8[:, at, 1])
                v.drain()
                for x, hot in enumerate((first, second)):
                    for b in range(b0, b1):
                        v.tensor_scalar(hot[:, b, :], const[:, C_EXPERT:C_EXPERT + EXPERTS], pick_f[:, 1 + x, b:b + 1], None, ALU.is_equal)
                v.drain()
                v.tensor_tensor(both[:, at, :], first[:, at, :], second[:, at, :], ALU.add).then_inc(both_ready, 1)
                v.tensor_tensor(shifted[:, at, 4:5], top8[:, at, 1:2], top8[:, at, 0:1], ALU.subtract).then_inc(shifted_ready, 1)

            pick(0, TB - 1)
            pick(TB - 1, TB)
            v.wait_ge(counted, 1)
            n_blocks, shift, ends, starts = (per_expert[:, x, :] for x in range(1, 5))
            v.memset(ahead[:, 0, :], 0.0)
            v.tensor_copy(ahead[:, 1:TB + 1, :], bank_c[:, 256:256 + EXPERTS * TB].rearrange("p (b e) -> p b e", b=TB))
            v.drain()
            for b in range(1, TB):
                v.tensor_tensor(ahead[:, b + 1, :], ahead[:, b + 1, :], ahead[:, b, :], ALU.add)
                v.drain()
            counts = ahead[:, TB, :]
            v.tensor_tensor(above_count[:], counts.rearrange("p (a e) -> p e a", a=1).to_broadcast((P, EXPERTS, TB - 1)),
                            const[:, C_FIRST + 1:C_FIRST + TB].rearrange("p (a x) -> p a x", a=1).to_broadcast((P, EXPERTS, TB - 1)), ALU.is_gt)
            v.tensor_tensor(over[:], bank_c[:, 0:EXPERTS * TB].rearrange("p (b e) -> p b e", b=TB), ahead[:, 0:TB, :], ALU.add)
            v.drain()
            v.tensor_reduce(n_blocks, above_count[:], AX.X, ALU.add)
            v.drain()
            v.tensor_tensor_scan(ends, n_blocks, zeros[:], 0.0, ALU.add, ALU.add)
            v.drain()
            v.tensor_tensor(starts, ends, n_blocks, ALU.subtract)
            v.drain()
            v.scalar_tensor_tensor(shift, starts, float(EXPERTS - 1), const[:, C_EXPERT:C_EXPERT + EXPERTS], ALU.add, ALU.subtract)
            v.tensor_scalar(offm[:], over[:], float(P), float(P), ALU.is_ge, ALU.mult)
            v.drain()
            v.tensor_tensor(offm[:], offm[:], per_expert[:, 2:3, :].to_broadcast((P, TB, EXPERTS)), ALU.mult)
            v.tensor_tensor(over[:], over[:], const[:, C_FIRST:C_FIRST + EXPERTS].rearrange("p (a e) -> p a e", a=1).to_broadcast((P, TB, EXPERTS)), ALU.add)
            v.drain()
            v.tensor_tensor(offm[:], offm[:], over[:], ALU.add)
            v.drain()
            for n, hot in enumerate((first, second)):
                v.tensor_tensor(masked[:], hot[:], offm[:], ALU.mult)
                v.drain()
                v.tensor_reduce(slot_f[:, n, :], masked[:], AX.X, ALU.add)
                v.drain()
            all_slots = slot_f[:].rearrange("p n b -> p (n b)")
            v.tensor_scalar(block_f[:], all_slots, 1.0 / P, -(P - 1) / 2 / P, ALU.mult, ALU.add)
            v.drain()
            for shift in (ROUND, -ROUND):
                v.tensor_scalar(block_f[:], block_f[:], shift, None, ALU.add)
                v.drain()
            v.scalar_tensor_tensor(place_f[:], block_f[:], -float(P), all_slots, ALU.mult, ALU.add)
            v.drain()
            v.sem_inc(slots_ready, 1)
            for c in range(2 * TB):
                last = v.tensor_scalar(place[:, c, :], column[:], place_f[:, c:c + 1], None, ALU.is_equal)
                if c % 2:
                    last = v.tensor_scalar(of_block[:, c, :], column[:, 0:BLOCKS], block_f[:, c:c + 1], choice_id[:, c:c + 1],
                                           ALU.is_equal, ALU.mult)
                last.then_inc(placed, 1)
            v.wait_ge(exp_ready, 1)
            v.tensor_reduce(soft[:, 0, :], expd[:, :, 0:GROUPS], AX.X, ALU.add)
            v.tensor_scalar(soft[:, 1, :], expd[:, :, 4], 1.0, None, ALU.add)
            v.drain()
            v.tensor_tensor(soft[:, 2, :], soft[:, 0, :], soft[:, 1, :], ALU.mult)
            v.drain()
            v.reciprocal(weights[:, 0, :], soft[:, 2, :])
            v.drain()
            v.tensor_tensor(weights[:, 1, :], weights[:, 0, :], expd[:, :, 4], ALU.mult)
            v.tensor_tensor(compare[:], per_expert[0:1, 3:4, :].to_broadcast((1, SPARE, EXPERTS)),
                            const[0:1, C_BLOCK:C_BLOCK + SPARE].rearrange("p (j a) -> p j a", a=1).to_broadcast((1, SPARE, EXPERTS)), ALU.is_le)
            v.drain()
            v.tensor_reduce(eid_f[:, 0:SPARE], compare[:], AX.X, ALU.add)
            v.drain()
            v.tensor_scalar(eid_f[:, 0:SPARE], eid_f[:, 0:SPARE], float(EXPERTS - 1), None, ALU.min)
            v.tensor_copy(eid_f[:, SPARE:SPARE + 1], per_expert[0:1, 3, EXPERTS - 1:EXPERTS])
            v.drain()
            v.tensor_copy(eid[:], eid_f[:])
            v.wait_ge(table_done, 1)
            v.tensor_scalar(above[:], bank_h[0][:, 0:BLOCKS], 0.0, float(NONE), ALU.is_equal, ALU.mult)
            v.drain()
            v.scalar_tensor_tensor(choice_f[:], bank_h[0][:, 0:BLOCKS], -1.0, above[:], ALU.add, ALU.add)
            v.drain()
            v.tensor_copy(choice[:], choice_f[:])
            v.tensor_scalar(above[:], choice_f[:], float(TOK), -float(TOK), ALU.is_ge, ALU.mult)
            v.drain()
            v.tensor_tensor(choice_f[:], choice_f[:], above[:], ALU.add)
            v.drain()
            v.tensor_copy(token[:], choice_f[:])


def run_experts(nc, d, keep):
    with ExitStack() as ctx:
        sb = lambda name, shape, dt=F32: ctx.enter_context(nc.sbuf_tensor(name, shape, dt))
        pb = lambda name: ctx.enter_context(nc.psum_tensor(name, [P, 512], F32))
        sem = lambda name: ctx.enter_context(nc.semaphore("e_" + name))
        const, eid = keep["const"], keep["eid"]
        ident = const[:, C_ID:C_ID + P]
        up_raw, down_raw, (up_hi, up_lo), (down_hi, down_lo) = keep["up_raw"], keep["down_raw"], keep["up_parts"], keep["down_parts"]
        rows, y_rows = keep["rows"], keep["y_rows"]
        xT_hi, xT_lo = sb("xT_hi", [P, 2, KT, P], F32R), sb("xT_lo", [P, 2, KT, P], F32R)
        silu, act_rows = sb("silu", [P, DE]), sb("act_rows", [P, DE])
        aT_hi, aT_lo = sb("aT_hi", [P, 2, P], F32R), sb("aT_lo", [P, 2, P], F32R)
        choice, token = keep["choice"], keep["token"]
        bank_g = [pb("bank_g0"), pb("bank_g1")]
        bank_x = [pb("bank_x0"), pb("bank_x1")]
        bank_a = pb("bank_a")
        bank_d = [pb("bank_d0"), pb("bank_d1")]
        two = lambda n: [sem(n + "0"), sem(n + "1")]
        rows_in, y_stored = two("rows_in"), two("y_stored")
        up_in, down_in, up_hi_done, up_lo_done, down_hi_done, down_lo_done = (
            keep[n] for n in ("up_in", "down_in", "up_hi_done", "up_lo_done", "down_hi_done", "down_lo_done"))
        (up_used, down_used, x_turned, x_hi_done, x_lo_done,
         silu_done, act_done, a_turned, a_hi_done, a_lo_done, y_left, y_right) = (sem(n) for n in (
             "up_used", "down_used", "x_turned",
             "x_hi_done", "x_lo_done", "silu_done", "act_done", "a_turned", "a_hi_done", "a_lo_done", "y_left", "y_right"))
        block = ctx.enter_context(nc.Block())

        def run(eng, body, j0, j1):
            j = j0
            while j < j1 and (j < 3 or j == j0):
                body(j, j // 2, j % 2, j == j0, j == j1 - 1)
                j += 1
            pairs = (j1 - 1 - j) // 2
            with eng.Fori(j // 2, j // 2 + pairs) as i:
                body(2 * i + 1, i, 1, False, False)
                body(2 * i + 2, i + 1, 0, False, False)
            for j in range(j + 2 * pairs, j1):
                body(j, j // 2, j % 2, False, j == j1 - 1)

        def all_blocks(eng, stretch):
            stretch(0, EXPERTS)
            spare = eng.value_load(eid[0:1, SPARE:SPARE + 1], min_val=0, max_val=SPARE)
            with eng.If(spare > 0):
                stretch(EXPERTS, BLOCKS)

        @block.sync
        def _(sp):
            def body(j, n, par, first, last):
                if not isinstance(j, int) and keep["spare"]:
                    e = sp.value_load(eid[0:1, bass.ds(j - EXPERTS, 1)], min_val=0, max_val=EXPERTS - 1)
                elif keep["spare"]:
                    e = sp.value_load(eid[0:1, j - EXPERTS:j - EXPERTS + 1], min_val=0, max_val=EXPERTS - 1)
                else:
                    e = j if isinstance(j, int) else sp.snap(j)
                up = d["w_gate_up"][0, bass.ds(e, 1)].rearrange("a (k p) n -> p (a k) n", p=P)
                down = d["w_down"][0, bass.ds(e, 1)].rearrange("a (k p) n -> p (a k) n", p=P)
                if isinstance(j, int) and j < 3:
                    return
                wait(sp, up_lo_done, 4 * j - 4)
                sp.dma_start(up_raw[par][:], up).then_inc(up_in[par], 16)
                wait(sp, down_lo_done, 2 * j - 2)
                sp.dma_start(down_raw[par][:], down).then_inc(down_in[par], 16)

            def stretch(j0, j1):
                keep["spare"] = j0 > 0
                run(sp, body, j0, j1)

            all_blocks(sp, stretch)

        @block.gpsimd
        def _(g):
            def gather(j):
                wait(g, x_turned, 2 * (j - 1))
                g.indirect_dma_start(out=rows[:, j % 2, :], out_offset=None, in_=d["h_rows"],
                                     in_offset=bass.IndirectOffsetOnAxis(ap=token[:, j:j + 1], axis=0),
                                     bounds_check=TOK - 1, oob_is_err=False).then_inc(rows_in[j % 2], 16)

            def scatter(j):
                g.wait_ge(y_left, j + 1)
                g.wait_ge(y_right, j + 1)
                g.indirect_dma_start(out=d["y_choice"], out_offset=bass.IndirectOffsetOnAxis(ap=choice[:, j:j + 1], axis=0),
                                     in_=y_rows[:, j % 2, :], in_offset=None,
                                     bounds_check=2 * TOK - 1, oob_is_err=False).then_inc(y_stored[j % 2], 16)

            def stretch(j0, j1):
                gather(j0)
                gather(j0 + 1)
                for j in range(j0, j1):
                    if j + 2 < j1:
                        gather(j + 2)
                    if j > j0:
                        scatter(j - 1)
                scatter(j1 - 1)
                g.wait_ge(y_stored[0], 16 * ((j1 + 1) // 2))
                g.wait_ge(y_stored[1], 16 * (j1 // 2))

            all_blocks(g, stretch)

        @block.tensor
        def _(pe):
            def turn_rows(j, n, par):
                pe.wait_ge(rows_in[par], 16 * (n + 1))
                for half in range(2):
                    wait(pe, x_lo_done, 2 * j - 1 + half)
                    for k in range(4):
                        kk = 4 * half + k
                        last = pe.transpose(bank_x[half][:, P * k:P * (k + 1)], rows[:, par, P * kk:P * (kk + 1)], ident)
                    last.then_inc(x_turned, 1)

            def gate_up(j, par):
                pe.wait_ge(x_lo_done, 2 * j + 2)
                wait(pe, act_done, j - 1)
                for k in range(KT):
                    if k % 2 == 0:
                        pe.wait_ge(up_lo_done, 4 * j + k // 2 + 1)
                    pe.matmul(bank_g[par][:], xT_hi[:, par, k, :], up_hi[:, k, :], start=(k == 0), stop=False)
                    pe.matmul(bank_g[par][:], xT_hi[:, par, k, :], up_lo[:, k, :], start=False, stop=False)
                    last = pe.matmul(bank_g[par][:], xT_lo[:, par, k, :], up_hi[:, k, :], start=False, stop=(k == KT - 1))
                    if k % 2 == 1:
                        last.then_inc(up_used, 1)

            def turn_act(j):
                pe.wait_ge(act_done, j + 1)
                wait(pe, a_lo_done, j)
                for k in range(2):
                    last = pe.transpose(bank_a[:, P * k:P * (k + 1)], act_rows[:, P * k:P * (k + 1)], ident)
                last.then_inc(a_turned, 1)

            def down(j, par):
                pe.wait_ge(a_lo_done, j + 1)
                wait(pe, y_left, j)
                wait(pe, y_right, j)
                for k in range(2):
                    pe.wait_ge(down_lo_done, 2 * j + k + 1)
                    for strip in range(2):
                        cols = slice(512 * strip, 512 * (strip + 1))
                        pe.matmul(bank_d[strip][:], aT_hi[:, k, :], down_hi[:, par, k, cols], start=(k == 0), stop=False)
                        pe.matmul(bank_d[strip][:], aT_hi[:, k, :], down_lo[:, par, k, cols], start=False, stop=False)
                        last = pe.matmul(bank_d[strip][:], aT_lo[:, k, :], down_hi[:, par, k, cols], start=False, stop=(k == 1))
                    last.then_inc(down_used, 1)

            def body(j, n, par, first, last):
                if not last:
                    turn_rows(j + 1, n + 1 if par else n, 1 - par)
                gate_up(j, par)
                if not first:
                    down(j - 1, 1 - par)
                turn_act(j)

            def stretch(j0, j1):
                turn_rows(j0, j0 // 2, 0)
                run(pe, body, j0, j1)
                down(j1 - 1, (j1 - 1) % 2)

            all_blocks(pe, stretch)

        @block.scalar
        def _(act):
            def split_up(j, n, par, parts=range(4)):
                act.wait_ge(up_in[par], 16 * (n + 1))
                for x in parts:
                    wait(act, up_used, 4 * j - 3 + x)
                    act.copy(up_hi[:, 2 * x:2 * x + 2, :], up_raw[par][:, 2 * x:2 * x + 2, :]).then_inc(up_hi_done, 1)

            def split_down(j, n, par):
                act.wait_ge(down_in[par], 16 * (n + 1))
                for x in range(2):
                    wait(act, down_used, 2 * j - 3 + x)
                    act.copy(down_hi[:, par, x, :], down_raw[par][:, x, :]).then_inc(down_hi_done, 1)

            def take_rows(j, par):
                for half in range(2):
                    act.wait_ge(x_turned, 2 * j + half + 1)
                    act.copy(xT_hi[:, par, 4 * half:4 * half + 4, :], bank_x[half][:].rearrange("p (k c) -> p k c", k=4)).then_inc(x_hi_done, 1)

            def store(j, par, n):
                act.wait_ge(down_used, 2 * j + 2)
                wait(act, y_stored[par], 16 * n)
                act.copy(y_rows[:, par, 0:512], bank_d[0][:]).then_inc(y_left, 1)

            def body(j, n, par, first, last):
                if not last:
                    take_rows(j + 1, 1 - par)
                if not isinstance(j, int) or j > 0:
                    split_down(j, n, par)
                if not last:
                    split_up(j + 1, n + 1 if par else n, 1 - par, range(3))
                act.wait_ge(up_used, 4 * j + 4)
                wait(act, act_done, j)
                act.activation(silu[:], bank_g[par][:, 0:DE], ACT.Silu).then_inc(silu_done, 1)
                if not last:
                    split_up(j + 1, n + 1 if par else n, 1 - par, (3,))
                if not first:
                    store(j - 1, 1 - par, n if par else n - 1)
                act.wait_ge(a_turned, j + 1)
                act.copy(aT_hi[:], bank_a[:, 0:2 * P].rearrange("p (k c) -> p k c", k=2)).then_inc(a_hi_done, 1)

            def stretch(j0, j1):
                if j0 > 0:
                    split_up(j0, j0 // 2, 0)
                take_rows(j0, 0)
                run(act, body, j0, j1)
                store(j1 - 1, (j1 - 1) % 2, (j1 - 1) // 2)

            all_blocks(act, stretch)

        @block.vector
        def _(v):
            def split_up(j, par, parts=range(4)):
                for x in parts:
                    v.wait_ge(up_hi_done, 4 * j + x + 1)
                    s = slice(2 * x, 2 * x + 2)
                    v.tensor_tensor(up_lo[:, s, :], up_raw[par][:, s, :], up_hi[:, s, :].bitcast(F32), ALU.subtract).then_inc(up_lo_done, 1)

            def take_rows(j, par):
                for half in range(2):
                    v.wait_ge(x_hi_done, 2 * j + half + 1)
                    s = slice(4 * half, 4 * half + 4)
                    v.tensor_tensor(xT_lo[:, par, s, :], bank_x[half][:].rearrange("p (k c) -> p k c", k=4), xT_hi[:, par, s, :].bitcast(F32),
                                    ALU.subtract).then_inc(x_lo_done, 1)

            def store(j, par, n):
                v.wait_ge(down_used, 2 * j + 2)
                wait(v, y_stored[par], 16 * n)
                v.tensor_copy(y_rows[:, par, 512:D], bank_d[1][:]).then_inc(y_right, 1)

            def body(j, n, par, first, last):
                if not last:
                    take_rows(j + 1, 1 - par)
                for x in range(0 if isinstance(j, int) and j == 0 else 2):
                    v.wait_ge(down_hi_done, 2 * j + x + 1)
                    v.tensor_tensor(down_lo[:, par, x, :], down_raw[par][:, x, :], down_hi[:, par, x, :].bitcast(F32), ALU.subtract).then_inc(down_lo_done, 1)
                if not last:
                    split_up(j + 1, 1 - par, range(3))
                v.wait_ge(silu_done, j + 1)
                wait(v, a_turned, j)
                v.tensor_tensor(act_rows[:], silu[:], bank_g[par][:, DE:2 * DE], ALU.mult).then_inc(act_done, 1)
                if not last:
                    split_up(j + 1, 1 - par, (3,))
                if not first:
                    store(j - 1, 1 - par, n if par else n - 1)
                v.wait_ge(a_hi_done, j + 1)
                v.tensor_tensor(aT_lo[:], bank_a[:, 0:2 * P].rearrange("p (k c) -> p k c", k=2), aT_hi[:].bitcast(F32), ALU.subtract).then_inc(a_lo_done, 1)

            def stretch(j0, j1):
                if j0 > 0:
                    split_up(j0, 0)
                take_rows(j0, 0)
                run(v, body, j0, j1)
                store(j1 - 1, (j1 - 1) % 2, (j1 - 1) // 2)

            all_blocks(v, stretch)


def combine(nc, d, keep):
    with ExitStack() as ctx:
        sb = lambda name, shape, dt=F32: ctx.enter_context(nc.sbuf_tensor(name, shape, dt))
        sem = lambda name: ctx.enter_context(nc.semaphore("c_" + name))
        h, weights, const = keep["h"], keep["weights"], keep["const"]
        ident = const[:, C_ID:C_ID + P]
        BY_PE = 2
        ln_g, ln_b, small_in = keep["ln2_g"], keep["ln2_b"], keep["ln2_in"]
        picked = sb("picked", [P, TB, 2, D])
        diag, diag_alpha = sb("diag", [P, TB, 2, P]), sb("diag_alpha", [P, P])
        stats, mv, scratch, eps = sb("stats2", [P, TB, 12]), sb("mv2", [P, TB, 2]), sb("scratch2", [P, TB, 4]), sb("eps2", [P, 1])
        bank_y = [ctx.enter_context(nc.psum_tensor(f"bank_y{x}", [P, D], F32)) for x in range(4)]
        picked_in = [[sem(f"picked_in{b}{n}") for n in range(2)] for b in range(TB)]
        summed, var_ready, centered, scaled, y_ready, y_stored, consts_done, diag_ready = (sem(n) for n in (
            "summed", "var_ready", "centered", "scaled", "y_ready", "y_stored", "consts_done", "diag_ready"))
        block = ctx.enter_context(nc.Block())

        @block.sync
        def _(sp):
            for b in range(TB):
                for n in range(2):
                    sp.dma_start(picked[:, b, n, :], d["y_choice"][TOK * n + P * b:TOK * n + P * (b + 1), :]).then_inc(picked_in[b][n], 16)
            for b in range(TB):
                sp.wait_ge(y_ready, b + 1)
                out = d["y_prompt"][0, P * b:P * (b + 1), :] if b < QB else d["y_sample"].rearrange("s q d -> (s q) d")
                sp.dma_start(out, picked[:, b, 0, :]).then_inc(y_stored, 16)
            sp.wait_ge(y_stored, 16 * TB)

        @block.tensor
        def _(pe):
            strips = [slice(512 * x, 512 * (x + 1)) for x in range(2)]

            def residual(b):
                for cols in strips:
                    pe.matmul(bank_y[b % 4][:, cols], diag_alpha[:], h[:, b, cols], start=True, stop=False)

            pe.wait_ge(consts_done, 1)
            for b in range(BY_PE):
                residual(b)
            pe.wait_ge(diag_ready, 1)
            for b in range(TB):
                if b >= 4:
                    pe.wait_ge(centered, b - 3)
                for n in range(2):
                    pe.wait_ge(picked_in[b][n], 16)
                    for cols in strips:
                        last = pe.matmul(bank_y[b % 4][:, cols], diag[:, b, n, :], picked[:, b, n, cols],
                                         start=(n == 0 and b >= BY_PE), stop=(n == 1))
                last.then_inc(summed, 1)

        @block.scalar
        def _(act):
            act.wait_ge(consts_done, 1)
            for b in range(TB):
                y = picked[:, b, 0, :]
                center(act, y, bank_y[b % 4][:] if b < BY_PE else y, mv[:, b, :], scratch[:, b, :], eps, b + 1, (var_ready, centered))

        @block.gpsimd
        def _(g):
            g.wait_ge(small_in, 32)
            for b in range(TB - 1):
                y = picked[:, b, 0, :]
                g.wait_ge(scaled, b + 1)
                g.tensor_tensor(y, y, ln_b, ALU.add).then_inc(y_ready, 1)

        @block.vector
        def _(v):
            def sums(b):
                y = bank_y[b % 4][:]
                v.wait_ge(summed, b + 1)
                if b >= BY_PE:
                    y = picked[:, b, 0, :]
                    v.scalar_tensor_tensor(y, h[:, b, :], ALPHA, bank_y[b % 4][:], ALU.mult, ALU.add)
                    v.drain()
                moments(v, y, stats[:, b, :], mv[:, b, :], scratch[:, b, :], (var_ready, centered))

            def finish(b):
                y = picked[:, b, 0, :]
                v.wait_ge(centered, b + 1)
                v.reciprocal(scratch[:, b, 1:2], scratch[:, b, 0:1])
                v.drain()
                last = v.scalar_tensor_tensor(y, y, scratch[:, b, 1:2], ln_g, ALU.mult, ALU.mult)
                if b < TB - 1:
                    last.then_inc(scaled, 1)
                else:
                    v.drain()
                    v.wait_ge(y_ready, TB - 1)
                    v.tensor_tensor(y, y, ln_b, ALU.add).then_inc(y_ready, 1)

            v.memset(eps[:], EPS)
            v.tensor_scalar(diag_alpha[:], ident, ALPHA, None, ALU.mult).then_inc(consts_done, 1)
            for b in range(TB):
                for n in range(2):
                    last = v.tensor_scalar(diag[:, b, n, :], ident, weights[:, n, b:b + 1], None, ALU.mult)
            last.then_inc(diag_ready, 1)
            sums(0)
            v.wait_ge(small_in, 32)
            for b in range(TB):
                if b + 1 < TB:
                    sums(b + 1)
                finish(b)


def program(nc, d):
    with ExitStack() as ctx:
        sb = lambda name, shape, dt=F32: ctx.enter_context(nc.sbuf_tensor(name, shape, dt))
        x_place = slab(nc, ctx, "x_slab", 2 * KT * T)
        x_hi, x_lo = x_place("x_hi", [P, KT, T], F32R, 0), x_place("x_lo", [P, KT, T], F32R, KT * T)
        keep = {"x_hi": x_hi, "x_lo": x_lo, "const": sb("const_sb", [P, C_COLUMN]), "yc": sb("yc", [P, KT, TOK]), "ya": sb("ya", [P, KT, TOK]),
                "weights": sb("weights", [P, 2, TB]), "eid": sb("eid", [1, SPARE + 1], I32),
                "choice": sb("choice", [P, BLOCKS], U32), "token": sb("token", [P, BLOCKS], U32)}
        keep["h"] = keep["yc"][:].rearrange("p k t -> p (k t)").rearrange("p (b n) -> p b n", n=D)
        d["gates"] = nc.dram_tensor("gates", [2, KT, P, TOK], F32).ap()
        d["h_rows"] = nc.dram_tensor("h_rows", [TOK, D], F32).ap()
        d["y_choice"] = nc.dram_tensor("y_choice", [2 * TOK, D], F32).ap()
        sem = lambda name: ctx.enter_context(nc.semaphore(name))
        keep["w_out_raw"] = sb("w_out_raw", [P, 2, D])
        for name, count in (("w_out_in", KT), ("up_in", 2), ("down_in", 2)):
            keep[name] = [sem(f"{name}{x}") for x in range(count)]
        for name in ("up_hi_done", "up_lo_done", "down_hi_done", "down_lo_done"):
            keep[name] = sem(name)
        free = keep["ya"][:].rearrange("p k t -> p (k t)")
        keep.update(ln2_g=free[:, 0:D], ln2_b=free[:, D:2 * D], ln2_in=sem("ln2_in"))
        project_and_attend(nc, d, keep)
        with nc.sbuf_tensor("first_up", [P, KT, 512], F32) as up, nc.sbuf_tensor("first_down", [P, 2, D], F32) as down, \
                nc.sbuf_tensor("w_hi_space", [P, KT * D], F32R) as w_hi, nc.sbuf_tensor("w_lo_space", [P, KT * D], F32R) as w_lo:
            keep["up_raw"] = [up, x_place("second_up", [P, KT, 512], F32, 0)]
            keep["down_raw"] = [down, x_place("second_down", [P, 2, D], F32, KT * 512)]
            keep["rows"] = x_place("rows", [P, 2, D], F32, KT * 512 + 2 * D)
            keep["y_rows"] = x_place("y_rows", [P, 2, D], F32, KT * 512 + 4 * D)
            keep["w_hi_space"], keep["w_lo_space"] = w_hi, w_lo
            keep["up_parts"] = [t[:, 0:KT * 512].rearrange("p (k n) -> p k n", n=512) for t in (w_hi, w_lo)]
            keep["down_parts"] = [t[:, KT * 512:KT * D].rearrange("p (a n) -> p a n", n=D).rearrange("p (b a) n -> p b a n", b=2) for t in (w_hi, w_lo)]
            route(nc, d, keep)
            run_experts(nc, d, keep)
        combine(nc, d, keep)


INPUTS = ["x_prompt", "x_sample", "cache_k", "cache_v", "state_conv", "meta_tokens", "w_in", "conv_w", "lambda_qk", "subln_g",
          "w_branch", "w_out", "ln1_g", "ln1_b", "w_group", "b_group", "w_router", "b_router", "w_gate_up", "w_down", "ln2_g", "ln2_b"]
OUTPUTS = {
    "y_prompt": (1, SEQ, D), "y_sample": (STREAMS, NEW, D),
    "new_k_prompt": (1, 1, META + SEQ, HEADS, P), "new_v_prompt": (1, 1, META + SEQ, HEADS, P), "new_conv_prompt": (1, 1, 2, D),
    "new_k_sample": (1, STREAMS, NEW, HEADS, P), "new_v_sample": (1, STREAMS, NEW, HEADS, P), "new_conv_sample": (1, STREAMS, 2, D),
}


def kernel(**inputs):
    import concourse.bacc as bacc
    from concourse.bass_utils import run_bass_kernel_spmd

    nc = bacc.Bacc("TRN2", target_bir_lowering=False, num_devices=1)
    arrays = {name: np.ascontiguousarray(inputs[name]) for name in INPUTS}
    arrays["const"] = constants()
    d = {name: nc.dram_tensor("in_" + name, a.shape, F32, kind="ExternalInput").ap() for name, a in arrays.items()}
    for name, shape in OUTPUTS.items():
        d[name] = nc.dram_tensor("out_" + name, shape, F32, kind="ExternalOutput").ap()
    program(nc, d)
    result = run_bass_kernel_spmd(nc, [{"in_" + n: a for n, a in arrays.items()}], core_ids=[0])
    return tuple(result.results[0]["out_" + name] for name in OUTPUTS)
```
